# Optimizing a Trainium2 kernel written in Bass

```python
import math
import jax, jax.numpy as jnp
from jax import lax
import numpy as np

D_MODEL = 2048
BATCH = 1
SEQ = 256
DEPTH = 1
DEC_BATCH = 1
DEC_SEQ = 32
PAST_LEN = 128

CHUNK = 64
HEAD_DIM = 64
H_A = 12
KV_A = 4
H_IDX = 8
D_IDX = 64
TOPK_MAX = 256
H_B = 10
KV_B = 2
WINDOW = 128
B_PREV = WINDOW // CHUNK
H_C = 10
C_PREV = 8
C_REACH = C_PREV * CHUNK
C_MAX_REL = 256
D_MIX = (H_A + H_B + H_C) * HEAD_DIM
D_FF = 5504
N_BUCKETS = 32
T5_MAX_DIST = 1024
EPS = 1e-6
NEG = -1e30
ATTN_SCALE = HEAD_DIM ** -0.5
IDX_SCALE = (H_IDX * D_IDX) ** -0.5
SPLIT_WIDTHS = (H_A * HEAD_DIM, KV_A * HEAD_DIM, KV_A * HEAD_DIM, H_IDX * D_IDX, D_IDX, H_IDX,
                H_B * HEAD_DIM, KV_B * HEAD_DIM, KV_B * HEAD_DIM,
                H_C * HEAD_DIM, H_C * HEAD_DIM, H_C * HEAD_DIM)
D_IN = sum(SPLIT_WIDTHS)

kernel_name = 'hybrid_streaming_encoder_step'

def rmsnorm(x, g):
    xf = x.astype(jnp.float32)
    y = xf * lax.rsqrt(jnp.mean(xf * xf, axis=-1, keepdims=True) + EPS)
    return (y * g.astype(jnp.float32)).astype(x.dtype)

def swiglu_ffn(x, g, w_gate, w_up, w_down):
    h = rmsnorm(x, g)
    return (jax.nn.silu(h @ w_gate) * (h @ w_up)) @ w_down

def t5_bucket(rel):
    nb = N_BUCKETS // 2
    max_exact = nb // 2
    n = jnp.abs(rel)
    nf = jnp.maximum(n, max_exact).astype(jnp.float32)
    large = max_exact + (jnp.log(nf / max_exact) / math.log(T5_MAX_DIST / max_exact)
                         * (nb - max_exact)).astype(jnp.int32)
    large = jnp.minimum(large, nb - 1)
    return jnp.where(rel > 0, nb, 0) + jnp.where(n < max_exact, n, large)

def t5_bias(rel, table):
    return jnp.moveaxis(table[t5_bucket(rel)], -1, 0)

def clip_bias(rel, table):
    return jnp.moveaxis(table[jnp.clip(rel, -C_MAX_REL, C_MAX_REL) + C_MAX_REL], -1, 0)

def band_rel(n_prev):
    i = jnp.arange(CHUNK)[:, None]
    j = jnp.arange((n_prev + 1) * CHUNK)[None, :]
    return j - n_prev * CHUNK - i

def project(h, w_in, qk_g):
    B, T, _ = h.shape
    z = h @ w_in
    offs = np.cumsum(SPLIT_WIDTHS)[:-1].tolist()
    qa, ka, va, qi, ki, wi, qb, kb, vb, qc, kc, vc = jnp.split(z, offs, axis=-1)
    heads = lambda t, n: t.reshape(B, T, n, HEAD_DIM)
    qa = rmsnorm(heads(qa, H_A), qk_g[0])
    ka = rmsnorm(heads(ka, KV_A), qk_g[1])
    va = heads(va, KV_A)
    qi = qi.reshape(B, T, H_IDX, D_IDX)
    qb = rmsnorm(heads(qb, H_B), qk_g[2])
    kb = rmsnorm(heads(kb, KV_B), qk_g[3])
    vb = heads(vb, KV_B)
    qc = rmsnorm(heads(qc, H_C), qk_g[4])
    kc = rmsnorm(heads(kc, H_C), qk_g[5])
    vc = heads(vc, H_C)
    return qa, ka, va, qi, ki, wi, qb, kb, vb, qc, kc, vc

def attend(q, k, v, bias, mask, sinks):
    B, T, H, _ = q.shape
    KVH = k.shape[2]
    G = H // KVH
    qg = q.reshape(B, T, KVH, G, HEAD_DIM)
    s = jnp.einsum('btkgd,blkd->bkgtl', qg, k).astype(jnp.float32) * ATTN_SCALE
    s = s + bias.astype(jnp.float32).reshape(KVH, G, T, -1)
    if mask is not None:
        s = jnp.where(mask, s, NEG)
    if sinks is None:
        p = jax.nn.softmax(s, axis=-1)
    else:
        sk = sinks.astype(jnp.float32).reshape(KVH, G, 1, 1)
        m = jnp.maximum(jnp.max(s, axis=-1, keepdims=True), sk)
        e = jnp.exp(s - m)
        p = e / (jnp.sum(e, axis=-1, keepdims=True) + jnp.exp(sk - m))
    o = jnp.einsum('bkgtl,blkd->btkgd', p.astype(v.dtype), v)
    return o.reshape(B, T, H, HEAD_DIM)

def band_attention(q, k, v, n_prev, bias, sinks):
    B, S, H, _ = q.shape
    NC = S // CHUNK
    band = (n_prev + 1) * CHUNK
    pad = n_prev * CHUNK
    kp = jnp.pad(k, ((0, 0), (pad, 0), (0, 0), (0, 0)))
    vp = jnp.pad(v, ((0, 0), (pad, 0), (0, 0), (0, 0)))
    qc = jnp.moveaxis(q.reshape(B, NC, CHUNK, H, HEAD_DIM), 1, 0)

    def one(args):
        c, qb = args
        kb = lax.dynamic_slice_in_dim(kp, c * CHUNK, band, axis=1)
        vb = lax.dynamic_slice_in_dim(vp, c * CHUNK, band, axis=1)
        valid = jnp.arange(band) >= pad - c * CHUNK
        return attend(qb, kb, vb, bias, valid[None, None, None, None, :], sinks)

    out = lax.map(one, (jnp.arange(NC), qc))
    return jnp.moveaxis(out, 0, 1).reshape(B, S, H, HEAD_DIM)

def index_scores(qi, ki, wi):
    s = jax.nn.relu(jnp.einsum('bthd,bsd->bths', qi, ki).astype(jnp.float32))
    return jnp.einsum('bths,bth->bts', s, wi.astype(jnp.float32)) * IDX_SCALE

def sparse_attend(q, k, v, idx, valid, qpos, t5_a):
    B, T, H, _ = q.shape
    G = H // KV_A
    gather = jax.vmap(lambda rows, ii: rows[ii])
    ks = gather(k, idx)
    vs = gather(v, idx)
    qg = q.reshape(B, T, KV_A, G, HEAD_DIM)
    bias = t5_a[t5_bucket(idx - qpos[:, None])]
    bias = bias.reshape(B, T, -1, KV_A, G).transpose(0, 3, 4, 1, 2).astype(jnp.float32)
    s = jnp.einsum('btkgd,btnkd->bkgtn', qg, ks).astype(jnp.float32) * ATTN_SCALE + bias
    s = jnp.where(valid[:, None, None], s, NEG)
    p = jax.nn.softmax(s, axis=-1)
    o = jnp.einsum('bkgtn,btnkd->btkgd', p.astype(v.dtype), vs)
    return o.reshape(B, T, H, HEAD_DIM)

def dsa_prompt(qa, ka, va, qi, ki, wi, t5_a):
    B, S = qa.shape[:2]
    NB = S // CHUNK
    k_sel = min(TOPK_MAX, S // 4)
    kpos = jnp.arange(S)
    to_blocks = lambda t: jnp.moveaxis(t.reshape((B, NB, CHUNK) + t.shape[2:]), 1, 0)

    def one(args):
        c, qb, qib, wib = args
        qpos = c * CHUNK + jnp.arange(CHUNK)
        vis_end = (c + 1) * CHUNK
        sc = jnp.where(kpos < vis_end, index_scores(qib, ki, wib), NEG)
        _, idx = lax.top_k(sc, k_sel)
        return sparse_attend(qb, ka, va, idx, idx < vis_end, qpos, t5_a)

    out = lax.map(one, (jnp.arange(NB), to_blocks(qa), to_blocks(qi), to_blocks(wi)))
    return jnp.moveaxis(out, 0, 1).reshape(B, S, H_A, HEAD_DIM)

def dsa_sample(qa, ka, va, qi, ki, wi, t5_a, past_len):
    T = qa.shape[1]
    k_sel = min(TOPK_MAX, ka.shape[1] // 4)
    _, idx = lax.top_k(index_scores(qi, ki, wi), k_sel)
    valid = jnp.ones(idx.shape, dtype=bool)
    return sparse_attend(qa, ka, va, idx, valid, past_len + jnp.arange(T), t5_a)

def mixer_prompt(h, w_in, w_out, qk_g, sinks, c_table, t5_table):
    B, S, _ = h.shape
    qa, ka, va, qi, ki, wi, qb, kb, vb, qc, kc, vc = project(h, w_in, qk_g)
    oa = dsa_prompt(qa, ka, va, qi, ki, wi, t5_table[:, :H_A])
    ob = band_attention(qb, kb, vb, B_PREV, t5_bias(band_rel(B_PREV), t5_table[:, H_A:]), sinks)
    oc = band_attention(qc, kc, vc, C_PREV, clip_bias(band_rel(C_PREV), c_table), None)
    o = jnp.concatenate([oa.reshape(B, S, -1), ob.reshape(B, S, -1), oc.reshape(B, S, -1)], axis=-1) @ w_out
    state = (ka, va, ki, kb[:, -WINDOW:], vb[:, -WINDOW:], kc[:, -C_REACH:], vc[:, -C_REACH:])
    return o, state

def mixer_sample(h, c_ak, c_av, c_aki, c_bk, c_bv, c_ck, c_cv, w_in, w_out, qk_g, sinks, c_table, t5_table):
    B, T, _ = h.shape
    past_len = c_ak.shape[1]
    qa, ka, va, qi, ki, wi, qb, kb, vb, qc, kc, vc = project(h, w_in, qk_g)
    ka_all = jnp.concatenate([c_ak, ka], axis=1)
    va_all = jnp.concatenate([c_av, va], axis=1)
    ki_all = jnp.concatenate([c_aki, ki], axis=1)
    oa = dsa_sample(qa, ka_all, va_all, qi, ki_all, wi, t5_table[:, :H_A], past_len)
    n_b = c_bk.shape[1]
    kb_all = jnp.concatenate([c_bk, kb], axis=1)
    vb_all = jnp.concatenate([c_bv, vb], axis=1)
    rel_b = jnp.arange(n_b + T)[None, :] - n_b - jnp.arange(T)[:, None]
    ob = attend(qb, kb_all, vb_all, t5_bias(rel_b, t5_table[:, H_A:]), None, sinks)
    n_c = c_ck.shape[1]
    kc_all = jnp.concatenate([c_ck, kc], axis=1)
    vc_all = jnp.concatenate([c_cv, vc], axis=1)
    rel_c = jnp.arange(n_c + T)[None, :] - n_c - jnp.arange(T)[:, None]
    oc = attend(qc, kc_all, vc_all, clip_bias(rel_c, c_table), None, None)
    o = jnp.concatenate([oa.reshape(B, T, -1), ob.reshape(B, T, -1), oc.reshape(B, T, -1)], axis=-1) @ w_out
    state = (ka, va, ki, kb_all[:, -n_b:], vb_all[:, -n_b:], kc_all[:, -n_c:], vc_all[:, -n_c:])
    return o, state

def setup_inputs(seed: int = 0) -> dict:
    key = jax.random.key(seed)
    ks = jax.random.split(key, 20)
    nrm = lambda k, shape, s: jax.random.normal(k, shape, jnp.float32) * s
    n_b = min(WINDOW, PAST_LEN)
    n_c = min(C_REACH, PAST_LEN)
    return {
        'x_prompt': nrm(ks[0], (BATCH, SEQ, D_MODEL), 1.0),
        'x_sample': nrm(ks[1], (DEC_BATCH, DEC_SEQ, D_MODEL), 1.0),
        'cache_a_k': nrm(ks[2], (DEPTH, DEC_BATCH, PAST_LEN, KV_A, HEAD_DIM), 1.0),
        'cache_a_v': nrm(ks[3], (DEPTH, DEC_BATCH, PAST_LEN, KV_A, HEAD_DIM), 1.0),
        'cache_a_kidx': nrm(ks[4], (DEPTH, DEC_BATCH, PAST_LEN, D_IDX), 1.0),
        'cache_b_k': nrm(ks[5], (DEPTH, DEC_BATCH, n_b, KV_B, HEAD_DIM), 1.0),
        'cache_b_v': nrm(ks[6], (DEPTH, DEC_BATCH, n_b, KV_B, HEAD_DIM), 1.0),
        'cache_c_k': nrm(ks[7], (DEPTH, DEC_BATCH, n_c, H_C, HEAD_DIM), 1.0),
        'cache_c_v': nrm(ks[8], (DEPTH, DEC_BATCH, n_c, H_C, HEAD_DIM), 1.0),
        'w_in': nrm(ks[9], (DEPTH, D_MODEL, D_IN), D_MODEL ** -0.5),
        'w_out': nrm(ks[10], (DEPTH, D_MIX, D_MODEL), D_MIX ** -0.5),
        'qk_norm': 1.0 + nrm(ks[11], (DEPTH, 6, HEAD_DIM), 0.01),
        'sinks': nrm(ks[12], (DEPTH, H_B), 0.5),
        'c_rel_bias': nrm(ks[13], (DEPTH, 2 * C_MAX_REL + 1, H_C), 0.1),
        't5_rel_bias': nrm(ks[14], (N_BUCKETS, H_A + H_B), 0.1),
        'norm_gains': 1.0 + nrm(ks[15], (DEPTH, 3, D_MODEL), 0.01),
        'w_ffn_gate': nrm(ks[16], (DEPTH, 2, D_MODEL, D_FF), D_MODEL ** -0.5),
        'w_ffn_up': nrm(ks[17], (DEPTH, 2, D_MODEL, D_FF), D_MODEL ** -0.5),
        'w_ffn_down': nrm(ks[18], (DEPTH, 2, D_FF, D_MODEL), D_FF ** -0.5),
    }

def reference(x_prompt, x_sample, cache_a_k, cache_a_v, cache_a_kidx, cache_b_k, cache_b_v, cache_c_k, cache_c_v,
              w_in, w_out, qk_norm, sinks, c_rel_bias, t5_rel_bias, norm_gains, w_ffn_gate, w_ffn_up, w_ffn_down):
    xp = x_prompt
    xs = x_sample
    p_states = []
    s_states = []
    for l in range(DEPTH):
        lw = (w_in[l], w_out[l], qk_norm[l], sinks[l], c_rel_bias[l], t5_rel_bias)
        ffn1 = (norm_gains[l, 0], w_ffn_gate[l, 0], w_ffn_up[l, 0], w_ffn_down[l, 0])
        ffn2 = (norm_gains[l, 2], w_ffn_gate[l, 1], w_ffn_up[l, 1], w_ffn_down[l, 1])
        xp = xp + 0.5 * swiglu_ffn(xp, *ffn1)
        xs = xs + 0.5 * swiglu_ffn(xs, *ffn1)
        op, sp = mixer_prompt(rmsnorm(xp, norm_gains[l, 1]), *lw)
        os_, ss = mixer_sample(rmsnorm(xs, norm_gains[l, 1]), cache_a_k[l], cache_a_v[l], cache_a_kidx[l],
                               cache_b_k[l], cache_b_v[l], cache_c_k[l], cache_c_v[l], *lw)
        xp = xp + op
        xs = xs + os_
        xp = xp + 0.5 * swiglu_ffn(xp, *ffn2)
        xs = xs + 0.5 * swiglu_ffn(xs, *ffn2)
        p_states.append(sp)
        s_states.append(ss)
    p_ak, p_av, p_aki, p_bk, p_bv, p_ck, p_cv = [jnp.stack(t, axis=0) for t in zip(*p_states)]
    s_ak, s_av, s_aki, s_bk, s_bv, s_ck, s_cv = [jnp.stack(t, axis=0) for t in zip(*s_states)]
    return (xp, xs, p_ak, p_av, p_aki, p_bk, p_bv, p_ck, p_cv, s_ak, s_av, s_aki, s_bk, s_bv, s_ck, s_cv)


_drawn_inputs = setup_inputs


def setup_inputs(seed=0):
    import zlib

    import numpy as np

    out = dict(_drawn_inputs(seed))
    spreads = {}
    factors = {'qk_norm': 5.254, 'sinks': 8.0, 'c_rel_bias': 7.729, 't5_rel_bias': 4.903}
    for name, (base, spread) in spreads.items():
        noise = np.random.default_rng([zlib.crc32(name.encode()), seed]).standard_normal(out[name].shape)
        drawn = base * np.exp(spread * noise) if base else spread * noise
        out[name] = __import__('jax').numpy.asarray(drawn.astype(out[name].dtype))
    for name, factor in factors.items():
        out[name] = (out[name] * factor).astype(out[name].dtype)
    return out
```

```python
from contextlib import ExitStack

import numpy as np

import concourse.bass as bass
from concourse import mybir

ALU = mybir.AluOpType
ACT = mybir.ActivationFunctionType
AX_X = mybir.AxisListType.X
F32 = mybir.dt.float32
F32R = mybir.dt.float32r

P = 128
HD = 64
CHUNK = 64
H_A, KV_A, H_IDX, H_B, KV_B, H_C = 12, 4, 8, 10, 2, 10
T5_BUCKETS, T5_MAX_DIST, C_MAX_REL = 32, 1024, 256
EPS = 1e-6
NEG = -1e30
TAKEN = -3e38
ATTN_SCALE = HD ** -0.5
IDX_SCALE = (H_IDX * HD) ** -0.5
VEC = 3 * P


def t5_onehot():
    nb = T5_BUCKETS // 2
    exact = nb // 2
    rel = 127 - np.arange(VEC)
    n = np.abs(rel)
    nf = np.maximum(n, exact).astype(np.float32)
    large = exact + (np.log(nf / np.float32(exact)) / np.float32(np.log(T5_MAX_DIST / exact))
                     * np.float32(nb - exact)).astype(np.int32)
    bucket = np.where(rel > 0, nb, 0) + np.where(n < exact, n, np.minimum(large, nb - 1))
    return (np.arange(T5_BUCKETS)[:, None] == bucket[None, :]).astype(np.float32)


class Phase:

    def __init__(self, name, strips, tiles, n0, ld0, **more):
        self.name, self.strips, self.tiles, self.n0, self.ld0 = name, strips, tiles, n0, ld0
        self.more = more


def plan_phases(d_tiles, f_tiles):
    phases, n, ld = [], 0, 0
    thirds = [f_tiles - 2 * (f_tiles // 3), f_tiles // 3, f_tiles // 3]

    def add(name, strips, tiles, **more):
        nonlocal n, ld
        phases.append(Phase(name, strips, tiles, n, 0 if name == "wo" else ld, **more))
        n += strips
        ld += 0 if name == "wo" else strips // 2

    for ffn in range(2):
        f0 = 0
        for t, size in enumerate(thirds):
            add("up", 2 * size, d_tiles, ffn=ffn, f0=f0, size=size, first=t == 0)
            add("down", d_tiles, size, ffn=ffn, f0=f0, size=size, last=t == 2)
            f0 += size
        if ffn == 0:
            add("prep", 12, d_tiles)
            add("cb", 20, d_tiles)
            add("a", 6, d_tiles)
            add("wo", d_tiles, 16)
    for a, b in zip(phases, phases[1:]):
        a.next = b
    phases[-1].next = None
    return phases


def encoder_step(nc, xp, xs, cak, cav, caki, cbk, cbv, cck, ccv, w_in, w_out, qk_norm, sinks, c_bias, t5_bias,
                 gains, w_gate, w_up, w_down, onehot,
                 yp, ys, pak, pav, paki, pbk, pbv, pck, pcv, sak, sav, saki, sbk, sbv, sck, scv):
    T_P, D = xp.shape[1:]
    T_S = xs.shape[1]
    PAST = cak.shape[2]
    D_IN = w_in.shape[2]
    D_FF = w_gate.shape[3]
    NT = T_P + T_S
    DT, FT = D // P, D_FF // P
    assert T_P == 2 * P and T_S == 32 and PAST == P and w_out.shape[1] == 16 * P
    assert cbk.shape[2] == P and cck.shape[2] == P
    K_P, K_S = T_P // 4, (PAST + T_S) // 4
    phases = plan_phases(DT, FT)
    thirds = [p.more["size"] for p in phases if p.name == "up"][:3]

    o_qa = 0
    o_ka = o_qa + H_A * HD
    o_va = o_ka + KV_A * HD
    o_qi = o_va + KV_A * HD
    o_ki = o_qi + H_IDX * HD
    o_wi = o_ki + HD
    o_qb = o_wi + H_IDX
    o_kb = o_qb + H_B * HD
    o_vb = o_kb + KV_B * HD
    o_qc = o_vb + KV_B * HD
    o_kc = o_qc + H_C * HD
    o_vc = o_kc + H_C * HD
    assert o_vc + H_C * HD == D_IN

    ctx = ExitStack()
    with ctx:
        def sb(name, shape, dt=F32, scope=ctx):
            return scope.enter_context(nc.sbuf_tensor(name, shape, dt))

        def sem(name):
            return ctx.enter_context(nc.semaphore(name))

        xT = sb("xT", [P, DT, NT])
        h_hi = sb("h_hi", [P, DT, NT], F32R)
        h_lo = sb("h_lo", [P, DT, NT], F32R)
        raw = [sb(f"raw{s}", [P, 16, P]) for s in range(2)]
        w_hi = [sb(f"w_hi{s}", [P, 16, P], F32R) for s in range(2)]
        w_lo = [sb(f"w_lo{s}", [P, 16, P], F32R) for s in range(2)]
        with ExitStack() as ffn_scope:
            gu_hi = sb("gu_hi", [P, thirds[0], NT], F32R, ffn_scope)
            gu_lo = sb("gu_lo", [P, thirds[0], NT], F32R, ffn_scope)
        o_hi = sb("o_hi", [P, 16, NT], F32R)
        o_lo = sb("o_lo", [P, 16, NT], F32R)
        ident = sb("ident", [P, P])
        flip = sb("flip", [P, P])
        mean_d = sb("mean_d", [P, P])
        mean_hd = sb("mean_hd", [P, P])
        eps = sb("eps", [P, 1])
        g_cols = sb("g_cols", [P, 3 * DT])
        qk_cols = sb("qk_cols", [P, 6])
        sink_rows = sb("sink_rows", [P, 2, 5])
        neg_sinks = sb("neg_sinks", [P, 2, 5])
        rstd = sb("rstd", [P, NT])
        sumsq = sb("sumsq", [P, NT])
        sqx = sb("sqx", [P, NT])
        sd_x = sb("sd_x", [P, NT])
        KEYS = T_P + PAST + T_S
        kt_a = sb("kt_a", [P, 2, KEYS])
        kt_b = sb("kt_b", [P, KEYS])
        kt_i = [sb(f"kt_i{c}", [P, KEYS]) for c in range(2)]
        kt_c = sb("kt_c", [P, KEYS])
        kc_cache = sb("kc_cache", [P, 5, P])
        v_a = sb("v_a", [P, 4, 2 * P])
        v_b = sb("v_b", [P, 4, P])
        with ExitStack() as scope:
            xrow = sb("xrow", [P, 3, D], F32, scope)
        with ExitStack() as scope:
            g_act = sb("g_act", [P, NT], F32, scope)
            g_sig = sb("g_sig", [P, NT], F32, scope)
            u_act = sb("u_act", [P, NT], F32, scope)
            gu = sb("gu", [P, NT], F32, scope)
            y_rows = sb("y_rows", [P, 2, 3, P], F32, scope)
        z_prep = sb("z_prep", [P, 10, NT])
        z_q = [sb(f"z_q{s}", [P, NT]) for s in range(2)]
        z_k = sb("z_k", [P, NT])
        z_v = sb("z_v", [P, NT])
        zw = z_v[0:H_IDX, :]
        q_n = [[sb(f"q_n{s}_{c}", [P, NT]) for c in range(2)] for s in range(2)]
        sq = sb("sq", [P, NT])
        sd = sb("sd", [P, NT])
        rinv = sb("rinv", [P, NT])
        v_c = sb("v_c", [P, 4, P])
        with ExitStack() as scope:
            gain_rows = sb("gain_rows", [3 * DT, P], F32, scope)
            qk_rows = sb("qk_rows", [6, P], F32, scope)
            t5_rows = sb("t5_rows", [T5_BUCKETS, H_A + H_B], F32, scope)
            hot = sb("hot", [T5_BUCKETS, VEC], F32, scope)
            c_rows = sb("c_rows", [P, 3, H_C], F32, scope)
            cache_rows = sb("cache_rows", [P, 9, P], F32, scope)
            vec_t5 = sb("vec_t5", [H_A + H_B, VEC], F32, scope)
            vec_c = sb("vec_c", [H_C, VEC], F32, scope)
        k_rows = sb("k_rows", [P, 3, P])
        s_buf = [sb(f"s_buf{s}", [P, 2, T_P]) for s in range(2)]
        p_t = [sb(f"p_t{s}", [P, 4, P]) for s in range(2)]
        bias_rev = [sb(f"bias_rev{s}", [P, 2, T_P]) for s in range(2)]
        idx_acc = [sb(f"idx_acc{r}", [P, n]) for r, n in enumerate((2 * P, P, PAST + T_S))]
        a_mask = [sb(f"a_mask{r}", [P, n]) for r, n in enumerate((2 * P, P, PAST + T_S))]
        nmax = [sb(f"nmax{s}", [P, 2]) for s in range(2)]
        snk = [sb(f"snk{s}", [P, 2]) for s in range(2)]
        esnk = [sb(f"esnk{s}", [P, 2]) for s in range(2)]
        esum = [sb(f"esum{s}", [P, 2]) for s in range(2)]
        einv = [sb(f"einv{s}", [P, 2]) for s in range(2)]
        w_tok = sb("w_tok", [P, 3, H_IDX])
        top8 = sb("top8", [P, 8])
        CACHE_TILES = [(cache_rows[:, 0, :], kt_a[:, 0, T_P:T_P + PAST]), (cache_rows[:, 1, :], kt_a[:, 1, T_P:T_P + PAST]),
                       (cache_rows[:, 2, :], None), (cache_rows[:, 3, :], kt_b[:, T_P:T_P + PAST])]
        CACHE_TILES += [(cache_rows[:, 4 + i, :], kc_cache[:, i, :]) for i in range(5)]

        psum = [ctx.enter_context(nc.psum_tensor(f"bank{b}", [P, 512], F32)) for b in range(8)]
        bank_w = psum[0:2]
        bank_s = psum[2:4]
        bank_t = psum[4:6]
        bank_o = psum[6]
        bank_m = psum[7]

        vec_dram = nc.dram_tensor("bias_vectors", (H_A + H_B + H_C, VEC), F32, kind="Internal").ap()

        ld = [sem("strip_loaded0"), sem("strip_loaded1")]
        ld_wo = [sem("wo_strip_loaded0"), sem("wo_strip_loaded1")]
        hi_rdy = sem("w_hi_ready")
        lo_rdy = sem("w_lo_ready")
        used = sem("strip_multiplied")
        evac = sem("product_read")
        x_in = sem("x_loaded")
        small_in = sem("small_inputs_loaded")
        cache_in = sem("cache_rows_loaded")
        vcache_in = sem("v_cache_loaded")
        pool_built = sem("pool_constants_cleared")
        consts = sem("constants_built")
        start_tr = sem("start_transposed")
        start_cp = sem("start_copied")
        vec_out = sem("bias_vectors_stored")
        sqx_rdy = sem("x_squares_ready")
        acc_rdy = sem("x_squares_summed")
        hhi_rdy = sem("h_hi_ready")
        hlo_rdy = sem("h_lo_ready")
        rstd_rdy = sem("x_rstd_ready")
        sig_rdy = sem("silu_ready")
        gu_rdy = sem("gated_ready")
        guh_rdy = sem("gated_hi_ready")
        gul_rdy = sem("gated_lo_ready")
        m_done = sem("misc_bank_written")
        m_free = sem("misc_bank_read")
        sq_rdy = sem("squares_ready")
        rinv_rdy = sem("inverse_norm_ready")
        qk_rdy = sem("qk_tile_normalized")
        qk_done = sem("scores_done")
        s_add = sem("scores_biased")
        masked = sem("unselected_masked")
        mx_raw = sem("sink_max_step")
        sum_sunk = sem("sink_added")
        mx_rdy = sem("neg_max_ready")
        e_rdy = sem("exponentials_ready")
        r_rdy = sem("inverse_sums_ready")
        p_rdy = sem("probabilities_ready")
        t_done = sem("probabilities_transposed")
        c_done = sem("transposed_copied")
        pv_done = sem("unit_output_done")
        ohi_rdy = sem("output_hi_ready")
        olo_rdy = sem("output_lo_ready")
        bias_ld = [sem("bias_loaded0"), sem("bias_loaded1")]
        bias_rdy = sem("bias_ready")
        window_msk = sem("bias_window_masked")
        kc_rdy = sem("c_key_cache_placed")
        vc_ld = sem("c_value_cache_loaded")
        v_out = sem("v_rows_stored")
        k_out = sem("k_rows_stored")
        misc_out = sem("cache_tails_stored")
        iq_done = sem("index_products_done")
        irelu = sem("index_relu_done")
        iacc = sem("index_scores_summed")
        mask_rdy = sem("selection_ready")
        y_tr = sem("y_transposed")
        y_cp = sem("y_copied")
        y_out = [sem("y_stored0"), sem("y_stored1")]
        pe_passed = sem("narrow_product_begins")
        pool_passed = sem("pool_passed_wait")
        dve_link = sem("vector_step")

        block = ctx.enter_context(nc.Block())

        TOK = [slice(P, 2 * P), slice(0, P), slice(T_P, NT)]
        ROWS = [P, P, T_S]
        NKEY = [T_P, P, PAST + T_S]
        KEY0 = [0, 0, T_P]
        PREP = {"ka": (0, 2), "va": (2, 4), "qi": (4, 8), "kb": (8, 9), "vb": (9, 10)}
        CONSTS = 3

        def strip_no(ph, j, s):
            return j * 2 + (ph.n0 + s)

        def following(ph, j, s):
            if s == 0:
                return ph, j, 1
            if isinstance(j, int) and j == ph.strips // 2 - 1:
                return (ph.next, 0, 0) if ph.next else None
            return ph, j + 1, 0

        def bodies(eng, ph, body, peel_first=False, strips=2):
            count = ph.strips // strips
            start = 1 if peel_first else 0
            if peel_first:
                body(0)
            with eng.Fori(start, count - 1) as i:
                body(i)
            body(count - 1)

        idx_units = [(r, t) for r in range(3) for t in range(4)]
        PREP_ITEMS = {
            8: [("n", "ka0"), ("v", "va0")],
            9: [("n", "ka1"), ("v", "va1")],
            10: [("w",)] + [("i", u) for u in range(0, 4)],
            11: [("i", u) for u in range(4, 12)],
            12: [("n", "kb"), ("v", "vb"), ("t", 0)],
            13: [("k", "ka0"), ("t", 1)],
            14: [("k", "ka1"), ("t", 2), ("n", "q0")],
            15: [("n", "q1"), ("k", "ki"), ("k", "kb"), ("n", "kc")],
        }
        misc_no, norm_no, kout_no, vout_no = {}, {}, {}, {}
        at = 1 + 1
        for step in range(8, 16):
            for it in PREP_ITEMS[step]:
                if it[0] in "nvkw":
                    misc_no[it] = at
                    at += 1
                if it[0] == "n":
                    norm_no[it] = len(norm_no)
                if it[0] == "k":
                    kout_no[it] = len(kout_no)
                if it[0] == "v":
                    vout_no[it] = len(vout_no)
        MISC_CB0, NORM_CB0 = at, len(norm_no)
        MISC_A0, NORM_A0 = MISC_CB0 + 5 * 4, NORM_CB0 + 3 * 4
        MISC_A1 = MISC_A0 + 2 + 2
        MISC_END = MISC_A1 + 2 * 2
        VOUT_PREP, KOUT_PREP = len(vout_no), len(kout_no)

        def norm_source(name):
            if name in ("q0", "q1"):
                s = int(name[1])
                return z_q[s], None, [(q_n[s][c][c * HD:(c + 1) * HD, :], slice(0, NT), slice(c * HD, (c + 1) * HD)) for c in range(2)]
            kt, z, g = {"ka0": (kt_a[:, 0, :], z_prep[:, 0, :], 1), "ka1": (kt_a[:, 1, :], z_prep[:, 1, :], 1),
                        "kb": (kt_b[:, :], z_prep[:, 8, :], 3), "kc": (kt_c[:, :], z_k[:, :], 5)}[name]
            return z, g, [(kt[:, 0:T_P], slice(0, T_P), slice(0, P)), (kt[:, T_P + PAST:KEYS], slice(T_P, NT), slice(0, P))]

        @block.sync
        def _(sp):
            for t in range(2):
                sp.dma_start(xrow[:, t, :], xp[0, t * P:(t + 1) * P, :]).then_inc(x_in, 16)
            sp.dma_start(xrow[0:T_S, 2, :], xs[0]).then_inc(x_in, 16)

            def pieces(ph, j, s):
                half = [slice(0, 8), slice(8, ph.tiles)]
                m = ph.more
                if ph.name == "up":
                    w = (w_gate if s == 0 else w_up)[0, m["ffn"]].rearrange("(k p) n -> p k n", p=P)
                    col = bass.ds(j * P + m["f0"] * P, P)
                    return [(raw[s][:, k, :], w[:, k, col]) for k in half]
                if ph.name == "down":
                    f0, f1 = m["f0"], m["f0"] + m["size"]
                    w = w_down[0, m["ffn"], f0 * P:f1 * P].rearrange("(k p) n -> p k n", p=P)
                    col = bass.ds(j * 2 * P + s * P, P)
                    return [(raw[s][:, k, :], w[:, k, col]) for k in half]
                w = w_in[0].rearrange("(k p) n -> p k n", p=P)
                if ph.name == "prep":
                    if not isinstance(j, int) or j < 4:
                        col = bass.ds(j * 2 * P + (o_ka + s * P), P)
                        return [(raw[s][:, k, :], w[:, k, col]) for k in half]
                    if (j, s) == (4, 0):
                        return [(raw[s][:, :, c:c + HD], w[:, :, o_ki:o_ki + HD]) for c in (0, HD)]
                    if (j, s) == (4, 1):
                        return [(raw[s][:, k, 0:H_IDX], w[:, k, o_wi:o_wi + H_IDX]) for k in half]
                    col = slice(o_kb, o_kb + P) if s == 0 else slice(o_vb, o_vb + P)
                    return [(raw[s][:, k, :], w[:, k, col]) for k in half]
                raise AssertionError(ph.name)

            def w_in_cols(s, cols):
                w = w_in[0].rearrange("(k p) n -> p k n", p=P)
                if len(cols) == 1:
                    return [(raw[s][:, k, :], w[:, k, cols[0]]) for k in (slice(0, 8), slice(8, 16))]
                return [(raw[s][:, :, c * HD:(c + 1) * HD], w[:, :, cols[c]]) for c in range(2)]

            def load(ph, j, s, what=None):
                n = strip_no(ph, j, s)
                if not (isinstance(n, int) and n < 2):
                    sp.wait_ge(lo_rdy, n * 2 - 2)
                for dst, src in what or pieces(ph, j, s):
                    sp.dma_start(dst, src).then_inc(ld[s], 16)

            for ph in phases:
                if ph.name in ("up", "down"):
                    first = 1 if ph.n0 == 0 else 0
                    if first:
                        load(ph, 0, 0)
                        load(ph, 0, 1)
                    with sp.Fori(first, ph.strips // 2) as j:
                        load(ph, j, 0)
                        load(ph, j, 1)
                elif ph.name == "prep":
                    with sp.Fori(0, 4) as j:
                        load(ph, j, 0)
                        load(ph, j, 1)
                    for j in (4, 5):
                        load(ph, j, 0)
                        load(ph, j, 1)
                elif ph.name == "cb":
                    with sp.Fori(0, 5) as i:
                        load(ph, i * 2, 0, w_in_cols(0, [bass.ds(i * P + o_qc, P)]))
                        load(ph, i * 2, 1, w_in_cols(1, [bass.ds(i * HD + o_qb, HD), bass.ds(i * HD + (o_qb + 5 * HD), HD)]))
                        load(ph, i * 2 + 1, 0, w_in_cols(0, [bass.ds(i * P + o_kc, P)]))
                        load(ph, i * 2 + 1, 1, w_in_cols(1, [bass.ds(i * P + o_vc, P)]))
                elif ph.name == "a":
                    with sp.Fori(0, 3) as i:
                        for s in range(2):
                            c = o_qa + s * 6 * HD
                            load(ph, i, s, w_in_cols(s, [bass.ds(i * HD + c, HD), bass.ds(i * HD + (c + 3 * HD), HD)]))
                else:
                    wo = w_out[0]
                    with sp.Fori(0, ph.strips // 2) as j:
                        for s in range(2):
                            sp.wait_ge(lo_rdy, strip_no(ph, j, s) * 2 - 2)
                            col = bass.ds(j * 2 * P + s * P, P)
                            for g in range(2):
                                for c in range(2):
                                    r = (6 * g + 3 * c) * HD
                                    sp.dma_start(raw[s][c * HD:(c + 1) * HD, 3 * g:3 * g + 3, :],
                                                 wo[r:r + 3 * HD, col].rearrange("(k p) n -> p k n", p=HD)).then_inc(ld_wo[s], 16)
                            for c in range(2):
                                r = (H_A + 5 * c) * HD
                                sp.dma_start(raw[s][c * HD:(c + 1) * HD, 6:11, :],
                                             wo[r:r + 5 * HD, col].rearrange("(k p) n -> p k n", p=HD)).then_inc(ld_wo[s], 16)
                            r = (H_A + H_B) * HD
                            sp.dma_start(raw[s][:, 11:16, :],
                                         wo[r:r + 5 * P, col].rearrange("(k p) n -> p k n", p=P)).then_inc(ld_wo[s], 16)
        WO_LOADS = 7

        @block.tensor
        def _(pe):
            def products(ph, j, s, rhs, ks, n, first_k, last_k, when=None):
                for k in ks:
                    if when:
                        when(k)
                    hi, lo = rhs(k)
                    out = bank_w[s][:, 0:NT]
                    pe.matmul(out, w_hi[s][:, k, :], hi, start=(k == first_k), stop=False)
                    pe.matmul(out, w_hi[s][:, k, :], lo, start=False, stop=False)
                    mm = pe.matmul(out, w_lo[s][:, k, :], hi, start=False, stop=(k == last_k))
                return mm

            def strip(ph, j, s, rhs, when=None, part=None):
                n = strip_no(ph, j, s)
                if part in (None, 0):
                    if not (isinstance(n, int) and n < 2):
                        pe.wait_ge(evac, n - 1)
                    pe.wait_ge(lo_rdy, n * 2 + 1)
                    mm = products(ph, j, s, rhs, range(0, 8), n, 0, ph.tiles - 1, when)
                if part in (None, 1):
                    pe.wait_ge(lo_rdy, n * 2 + 2)
                    mm = products(ph, j, s, rhs, range(8, ph.tiles), n, 0, ph.tiles - 1, when)
                    mm.then_inc(used, 1)

            def narrow_strip(ph, j, s, rhs, m):
                n = strip_no(ph, j, s)
                pe.wait_ge(evac, n - 1)
                pe.wait_ge(lo_rdy, n * 2 + 2)
                out = bank_w[s][0:m, 0:NT]
                for k in range(ph.tiles):
                    hi, lo = rhs(k)
                    pe.matmul(bank_w[s][:, 0:NT], w_hi[s][:, k, :], hi, start=(k == 0), stop=False)
                    pe.matmul(bank_w[s][:, 0:NT], w_hi[s][:, k, :], lo, start=False, stop=False)
                    mm = pe.matmul(bank_w[s][:, 0:NT], w_lo[s][:, k, :], hi, start=False, stop=(k == ph.tiles - 1))
                mm.then_inc(used, 1)

            def h_rhs(k):
                return h_hi[:, k, :], h_lo[:, k, :]

            def gu_rhs(k):
                return gu_hi[:, k, :], gu_lo[:, k, :]

            def o_rhs(k):
                return o_hi[:, k, :], o_lo[:, k, :]

            def misc_begin(m):
                if not (isinstance(m, int) and m == 0):
                    pe.wait_ge(m_free, m)

            def x_norm(index):
                pe.wait_ge(acc_rdy, DT * (index + 1))
                misc_begin([0, 1, MISC_END][index])
                pe.matmul(bank_m[:, 0:NT], mean_d[:, :], sumsq[:, :], start=True, stop=True).then_inc(m_done, 1)

            def head_sum(m, q):
                pe.wait_ge(sq_rdy, q + 1)
                misc_begin(m)
                pe.matmul(bank_m[:, 0:NT], mean_hd[:, :], sq[:, :], start=True, stop=True).then_inc(m_done, 1)

            def turn_rows(m, tile, sample0):
                misc_begin(m)
                for t in range(2):
                    pe.transpose(bank_m[:, t * P:(t + 1) * P], tile[:, t * P:(t + 1) * P], ident[:, :])
                pe.transpose(bank_m[0:T_S, 2 * P:3 * P], tile[:, sample0:sample0 + T_S], ident[:, :]).then_inc(m_done, 1)

            def settled():
                pe.sem_inc(pe_passed, 1)

            def scores(U, r, b, q, kt):
                if not (isinstance(U, int) and U < 2):
                    pe.wait_ge(s_add, U - 1)
                out = bank_s[b]
                for c in range(2):
                    mm = pe.matmul(out[0:ROWS[r], c * NKEY[r]:(c + 1) * NKEY[r]], q[c][:, TOK[r]],
                                   kt[:, KEY0[r]:KEY0[r] + NKEY[r]], start=True, stop=True)
                mm.then_inc(qk_done, 1)

            def turn_p(U, r, b):
                pe.wait_ge(p_rdy, U + 1)
                if not (isinstance(U, int) and U < 2):
                    pe.wait_ge(c_done, U - 1)
                m = ROWS[r]
                if r == 2:
                    settled()
                for c in range(2):
                    if r < 2:
                        for kc in range(NKEY[r] // P):
                            o = (c * (NKEY[r] // P) + kc) * P
                            mm = pe.transpose(bank_t[b][:, o:o + P], s_buf[b][:, c, kc * P:(kc + 1) * P], ident[:, :])
                    else:
                        pe.transpose(bank_t[b][:, c * P:c * P + m], s_buf[b][0:m, c, 0:P], ident[0:m, 0:m])
                        mm = pe.transpose(bank_t[b][0:T_S, (2 + c) * P:(2 + c) * P + m], s_buf[b][0:m, c, P:P + T_S],
                                          ident[0:m, 0:m])
                mm.then_inc(t_done, 1)

            def out_v(U, r, b, pr, v):
                pe.wait_ge(c_done, U + 1)
                if r == 0 and not (isinstance(pr, int) and pr < 1):
                    pe.wait_ge(olo_rdy, pr)
                for c in range(2):
                    out = bank_o[c * HD:(c + 1) * HD, TOK[r]]
                    cols = slice(c * HD, (c + 1) * HD)
                    if r < 2:
                        nk = NKEY[r] // P
                        for kc in range(nk):
                            mm = pe.matmul(out, v[:, kc, cols], p_t[b][:, c * nk + kc, :], start=(kc == 0), stop=(kc == nk - 1))
                    else:
                        pe.matmul(out, v[:, 2, cols], p_t[b][:, c, 0:T_S], start=True, stop=False)
                        mm = pe.matmul(out, v[0:T_S, 3, cols], p_t[b][0:T_S, 2 + c, 0:T_S], start=False, stop=True)
                mm.then_inc(pv_done, 1)

            def attention_hooks(kind, body, norms_done, strips_done, norms, turn):
                U, pr = body * 6, body * 2
                if kind == "cb":
                    kt, v = [kt_c, kt_b], [v_c, v_b]
                else:
                    kt, v = [kt_a[:, 0, :], kt_a[:, 1, :]], [v_a[:, :, 0:P], v_a[:, :, P:2 * P]]

                def sc(u):
                    p, r = divmod(u, 3)
                    if r == 2 and p == 0 and kind == "cb":
                        pe.wait_ge(kc_rdy, body + 1)
                    scores(U + u, r, u % 2, q_n[p], kt[p])

                def tp(u):
                    turn_p(U + u, u % 3, u % 2)

                def pv(u):
                    p, r = divmod(u, 3)
                    if u == 0 and kind == "cb":
                        pe.wait_ge(m_free, turn + 1)
                        pe.wait_ge(vc_ld, body * 16 + 16)
                    out_v(U + u, r, u % 2, pr + p, v[p])

                def hook0():
                    pe.wait_ge(qk_rdy, norms_done)
                    if kind == "cb":
                        pe.wait_ge(evac, strips_done)
                        turn_rows(turn, z_v, T_P)
                        turn_rows(turn + 1, kt_c, T_P + PAST)
                    sc(0), sc(1)

                def hook1():
                    tp(0), tp(1), sc(2), sc(3)

                def hook2():
                    pv(0), pv(1), tp(2), tp(3), sc(4), sc(5)
                    if norms:
                        head_sum(*norms[0])

                def hook3():
                    pv(2), pv(3), tp(4), tp(5)
                    if norms:
                        head_sum(*norms[1])
                    pv(4), pv(5)
                    if len(norms) > 2:
                        head_sum(*norms[2])
                return hook0, hook1, hook2, hook3

            def prep_items(step):
                for it in PREP_ITEMS[step]:
                    if it[0] == "n":
                        head_sum(misc_no[it], norm_no[it])
                    elif it[0] == "v":
                        if it[1] == "vb":
                            pe.wait_ge(evac, phase["prep"].n0 + 12)
                            turn_rows(misc_no[it], z_prep[:, 9, :], T_P)
                        else:
                            pe.wait_ge(evac, phase["prep"].n0 + 4)
                            turn_rows(misc_no[it], z_prep[:, 2 + int(it[1][2]), :], T_P)
                    elif it[0] == "k":
                        kt = {"ka0": kt_a[:, 0, :], "ka1": kt_a[:, 1, :], "ki": kt_i[0], "kb": kt_b}[it[1]]
                        if it[1] != "ki":
                            pe.wait_ge(qk_rdy, norm_no[("n", it[1])] + 1)
                        turn_rows(misc_no[it], kt, T_P + PAST)
                    elif it[0] == "w":
                        misc_begin(misc_no[it])
                        pe.wait_ge(evac, phase["prep"].n0 + 10)
                        for t, (a, b) in enumerate(((0, P), (P, 2 * P), (2 * P, NT))):
                            mm = pe.transpose(bank_m[0:b - a, t * H_IDX:(t + 1) * H_IDX], zw[:, a:b], ident[0:H_IDX, 0:H_IDX])
                        mm.then_inc(m_done, 1)
                    elif it[0] == "i":
                        u = it[1]
                        r, t = idx_units[u]
                        pe.wait_ge(evac, phase["prep"].n0 + 9)
                        if u >= 2:
                            pe.wait_ge(irelu, u - 1)
                        for c in range(2):
                            mm = pe.matmul(bank_s[u % 2][0:ROWS[r], c * NKEY[r]:(c + 1) * NKEY[r]],
                                           z_prep[:, 4 + t, TOK[r]], kt_i[c][:, KEY0[r]:KEY0[r] + NKEY[r]],
                                           start=True, stop=True)
                        mm.then_inc(iq_done, 1)

            phase = {p.name: p for p in phases if p.name not in ("up", "down")}

            pe.wait_ge(consts, CONSTS)
            pe.wait_ge(small_in, 16 * 7)
            start_bank = [0]

            def start_slot():
                n = start_bank[0]
                start_bank[0] += 1
                if n >= 2:
                    pe.wait_ge(start_cp, n - 1)
                return bank_t[n % 2]

            b = start_slot()
            pe.transpose(b[:, 0:3 * DT], gain_rows[:, :], ident[0:3 * DT, 0:3 * DT])
            pe.transpose(b[:, 3 * DT:3 * DT + 6], qk_rows[:, :], ident[0:6, 0:6]).then_inc(start_tr, 1)
            pe.wait_ge(x_in, 48)
            for k in range(DT):
                b = start_slot()
                for t in range(2):
                    pe.transpose(b[:, t * P:(t + 1) * P], xrow[:, t, k * P:(k + 1) * P], ident[:, :])
                pe.transpose(b[:, T_P:NT], xrow[0:T_S, 2, k * P:(k + 1) * P], ident[0:T_S, 0:T_S]).then_inc(start_tr, 1)
            b = start_slot()
            pe.matmul(b[0:H_A + H_B, 0:VEC], t5_rows[:, :], hot[:, :],
                      start=True, stop=True).then_inc(start_tr, 1)
            b = start_slot()
            for blk in range(3):
                c0 = (2 - blk) * P
                mm = pe.matmul(b[0:H_C, c0:c0 + P], c_rows[:, blk, :], flip[:, :], start=True, stop=True)
            mm.then_inc(start_tr, 1)
            pe.wait_ge(cache_in, 16 * 5)
            for src, _ in CACHE_TILES:
                b = start_slot()
                pe.transpose(b[:, 0:P], src, ident[:, :]).then_inc(start_tr, 1)

            def h_when(index):
                def when(k):
                    pe.wait_ge(hlo_rdy, DT * index + k + 1)
                return when

            gated = 0
            for ph in phases:
                if ph.name == "up":
                    if ph.more["first"]:
                        index = 2 * ph.more["ffn"]
                        strip(ph, 0, 0, h_rhs, h_when(index))
                        x_norm(index)
                        strip(ph, 0, 1, h_rhs)
                    with pe.Fori(1 if ph.more["first"] else 0, ph.strips // 2) as j:
                        strip(ph, j, 0, h_rhs)
                        strip(ph, j, 1, h_rhs)
                elif ph.name == "down":
                    last = ph.tiles - 1

                    def gu_when(k, g=gated, last=last):
                        if k == 0:
                            pe.wait_ge(gul_rdy, g + last)
                        if k == last:
                            pe.wait_ge(gul_rdy, g + last + 1)
                    with pe.Fori(0, ph.strips // 2) as j:
                        strip(ph, j, 0, gu_rhs, gu_when)
                        strip(ph, j, 1, gu_rhs, gu_when)
                    gated += ph.tiles
                elif ph.name == "prep":
                    strip(ph, 0, 0, h_rhs, h_when(1))
                    x_norm(1)
                    strip(ph, 0, 1, h_rhs)
                    with pe.Fori(1, 4) as j:
                        strip(ph, j, 0, h_rhs)
                        strip(ph, j, 1, h_rhs)
                    strip(ph, 4, 0, h_rhs)
                    prep_items(8)
                    narrow_strip(ph, 4, 1, h_rhs, H_IDX)
                    prep_items(9)
                    strip(ph, 5, 0, h_rhs)
                    prep_items(10)
                    strip(ph, 5, 1, h_rhs)
                    prep_items(11)
                    pe.wait_ge(vcache_in, 32)
                elif ph.name == "cb":
                    for t in range(4):
                        strip(ph, t // 2, t % 2, h_rhs)
                        prep_items(12 + t)
                    def cb_body(i, ph=ph):
                        m, q = i * 5 + (MISC_CB0 - 5), i * 3 + (NORM_CB0 - 3)
                        hooks = attention_hooks("cb", i - 1, q, i * 4 + ph.n0, [(m + 2, q), (m + 3, q + 1), (m + 4, q + 2)], m)
                        for t in range(4):
                            strip(ph, i * 2 + t // 2, t % 2, h_rhs)
                            hooks[t]()
                    cb_body(1)
                    with pe.Fori(2, 5) as i:
                        cb_body(i)
                elif ph.name == "a":
                    hooks = attention_hooks("cb", 4, NORM_A0, ph.n0, [(MISC_A0 + 2, NORM_A0), (MISC_A0 + 3, NORM_A0 + 1)], MISC_A0)
                    for t in range(4):
                        strip(ph, 0, t // 2, h_rhs, part=t % 2)
                        hooks[t]()
                    with pe.Fori(1, 3) as i:
                        m, q = i * 2 + (MISC_A1 - 2), i * 2 + NORM_A0
                        hooks = attention_hooks("a", i + 4, q, None, [(m, q), (m + 1, q + 1)], None)
                        for t in range(4):
                            strip(ph, i, t // 2, h_rhs, part=t % 2)
                            hooks[t]()
                else:
                    hooks = attention_hooks("a", 7, NORM_A0 + 6, None, [], None)
                    order = [11, 12, 13, 14, 15, 6, 7, 8, 9, 10, 0, 3, 1, 4, 2, 5]

                    def wo(j, s, ks):
                        n = strip_no(ph, j, s)
                        if ks[0] == order[0]:
                            pe.wait_ge(evac, n - 1)
                            pe.wait_ge(lo_rdy, n * 2 + 2)
                        mm = products(ph, j, s, o_rhs, ks, n, order[0], order[-1])
                        if ks[-1] == order[-1]:
                            mm.then_inc(used, 1)
                    pe.wait_ge(olo_rdy, 10)
                    hooks[0]()
                    wo(0, 0, order[0:5])
                    hooks[1]()
                    wo(0, 0, order[5:10])
                    hooks[2]()
                    pe.wait_ge(olo_rdy, 14)
                    wo(0, 0, order[10:14])
                    wo(0, 1, order[0:5])
                    hooks[3]()
                    wo(0, 1, order[5:14])
                    pe.wait_ge(olo_rdy, 16)
                    wo(0, 0, order[14:16])
                    wo(0, 1, order[14:16])
                    with pe.Fori(1, ph.strips // 2) as j:
                        wo(j, 0, order)
                        wo(j, 1, order)
            for k in range(DT):
                pe.wait_ge(evac, phases[-1].n0 + k + 1)
                if k >= 2:
                    pe.wait_ge(y_cp, k - 1)
                for t in range(2):
                    pe.transpose(bank_t[k % 2][:, t * P:(t + 1) * P], xT[:, k, t * P:(t + 1) * P], ident[:, :])
                pe.transpose(bank_t[k % 2][0:T_S, 2 * P:3 * P], xT[:, k, T_P:NT], ident[:, :]).then_inc(y_tr, 1)

        PAIR_TILE = {"c": 11, "b": 6}
        START_COPIES = 1 + DT + 2 + 9

        def v_place(name):
            if name == "vb":
                cols = slice(0, P)
                flat = lambda t: t[0, 0].rearrange("t h d -> t (h d)")
                return v_b, cols, flat(pbv), flat(sbv)[P - T_S:P], 1
            t = int(name[2])
            cols = slice(t * P, (t + 1) * P)
            flat = lambda x: x[0, 0].rearrange("t h d -> t (h d)")[:, cols]
            return v_a, cols, flat(pav), flat(sav), 0

        def k_place(name):
            flat = lambda x: x[0, 0].rearrange("t h d -> t (h d)")
            if name == "ki":
                return paki[0, 0], saki[0, 0], 0, HD
            if name == "kb":
                return flat(pbk), flat(sbk)[P - T_S:P], 1, P
            cols = slice(int(name[2]) * P, (int(name[2]) + 1) * P)
            return flat(pak)[:, cols], flat(sak)[:, cols], 0, P

        @block.scalar
        def _(act):
            act.dma_start(gain_rows[:, :], gains[0].rearrange("g (k p) -> (g k) p", p=P)).then_inc(small_in, 16)
            for c in range(2):
                act.dma_start(qk_rows[:, c * HD:(c + 1) * HD], qk_norm[0]).then_inc(small_in, 16)
            act.dma_start(t5_rows[:, :], t5_bias).then_inc(small_in, 16)
            act.dma_start(hot[:, :], onehot).then_inc(small_in, 16)
            act.dma_start(c_rows[:, :, :], c_bias[0, 0:VEC].rearrange("(b p) h -> p b h", p=P)).then_inc(small_in, 16)
            act.dma_start(sink_rows[:, :, :].rearrange("p a b -> p (a b)"), bass.AP(sinks.tensor, 0, [[0, P], [1, H_B]])).then_inc(small_in, 16)
            act.dma_start(cache_rows[:, 0:2, :].rearrange("p t c -> p (t c)"), cak[0, 0].rearrange("t h d -> t (h d)")).then_inc(cache_in, 16)
            for c in range(2):
                act.dma_start(cache_rows[:, 2, c * HD:(c + 1) * HD], caki[0, 0]).then_inc(cache_in, 16)
            act.dma_start(cache_rows[:, 3, :], cbk[0, 0].rearrange("t h d -> t (h d)")).then_inc(cache_in, 16)
            act.dma_start(cache_rows[:, 4:9, :].rearrange("p t c -> p (t c)"), cck[0, 0].rearrange("t h d -> t (h d)")).then_inc(cache_in, 16)
            act.dma_start(v_a[:, 2, :], cav[0, 0].rearrange("t h d -> t (h d)")).then_inc(vcache_in, 16)
            act.dma_start(v_b[:, 2, :], cbv[0, 0].rearrange("t h d -> t (h d)")).then_inc(vcache_in, 16)

            def split(at):
                if at is None:
                    return
                ph, j, s = at
                n = strip_no(ph, j, s)
                if ph.name == "wo":
                    act.wait_ge(ld_wo[s], j * (16 * WO_LOADS) + 16 * WO_LOADS)
                else:
                    act.wait_ge(ld[s], j * 32 + (ph.ld0 * 32 + 32))
                if not (isinstance(n, int) and n < 2):
                    act.wait_ge(used, n - 1)
                for k in (slice(0, 8), slice(8, ph.tiles)):
                    act.activation(w_hi[s][:, k, :], raw[s][:, k, :], ACT.Copy).then_inc(hi_rdy, 1)

            def h_tile(index, j):
                H = j + DT * index
                if not (isinstance(H, int) and H == 0):
                    act.wait_ge(acc_rdy, H)
                act.activation(sqx[:, :], xT[:, j, :], ACT.Square).then_inc(sqx_rdy, 1)
                act.activation(h_hi[:, j, :], xT[:, j, :], ACT.Copy, scale=g_cols[:, bass.ds(j + index * DT, 1)]).then_inc(hhi_rdy, 1)

            def x_norm(index):
                m = [0, 1, MISC_END][index]
                act.wait_ge(m_done, m + 1)
                if index:
                    act.wait_ge(rstd_rdy, index)
                act.activation(sd_x[:, :], bank_m[:, 0:NT], ACT.Sqrt, bias=eps[:, :]).then_inc(m_free, 1)

            def squares(z, n_done):
                act.wait_ge(evac, n_done)
                act.activation(sq[:, :], z, ACT.Square).then_inc(sq_rdy, 1)

            def deviation(m, q):
                act.wait_ge(m_done, m + 1)
                if not (isinstance(q, int) and q == 0):
                    act.wait_ge(rinv_rdy, q)
                act.activation(sd[:, :], bank_m[:, 0:NT], ACT.Sqrt, bias=eps[:, :]).then_inc(m_free, 1)

            def place_v(m, v, cols):
                act.wait_ge(m_done, m + 1)
                act.activation(v[:, 0:2, cols], bank_m[:, 0:2 * P].rearrange("p (t c) -> p t c", t=2), ACT.Copy)
                act.activation(v[0:T_S, 3, cols], bank_m[0:T_S, 2 * P:3 * P], ACT.Copy).then_inc(m_free, 1)

            def place_k(m, kout):
                act.wait_ge(m_done, m + 1)
                if not (isinstance(kout, int) and kout == 0):
                    act.wait_ge(k_out, kout * 32)
                act.activation(k_rows[:, 0:2, :], bank_m[:, 0:2 * P].rearrange("p (t c) -> p t c", t=2), ACT.Copy)
                act.activation(k_rows[0:T_S, 2, :], bank_m[0:T_S, 2 * P:3 * P], ACT.Copy).then_inc(m_free, 1)

            def exps(U, u, sink):
                b, r = u % 2, u % 3
                m, n = ROWS[r], NKEY[r]
                act.wait_ge(mx_rdy, U + u + 1)
                for c in range(2):
                    a = act.activation(s_buf[b][0:m, c, 0:n], s_buf[b][0:m, c, 0:n], ACT.Exp, bias=nmax[b][0:m, c:c + 1],
                                       accum_out=esum[b][0:m, c:c + 1])
                if sink:
                    a = act.activation(esnk[b][0:m, :], snk[b][0:m, :], ACT.Exp)
                a.then_inc(e_rdy, 1)

            def copy_t(U, u):
                b, r = u % 2, u % 3
                act.wait_ge(t_done, U + u + 1)
                if not (isinstance(U, int) and U + u < 2):
                    act.wait_ge(pv_done, U + (u - 1))
                pt = bank_t[b][:, :].rearrange("p (t c) -> p t c", t=4)
                if r < 2:
                    k = 4 - 2 * r
                    a = act.activation(p_t[b][:, 0:k, :], pt[:, 0:k, :], ACT.Copy)
                else:
                    act.activation(p_t[b][:, 0:2, 0:T_S], pt[:, 0:2, 0:T_S], ACT.Copy)
                    a = act.activation(p_t[b][0:T_S, 2:4, 0:T_S], pt[0:T_S, 2:4, 0:T_S], ACT.Copy)
                a.then_inc(c_done, 1)

            def out_hi(U, p, tile):
                act.wait_ge(pv_done, U + (3 * p + 3))
                act.activation(o_hi[:, tile, :], bank_o[:, 0:NT], ACT.Copy).then_inc(ohi_rdy, 1)

            def prep_items(step):
                for it in PREP_ITEMS[step]:
                    if it[0] == "n":
                        if it[1] in ("q0", "q1", "kc"):
                            z, done = {"q0": (z_q[0], 1), "q1": (z_q[1], 2), "kc": (z_k, 3)}[it[1]]
                            squares(z[:, :], phase["cb"].n0 + done)
                        else:
                            z, done = {"ka0": (0, 1), "ka1": (1, 2), "kb": (8, 11)}[it[1]]
                            squares(z_prep[:, z, :], phase["prep"].n0 + done)
                        deviation(misc_no[it], norm_no[it])
                    elif it[0] == "v":
                        v, cols, _, _, _ = v_place(it[1])
                        place_v(misc_no[it], v, cols)
                    elif it[0] == "k":
                        place_k(misc_no[it], kout_no[it])
                    elif it[0] == "w":
                        act.wait_ge(m_done, misc_no[it] + 1)
                        act.activation(w_tok[:, 0:2, :], bank_m[:, 0:2 * H_IDX].rearrange("p (t c) -> p t c", t=2), ACT.Copy)
                        act.activation(w_tok[0:T_S, 2, :], bank_m[0:T_S, 2 * H_IDX:3 * H_IDX], ACT.Copy).then_inc(m_free, 1)
                    elif it[0] == "i":
                        u = it[1]
                        r, _ = idx_units[u]
                        act.wait_ge(iq_done, u + 1)
                        if u >= 2:
                            act.wait_ge(iacc, 2 * u - 2)
                        m, n = ROWS[r], NKEY[r]
                        act.activation(s_buf[u % 2][0:m, :, 0:n], bank_s[u % 2][0:m, 0:2 * n].rearrange("p (c k) -> p c k", c=2),
                                       ACT.Relu).then_inc(irelu, 1)

            phase = {p.name: p for p in phases if p.name not in ("up", "down")}

            split((phases[0], 0, 0))
            for j in range(DT):
                act.wait_ge(start_cp, 2 + j)
                h_tile(0, j)

            for ph in phases:
                if ph.name == "up":
                    F0 = sum(p.more["size"] for p in phases[:phases.index(ph)] if p.name == "up")

                    def body(j, ph=ph, F0=F0):
                        F = j + F0
                        n = strip_no(ph, j, 0)
                        split(following(ph, j, 0))
                        if ph.more["first"] and isinstance(j, int) and j == 0:
                            x_norm(2 * ph.more["ffn"])
                        act.wait_ge(evac, n + 1)
                        if not (isinstance(F, int) and F == 0):
                            act.wait_ge(gu_rdy, F)
                        act.activation(g_sig[:, :], g_act[:, :], ACT.Silu).then_inc(sig_rdy, 1)
                        split(following(ph, j, 1))
                        act.wait_ge(gu_rdy, F + 1)
                        act.activation(gu_hi[:, j, :], gu[:, :], ACT.Copy).then_inc(guh_rdy, 1)
                    bodies(act, ph, body, peel_first=ph.more["first"])
                elif ph.name == "down" or ph.name == "wo":
                    index = 1 if ph.name == "down" else 2
                    h_after = ph.name == "wo" or (ph.more["last"] and ph.more["ffn"] == 0)

                    def body(j, ph=ph, index=index, h_after=h_after):
                        for s in range(2):
                            if ph.name == "wo" and isinstance(j, int) and j == 0:
                                if s == 0:
                                    split(following(ph, 0, 0))
                                    attend_tail()
                                else:
                                    split(following(ph, 0, 1))
                            else:
                                split(following(ph, j, s))
                            if h_after:
                                act.wait_ge(evac, strip_no(ph, j, s) + 1)
                                h_tile(index, j * 2 + s)

                    def attend_tail():
                        U = 42
                        exps(U, 0, False), exps(U, 1, False)
                        copy_t(U, 0), copy_t(U, 1), exps(U, 2, False), exps(U, 3, False)
                        copy_t(U, 2), copy_t(U, 3), exps(U, 4, False), exps(U, 5, False)
                        out_hi(U, 0, 2)
                        copy_t(U, 4), copy_t(U, 5)
                        out_hi(U, 1, 5)
                    bodies(act, ph, body, peel_first=ph.name == "wo")
                elif ph.name == "prep":
                    def body(j, ph=ph):
                        split(following(ph, j, 0))
                        if isinstance(j, int) and j == 0:
                            x_norm(1)
                        split(following(ph, j, 1))
                    body(0)
                    with act.Fori(1, 4) as j:
                        body(j)
                    for t in range(4):
                        split(following(ph, 4 + t // 2, t % 2))
                        prep_items(8 + t)
                elif ph.name == "cb":
                    for t in range(4):
                        split(following(ph, t // 2, t % 2))
                        prep_items(12 + t)

                    def body(i, ph=ph):
                        n, U = i * 4 + ph.n0, i * 6 - 6
                        m, q = i * 5 + (MISC_CB0 - 5), i * 3 + (NORM_CB0 - 3)
                        split((ph, i * 2, 1))
                        act.wait_ge(v_out, i * 32 + (VOUT_PREP - 1) * 32)
                        if not (isinstance(i, int) and i == 1):
                            act.wait_ge(pv_done, U)
                        place_v(m, v_c, slice(0, P))
                        place_k(m + 1, i + (KOUT_PREP - 1))
                        exps(U, 0, False), exps(U, 1, False)
                        split((ph, i * 2 + 1, 0))
                        squares(z_q[0][:, :], n + 1)
                        copy_t(U, 0), copy_t(U, 1), exps(U, 2, False), exps(U, 3, True)
                        split((ph, i * 2 + 1, 1))
                        copy_t(U, 2), copy_t(U, 3), exps(U, 4, True), exps(U, 5, True)
                        split((ph, i * 2 + 2, 0) if not isinstance(i, int) or i < 4 else (ph.next, 0, 0))
                        deviation(m + 2, q)
                        squares(z_q[1][:, :], n + 2)
                        out_hi(U, 0, i + (PAIR_TILE["c"] - 1))
                        copy_t(U, 4), copy_t(U, 5)
                        deviation(m + 3, q + 1)
                        squares(z_k[:, :], n + 3)
                        deviation(m + 4, q + 2)
                        out_hi(U, 1, i + (PAIR_TILE["b"] - 1))
                    body(1)
                    with act.Fori(2, 4) as i:
                        body(i)
                    body(4)
                elif ph.name == "a":
                    def body(i, ph=ph):
                        cb = isinstance(i, int) and i == 0
                        n, U = i * 2 + ph.n0, i * 6 + 24
                        if cb:
                            m, q = MISC_A0 + 2, NORM_A0
                        else:
                            m, q = i * 2 + (MISC_A1 - 2), i * 2 + NORM_A0
                        split((ph, i, 1))
                        if cb:
                            act.wait_ge(v_out, (VOUT_PREP + 4) * 32)
                            act.wait_ge(pv_done, U)
                            place_v(MISC_A0, v_c, slice(0, P))
                            place_k(MISC_A0 + 1, KOUT_PREP + 4)
                        exps(U, 0, False), exps(U, 1, False)
                        copy_t(U, 0), copy_t(U, 1), exps(U, 2, False), exps(U, 3, cb)
                        squares(z_q[0][:, :], n + 1)
                        split(following(ph, i, 1))
                        copy_t(U, 2), copy_t(U, 3), exps(U, 4, cb), exps(U, 5, cb)
                        deviation(m, q)
                        squares(z_q[1][:, :], n + 2)
                        out_hi(U, 0, PAIR_TILE["c"] + 4 if cb else i - 1)
                        copy_t(U, 4), copy_t(U, 5)
                        deviation(m + 1, q + 1)
                        out_hi(U, 1, PAIR_TILE["b"] + 4 if cb else i + 2)
                    body(0), body(1), body(2)
            yp_t, ys_t = yp[0].rearrange("(t p) c -> p t c", p=P), ys[0]
            for k in range(DT):
                act.wait_ge(y_cp, k + 1)
                act.dma_start(yp_t[:, :, k * P:(k + 1) * P], y_rows[:, k % 2, 0:2, :]).then_inc(y_out[k % 2], 16)
                act.dma_start(ys_t[:, k * P:(k + 1) * P], y_rows[0:T_S, k % 2, 2, :]).then_inc(y_out[k % 2], 16)
            for stored in y_out:
                act.wait_ge(stored, DT // 2 * 32)

        @block.vector
        def _(dve):
            steps = [0]

            def link(ins):
                steps[0] += 1
                ins.then_inc(dve_link, 1)
                dve.wait_ge(dve_link, steps[0])

            def split(at):
                if at is None:
                    return
                ph, j, s = at
                n = strip_no(ph, j, s)
                for half, k in enumerate((slice(0, 8), slice(8, ph.tiles))):
                    dve.wait_ge(hi_rdy, n * 2 + (half + 1))
                    dve.tensor_tensor(w_lo[s][:, k, :], raw[s][:, k, :], w_hi[s][:, k, :].bitcast(F32), ALU.subtract)\
                       .then_inc(lo_rdy, 1)

            def h_tile(index, j):
                H = j + DT * index
                dve.wait_ge(sqx_rdy, H + 1)
                if not (isinstance(H, int) and H == 0):
                    dve.wait_ge(acc_rdy, H)
                dve.tensor_tensor(sumsq[:, :], sumsq[:, :], sqx[:, :], ALU.add).then_inc(acc_rdy, 1)
                dve.wait_ge(hhi_rdy, H + 1)
                dve.scalar_tensor_tensor(h_lo[:, j, :], xT[:, j, :], g_cols[:, bass.ds(j + index * DT, 1)],
                                         h_hi[:, j, :].bitcast(F32), ALU.mult, ALU.subtract).then_inc(hlo_rdy, 1)

            def x_norm(index, n):
                m = [0, 1, MISC_END][index]
                dve.wait_ge(m_free, m + 1)
                if n:
                    dve.wait_ge(evac, n)
                dve.reciprocal(rstd[:, :], sd_x[:, :]).then_inc(rstd_rdy, 1)
                dve.wait_ge(rstd_rdy, index + 1)

            def read(n, s, dst, rows=slice(0, P), cols=slice(0, NT)):
                dve.wait_ge(used, n + 1)
                return dve.tensor_tensor(dst, bank_w[s][rows, cols], rstd[rows, cols], ALU.mult)

            def finish(name, m, q, gain):
                z, _, places = norm_source(name)
                dve.wait_ge(m_free, m + 1)
                if not (isinstance(q, int) and q == 0):
                    dve.wait_ge(qk_rdy, q)
                dve.reciprocal(rinv[:, :], sd[:, :]).then_inc(rinv_rdy, 1)
                dve.wait_ge(rinv_rdy, q + 1)
                for dst, cols, rows in places:
                    ins = dve.scalar_tensor_tensor(dst, z[rows, cols], qk_cols[rows, gain:gain + 1], rinv[rows, cols], ALU.mult, ALU.mult)
                ins.then_inc(qk_rdy, 1)

            def smax(kind, body, u):
                U = body * 6
                b, r, p = u % 2, u % 3, u // 3
                m, n = ROWS[r], NKEY[r]
                dve.wait_ge(qk_done, U + (u + 1))
                if not (isinstance(U, int) and U + u < 2):
                    dve.wait_ge(t_done, U + (u - 1))
                if r == 0:
                    if kind == "cb":
                        dve.wait_ge(bias_rdy, body * 2 + (p + 1))
                    else:
                        dve.wait_ge(bias_ld[p], body * 16 + 16)
                rev = [slice(None, None, -1), slice(P - 1, None, -1), slice(T_P - 1, T_P - 1 - n, -1)][r]
                s = s_buf[b][0:m, :, 0:n]
                dve.scalar_tensor_tensor(s, bank_s[b][0:m, 0:2 * n].rearrange("p (c k) -> p c k", c=2), ATTN_SCALE,
                                         bias_rev[p][0:m, :, rev], ALU.mult, ALU.add).then_inc(s_add, 1)
                dve.wait_ge(s_add, U + (u + 1))
                if kind == "a":
                    mask = a_mask[r][0:m, :]
                    for c in range(2):
                        ins = dve.tensor_tensor(s_buf[b][0:m, c, 0:n], s_buf[b][0:m, c, 0:n], mask, ALU.add)
                    ins.then_inc(masked, 1)
                    dve.wait_ge(masked, body * 6 + (u - 29))
                sink = kind == "cb" and p == 1
                red = dve.tensor_reduce(nmax[b][0:m, :], s, AX_X, ALU.max, negate=True)
                if not sink:
                    red.then_inc(mx_rdy, 1)
                else:
                    c0 = body * 6 + 2 * r
                    ns = neg_sinks[0:m, :, body]
                    red.then_inc(mx_raw, 1)
                    dve.wait_ge(mx_raw, c0 + 1)
                    dve.tensor_tensor(nmax[b][0:m, :], nmax[b][0:m, :], ns, ALU.min).then_inc(mx_raw, 1)
                    dve.wait_ge(mx_raw, c0 + 2)
                    dve.tensor_tensor(snk[b][0:m, :], nmax[b][0:m, :], ns, ALU.subtract).then_inc(mx_rdy, 1)

            def inverse(kind, body, u):
                b, r, p = u % 2, u % 3, u // 3
                m = ROWS[r]
                dve.wait_ge(e_rdy, body * 6 + (u + 1))
                if kind == "cb" and p == 1:
                    dve.tensor_tensor(esum[b][0:m, :], esum[b][0:m, :], esnk[b][0:m, :], ALU.add).then_inc(sum_sunk, 1)
                    dve.wait_ge(sum_sunk, body * 3 + (r + 1))
                dve.reciprocal(einv[b][0:m, :], esum[b][0:m, :]).then_inc(r_rdy, 1)

            def out_lo(body, p, tile):
                dve.wait_ge(ohi_rdy, body * 2 + (p + 1))
                dve.tensor_tensor(o_lo[:, tile, :], bank_o[:, 0:NT], o_hi[:, tile, :].bitcast(F32), ALU.subtract).then_inc(olo_rdy, 1)

            def prep_items(step):
                for it in PREP_ITEMS[step]:
                    if it[0] == "n":
                        gain = {"ka0": 1, "ka1": 1, "kb": 3, "q0": 4, "q1": 2, "kc": 5}[it[1]]
                        finish(it[1], misc_no[it], norm_no[it], gain)
                    elif it[0] == "i":
                        u = it[1]
                        r, t = idx_units[u]
                        m, n = ROWS[r], NKEY[r]
                        dve.wait_ge(irelu, u + 1)
                        if u == 0:
                            dve.wait_ge(m_free, misc_no[("w",)] + 1)
                        for c in range(2):
                            w = w_tok[0:m, [1, 0, 2][r], 2 * t + c:2 * t + c + 1]
                            acc = idx_acc[r][0:m, :]
                            if t == 0 and c == 0:
                                ins = dve.tensor_scalar(acc, s_buf[u % 2][0:m, c, 0:n], w, None, ALU.mult)
                            else:
                                dve.wait_ge(iacc, 2 * u + c)
                                ins = dve.scalar_tensor_tensor(acc, s_buf[u % 2][0:m, c, 0:n], w, acc, ALU.mult, ALU.add)
                            ins.then_inc(iacc, 1)
                    elif it[0] == "t":
                        r = it[1]
                        m, n = ROWS[r], NKEY[r]
                        acc = idx_acc[r][0:m, :]
                        dve.wait_ge(iacc, 8 * (r + 1))
                        link(dve.tensor_scalar(acc, acc, IDX_SCALE, None, ALU.mult))
                        if r < 2:
                            link(dve.memset(idx_acc[r][0:CHUNK, n - CHUNK:n], NEG))
                        for _ in range((K_P if r < 2 else K_S) // 8):
                            link(dve.max(top8[0:m, :], acc))
                            link(dve.match_replace(acc, top8[0:m, :], acc, TAKEN))
                        dve.tensor_scalar(a_mask[r][0:m, :], acc, TAKEN / 2, NEG, ALU.is_gt, ALU.mult).then_inc(mask_rdy, 1)

            for tile, value in ((sumsq[:, :], 0.0), (mean_d[:, :], 1.0 / D), (eps[:, :], EPS), (mean_hd[:, :], 0.0),
                                (mean_hd[0:HD, 0:HD], 1.0 / HD)):
                link(dve.memset(tile, value))
            dve.wait_ge(consts, 2)
            dve.memset(mean_hd[HD:P, HD:P], 1.0 / HD).then_inc(consts, 1)
            split((phases[0], 0, 0))
            n = 0

            def start_copy(dst, src_cols, rows=P):
                nonlocal n
                dve.wait_ge(start_tr, n + 1)
                dve.tensor_copy(dst, bank_t[n % 2][0:rows, src_cols]).then_inc(start_cp, 1)
                n += 1
            dve.wait_ge(start_tr, 1)
            dve.tensor_copy(g_cols[:, :], bank_t[0][:, 0:3 * DT])
            dve.tensor_copy(qk_cols[:, :], bank_t[0][:, 3 * DT:3 * DT + 6]).then_inc(start_cp, 1)
            n = 1
            for j in range(DT):
                start_copy(xT[:, j, :], slice(0, NT))
                dve.wait_ge(start_cp, n)
                h_tile(0, j)
            start_copy(vec_t5[:, :], slice(0, VEC), H_A + H_B)
            start_copy(vec_c[:, :], slice(0, VEC), H_C)
            for c in range(2):
                link(dve.memset(kt_i[c][(1 - c) * HD:(2 - c) * HD, :], 0.0))
            for _, dst in CACHE_TILES:
                if dst is None:
                    dve.wait_ge(start_tr, n + 1)
                    dve.tensor_copy(kt_i[0][0:HD, T_P:T_P + PAST], bank_t[n % 2][0:HD, 0:P])
                    dve.tensor_copy(kt_i[1][HD:P, T_P:T_P + PAST], bank_t[n % 2][HD:P, 0:P]).then_inc(start_cp, 1)
                    n += 1
                else:
                    start_copy(dst, slice(0, P))
            dve.wait_ge(small_in, 16 * 7)
            link(dve.tensor_scalar(neg_sinks[:, :, :].rearrange("p a b -> p (a b)"), sink_rows[:, :, :].rearrange("p a b -> p (a b)"),
                                   -1.0, None, ALU.mult))

            for ph in phases:
                if ph.name == "up":
                    F0 = sum(p.more["size"] for p in phases[:phases.index(ph)] if p.name == "up")

                    def body(j, ph=ph, F0=F0):
                        F = j + F0
                        n = strip_no(ph, j, 0)
                        later = not (isinstance(F, int) and F == 0)
                        split(following(ph, j, 0))
                        if ph.more["first"] and isinstance(j, int) and j == 0:
                            x_norm(2 * ph.more["ffn"], ph.n0)
                        if later:
                            dve.wait_ge(sig_rdy, F)
                        read(n, 0, g_act[:, :]).then_inc(evac, 1)
                        split(following(ph, j, 1))
                        if later:
                            dve.wait_ge(gu_rdy, F)
                        read(n + 1, 1, u_act[:, :]).then_inc(evac, 1)
                        dve.wait_ge(evac, n + 2)
                        dve.wait_ge(sig_rdy, F + 1)
                        if later:
                            dve.wait_ge(gul_rdy, F)
                            dve.wait_ge(guh_rdy, F)
                        dve.tensor_tensor(gu[:, :], g_sig[:, :], u_act[:, :], ALU.mult).then_inc(gu_rdy, 1)
                        dve.wait_ge(gu_rdy, F + 1)
                        dve.wait_ge(guh_rdy, F + 1)
                        dve.tensor_tensor(gu_lo[:, j, :], gu[:, :], gu_hi[:, j, :].bitcast(F32), ALU.subtract).then_inc(gul_rdy, 1)
                    bodies(dve, ph, body, peel_first=ph.more["first"])
                elif ph.name in ("down", "wo"):
                    index = 1 if ph.name == "down" else 2
                    factor = 0.5 if ph.name == "down" else 1.0
                    h_after = ph.name == "wo" or (ph.more["last"] and ph.more["ffn"] == 0)
                    done = 1 if ph.name == "down" and ph.more["ffn"] == 0 else 2 if ph.name == "wo" else 3
                    dve.wait_ge(hlo_rdy, DT * done)
                    if h_after:
                        dve.wait_ge(m_done, [0, 1, 2][index])
                        link(dve.memset(sumsq[:, :], 0.0))

                    def body(j, ph=ph, index=index, factor=factor, h_after=h_after):
                        for s in range(2):
                            n = strip_no(ph, j, s)
                            split(following(ph, j, s))
                            if ph.name == "wo" and isinstance(j, int) and j == 0 and s == 0:
                                attend_tail()
                            dve.wait_ge(used, n + 1)
                            dve.wait_ge(evac, n)
                            d = j * 2 + s
                            dve.scalar_tensor_tensor(xT[:, d, :], bank_w[s][:, 0:NT], factor, xT[:, d, :], ALU.mult, ALU.add)\
                               .then_inc(evac, 1)
                            if h_after:
                                dve.wait_ge(evac, n + 1)
                                h_tile(index, d)

                    def attend_tail():
                        smax("a", 7, 0), smax("a", 7, 1)
                        inverse("a", 7, 0), inverse("a", 7, 1)
                        smax("a", 7, 2), smax("a", 7, 3)
                        inverse("a", 7, 2), inverse("a", 7, 3)
                        smax("a", 7, 4), smax("a", 7, 5)
                        inverse("a", 7, 4), inverse("a", 7, 5)
                        out_lo(7, 0, 2)
                        out_lo(7, 1, 5)
                    bodies(dve, ph, body, peel_first=ph.name == "wo")
                elif ph.name == "prep":
                    def body(j, ph=ph):
                        n = strip_no(ph, j, 0)
                        split(following(ph, j, 0))
                        if isinstance(j, int) and j == 0:
                            x_norm(1, ph.n0)
                            for s in range(2):
                                for c in range(2):
                                    link(dve.memset(q_n[s][c][(1 - c) * HD:(2 - c) * HD, :], 0.0))
                        read(n, 0, z_prep[:, j * 2, :]).then_inc(evac, 1)
                        split(following(ph, j, 1))
                        read(n + 1, 1, z_prep[:, j * 2 + 1, :]).then_inc(evac, 1)
                    body(0)
                    with dve.Fori(1, 4) as j:
                        body(j)
                    n = ph.n0 + 8
                    split(following(ph, 4, 0))
                    for c in range(2):
                        part = slice(c * HD, (c + 1) * HD)
                        read(n, 0, kt_i[c][part, 0:T_P], rows=part, cols=slice(0, T_P))
                        ins = read(n, 0, kt_i[c][part, T_P + PAST:KEYS], rows=part, cols=slice(T_P, NT))
                    ins.then_inc(evac, 1)
                    dve.wait_ge(evac, n + 1)
                    prep_items(8)
                    split(following(ph, 4, 1))
                    read(n + 1, 1, zw[:, :], rows=slice(0, H_IDX)).then_inc(evac, 1)
                    prep_items(9)
                    split(following(ph, 5, 0))
                    read(n + 2, 0, z_prep[:, 8, :]).then_inc(evac, 1)
                    prep_items(10)
                    split(following(ph, 5, 1))
                    read(n + 3, 1, z_prep[:, 9, :]).then_inc(evac, 1)
                    prep_items(11)
                elif ph.name == "cb":
                    zs = [z_q[0], z_q[1], z_k, z_v]
                    for t in range(4):
                        split(following(ph, t // 2, t % 2))
                        read(ph.n0 + t, t % 2, zs[t][:, :]).then_inc(evac, 1)
                        dve.wait_ge(evac, ph.n0 + t + 1)
                        prep_items(12 + t)

                    def body(i, ph=ph):
                        n, a = i * 4 + ph.n0, i - 1
                        m, q = i * 5 + (MISC_CB0 - 5), i * 3 + (NORM_CB0 - 3)
                        split((ph, i * 2, 1))
                        dve.wait_ge(qk_rdy, q)
                        read(n, 0, z_q[0][:, :]).then_inc(evac, 1)
                        smax("cb", a, 0), smax("cb", a, 1)
                        split((ph, i * 2 + 1, 0))
                        inverse("cb", a, 0), inverse("cb", a, 1)
                        read(n + 1, 1, z_q[1][:, :]).then_inc(evac, 1)
                        smax("cb", a, 2), smax("cb", a, 3)
                        split((ph, i * 2 + 1, 1))
                        inverse("cb", a, 2), inverse("cb", a, 3)
                        read(n + 2, 0, z_k[:, :]).then_inc(evac, 1)
                        smax("cb", a, 4), smax("cb", a, 5)
                        split((ph, i * 2 + 2, 0) if not isinstance(i, int) or i < 4 else (ph.next, 0, 0))
                        inverse("cb", a, 4), inverse("cb", a, 5)
                        dve.wait_ge(evac, n + 3)
                        finish("q0", m + 2, q, 4)
                        read(n + 3, 1, z_v[:, :]).then_inc(evac, 1)
                        out_lo(a, 0, i + (PAIR_TILE["c"] - 1))
                        finish("q1", m + 3, q + 1, 2)
                        finish("kc", m + 4, q + 2, 5)
                        out_lo(a, 1, i + (PAIR_TILE["b"] - 1))
                    body(1)
                    with dve.Fori(2, 4) as i:
                        body(i)
                    body(4)
                elif ph.name == "a":
                    dve.wait_ge(mask_rdy, 3)

                    def body(i, ph=ph):
                        cb = isinstance(i, int) and i == 0
                        kind = "cb" if cb else "a"
                        n, a = i * 2 + ph.n0, i + 4
                        if cb:
                            m, q = MISC_A0 + 2, NORM_A0
                        else:
                            m, q = i * 2 + (MISC_A1 - 2), i * 2 + NORM_A0
                        split((ph, i, 1))
                        smax(kind, a, 0), smax(kind, a, 1)
                        inverse(kind, a, 0), inverse(kind, a, 1)
                        smax(kind, a, 2), smax(kind, a, 3)
                        dve.wait_ge(qk_rdy, q)
                        read(n, 0, z_q[0][:, :]).then_inc(evac, 1)
                        split(following(ph, i, 1))
                        inverse(kind, a, 2), inverse(kind, a, 3)
                        smax(kind, a, 4), smax(kind, a, 5)
                        inverse(kind, a, 4), inverse(kind, a, 5)
                        dve.wait_ge(evac, n + 1)
                        finish("q0", m, q, 0)
                        read(n + 1, 1, z_q[1][:, :]).then_inc(evac, 1)
                        out_lo(a, 0, PAIR_TILE["c"] + 4 if cb else i - 1)
                        dve.wait_ge(evac, n + 2)
                        finish("q1", m + 1, q + 1, 0)
                        out_lo(a, 1, PAIR_TILE["b"] + 4 if cb else i + 2)
                    body(0), body(1), body(2)
            for k in range(DT):
                dve.wait_ge(y_tr, k + 1)
                if k >= 2:
                    dve.wait_ge(y_out[k % 2], 32 * (k // 2))
                dve.tensor_copy(y_rows[:, k % 2, 0:2, :], bank_t[k % 2][:, 0:2 * P].rearrange("p (t c) -> p t c", t=2))
                dve.tensor_copy(y_rows[0:T_S, k % 2, 2, :], bank_t[k % 2][0:T_S, 2 * P:3 * P]).then_inc(y_cp, 1)

        @block.gpsimd
        def _(pool):
            pool.memset(ident[:, :], 0.0).then_inc(pool_built, 1)
            pool.wait_ge(pool_built, 1)
            pool.memset(flip[:, :], 0.0).then_inc(pool_built, 1)
            pool.wait_ge(pool_built, 2)
            pool.affine_select(out=ident[:, :], in_=ident[:, :], compare_op=ALU.not_equal, fill=1.0, base=0,
                               pattern=[[-1, P]], channel_multiplier=1).then_inc(consts, 1)
            pool.wait_ge(consts, 1)
            pool.affine_select(out=flip[:, :], in_=flip[:, :], compare_op=ALU.not_equal, fill=1.0, base=1 - P,
                               pattern=[[1, P]], channel_multiplier=1).then_inc(consts, 1)
            pool.wait_ge(consts, 2)

            def settled():
                pool.sem_inc(pool_passed, 1)

            for src, dst in ((cbk, sbk), (cbv, sbv), (cck, sck), (ccv, scv)):
                pool.dma_start(dst[0, 0, 0:P - T_S], src[0, 0, T_S:P]).then_inc(misc_out, 16)
            pool.wait_ge(start_cp, 1 + DT + 2)
            pool.dma_start(vec_dram[0:H_A + H_B, :], vec_t5[:, :]).then_inc(vec_out, 16)
            pool.dma_start(vec_dram[H_A + H_B:H_A + H_B + H_C, :], vec_c[:, :]).then_inc(vec_out, 16)
            pool.wait_ge(vec_out, 32)

            def windows(first, step, count, apart):
                return bass.AP(vec_dram.tensor, first * VEC, [[step * VEC, count], [1, P], [apart * VEC, 2], [1, T_P]])
            win = {"c": windows(H_A + H_B, 2, 5, 1), "b": windows(H_A, 1, 5, 5),
                   "a0": windows(0, 1, 3, 3), "a1": windows(6, 1, 3, 3)}

            def load_bias(kind, at, p, body):
                if not (isinstance(body, int) and body == 0):
                    pool.wait_ge(s_add, body * 6 + (3 * p - 3))
                    settled()
                pool.dma_start(bias_rev[p][:, :, :], win[kind][at]).then_inc(bias_ld[p], 16)
                if kind in "bc":
                    pool.wait_ge(bias_ld[p], body * 16 + 16)
                    settled()
                    if not (isinstance(body, int) and body == 0):
                        pool.wait_ge(p_rdy, body * 6 + (2 * p - 2))
                        settled()
                    if kind == "b":
                        pool.memset(bias_rev[p][CHUNK:P, :, T_P - CHUNK:T_P], NEG).then_inc(window_msk, 1)
                        pool.wait_ge(window_msk, body + 1)
                        settled()
                    pool.memset(bias_rev[p][0:CHUNK, :, 0:CHUNK], NEG).then_inc(bias_rdy, 1)
                    pool.wait_ge(bias_rdy, body * 2 + (p + 1))
                    settled()

            def place_c_cache(i):
                pool.tensor_copy(kt_c[:, T_P:T_P + PAST], kc_cache[:, i, :]).then_inc(kc_rdy, 1)
                pool.wait_ge(kc_rdy, i + 1)
                settled()
                pool.dma_start(v_c[:, 2, :], ccv_t[:, bass.ds(i * P, P)]).then_inc(vc_ld, 16)

            ccv_t = ccv[0, 0].rearrange("t h d -> t (h d)")

            def normalize(U, u):
                b, r = u % 2, u % 3
                m, n = ROWS[r], NKEY[r]
                if not (isinstance(U, int) and U + u == 0):
                    pool.wait_ge(p_rdy, U + u)
                pool.wait_ge(r_rdy, U + (u + 1))
                settled()
                for c in range(2):
                    ins = pool.tensor_scalar(s_buf[b][0:m, c, 0:n], s_buf[b][0:m, c, 0:n], einv[b][0:m, c:c + 1], None, ALU.mult)
                ins.then_inc(p_rdy, 1)

            def store_v(m, v, cols, prompt, sample, first):
                pool.wait_ge(m_free, m + 1)
                settled()
                pool.dma_start(prompt.rearrange("(t p) c -> p t c", p=P), v[:, first:2, cols]).then_inc(v_out, 16)
                pool.dma_start(sample, v[0:T_S, 3, cols]).then_inc(v_out, 16)

            def store_k(m, prompt, sample, first, width):
                pool.wait_ge(m_free, m + 1)
                settled()
                pool.dma_start(prompt.rearrange("(t p) c -> p t c", p=P), k_rows[:, first:2, 0:width]).then_inc(k_out, 16)
                pool.dma_start(sample, k_rows[0:T_S, 2, 0:width]).then_inc(k_out, 16)

            flat = lambda x: x[0, 0].rearrange("t h d -> t (h d)")

            def store_c(m, i):
                cols = bass.ds(i * P, P)
                store_v(m, v_c, slice(0, P), flat(pcv)[:, cols], flat(scv)[P - T_S:P, cols], 0)
                store_k(m + 1, flat(pck)[:, cols], flat(sck)[P - T_S:P, cols], 0, P)

            prep = next(p for p in phases if p.name == "prep")
            pool.wait_ge(evac, prep.n0 + 1)
            load_bias("c", 0, 0, 0)
            load_bias("b", 0, 1, 0)
            place_c_cache(0)
            for step in range(8, 16):
                for it in PREP_ITEMS[step]:
                    if it[0] == "v":
                        store_v(misc_no[it], *v_place(it[1]))
                    if it[0] == "k":
                        store_k(misc_no[it], *k_place(it[1]))

            def attend(body, nxt, at, turn):
                U = body * 6
                if turn is not None:
                    store_c(turn, body)
                normalize(U, 0), normalize(U, 1), normalize(U, 2), normalize(U, 3)
                if nxt:
                    load_bias(nxt[0], at, 0, body + 1)
                normalize(U, 4), normalize(U, 5)
                if nxt:
                    load_bias(nxt[1], at, 1, body + 1)
                if nxt and nxt[0] == "c":
                    pool.wait_ge(pv_done, U + 3)
                    settled()
                    place_c_cache(at)

            attend(0, ("c", "b"), 1, MISC_CB0)
            with pool.Fori(1, 4) as i:
                attend(i, ("c", "b"), i + 1, i * 5 + MISC_CB0)
            attend(4, ("a0", "a1"), 0, MISC_A0)
            with pool.Fori(5, 7) as i:
                attend(i, ("a0", "a1"), i - 4, None)
            attend(7, None, None, None)
            pool.wait_ge(misc_out, 64)
            pool.wait_ge(v_out, 32 * (VOUT_PREP + 5))
            pool.wait_ge(k_out, 32 * (KOUT_PREP + 5))


_INS = ["x_prompt", "x_sample", "cache_a_k", "cache_a_v", "cache_a_kidx", "cache_b_k", "cache_b_v", "cache_c_k", "cache_c_v",
        "w_in", "w_out", "qk_norm", "sinks", "c_rel_bias", "t5_rel_bias", "norm_gains", "w_ffn_gate", "w_ffn_up", "w_ffn_down"]


def kernel(**inputs):
    import concourse.bacc as bacc
    from concourse.bass_utils import run_bass_kernel_spmd

    nc = bacc.Bacc("TRN2", target_bir_lowering=False, num_devices=1)
    arrays, args = {}, []

    def add_input(name, a):
        a = np.ascontiguousarray(a)
        arrays[f"in_{name}"] = a
        args.append(nc.dram_tensor(f"in_{name}", a.shape, mybir.dt.from_np(a.dtype), kind="ExternalInput").ap())

    for name in _INS:
        add_input(name, inputs[name])
    add_input("t5_onehot", t5_onehot())
    shape = {name: tuple(inputs[name].shape) for name in _INS}
    depth, batch, past = shape["cache_a_k"][:3]
    seq, dec = shape["x_prompt"][1], shape["x_sample"][1]
    window = shape["cache_b_k"][2]
    outs = [shape["x_prompt"], shape["x_sample"], (depth, batch, seq, KV_A, HD), (depth, batch, seq, KV_A, HD),
            (depth, batch, seq, HD), (depth, batch, window, KV_B, HD), (depth, batch, window, KV_B, HD),
            (depth, batch, seq, H_C, HD), (depth, batch, seq, H_C, HD),
            (depth, batch, dec, KV_A, HD), (depth, batch, dec, KV_A, HD), (depth, batch, dec, HD),
            shape["cache_b_k"], shape["cache_b_v"], shape["cache_c_k"], shape["cache_c_v"]]
    for i, s in enumerate(outs):
        args.append(nc.dram_tensor(f"out_{i}", s, F32, kind="ExternalOutput").ap())
    encoder_step(nc, *args)
    r = run_bass_kernel_spmd(nc, [arrays], core_ids=[0])
    return tuple(r.results[0][f"out_{i}"] for i in range(len(outs)))
```

```python
from contextlib import ExitStack

import numpy as np

import concourse.bass as bass
from concourse import mybir

ALU = mybir.AluOpType
ACT = mybir.ActivationFunctionType
AX_X = mybir.AxisListType.X
F32 = mybir.dt.float32
F32R = mybir.dt.float32r

P = 128
HD = 64
CHUNK = 64
H_A, KV_A, H_IDX, H_B, KV_B, H_C = 12, 4, 8, 10, 2, 10
T5_BUCKETS, T5_MAX_DIST, C_MAX_REL = 32, 1024, 256
EPS = 1e-6
NEG = -1e30
TAKEN = -3e38
ATTN_SCALE = HD ** -0.5
IDX_SCALE = (H_IDX * HD) ** -0.5
VEC = 3 * P


def t5_onehot():
    nb = T5_BUCKETS // 2
    exact = nb // 2
    rel = 127 - np.arange(VEC)
    n = np.abs(rel)
    nf = np.maximum(n, exact).astype(np.float32)
    large = exact + (np.log(nf / np.float32(exact)) / np.float32(np.log(T5_MAX_DIST / exact))
                     * np.float32(nb - exact)).astype(np.int32)
    bucket = np.where(rel > 0, nb, 0) + np.where(n < exact, n, np.minimum(large, nb - 1))
    return (np.arange(T5_BUCKETS)[:, None] == bucket[None, :]).astype(np.float32)


class Phase:

    def __init__(self, name, strips, tiles, n0, ld0, **more):
        self.name, self.strips, self.tiles, self.n0, self.ld0 = name, strips, tiles, n0, ld0
        self.more = more


def plan_phases(d_tiles, f_tiles):
    phases, n, ld = [], 0, 0
    thirds = [f_tiles - 2 * (f_tiles // 3), f_tiles // 3, f_tiles // 3]

    def add(name, strips, tiles, **more):
        nonlocal n, ld
        phases.append(Phase(name, strips, tiles, n, 0 if name == "wo" else ld, **more))
        n += strips
        ld += 0 if name == "wo" else strips // 2

    for ffn in range(2):
        f0 = 0
        for t, size in enumerate(thirds):
            add("up", 2 * size, d_tiles, ffn=ffn, f0=f0, size=size, first=t == 0)
            add("down", d_tiles, size, ffn=ffn, f0=f0, size=size, last=t == 2)
            f0 += size
        if ffn == 0:
            add("prep", 12, d_tiles)
            add("cb", 20, d_tiles)
            add("a", 6, d_tiles)
            add("wo", d_tiles, 16)
    for a, b in zip(phases, phases[1:]):
        a.next = b
    phases[-1].next = None
    return phases


def encoder_step(nc, xp, xs, cak, cav, caki, cbk, cbv, cck, ccv, w_in, w_out, qk_norm, sinks, c_bias, t5_bias,
                 gains, w_gate, w_up, w_down, onehot,
                 yp, ys, pak, pav, paki, pbk, pbv, pck, pcv, sak, sav, saki, sbk, sbv, sck, scv):
    T_P, D = xp.shape[1:]
    T_S = xs.shape[1]
    PAST = cak.shape[2]
    D_IN = w_in.shape[2]
    D_FF = w_gate.shape[3]
    NT = T_P + T_S
    DT, FT = D // P, D_FF // P
    assert T_P == 2 * P and T_S == 32 and PAST == P and w_out.shape[1] == 16 * P
    assert cbk.shape[2] == P and cck.shape[2] == P
    K_P, K_S = T_P // 4, (PAST + T_S) // 4
    phases = plan_phases(DT, FT)
    thirds = [p.more["size"] for p in phases if p.name == "up"][:3]

    o_qa = 0
    o_ka = o_qa + H_A * HD
    o_va = o_ka + KV_A * HD
    o_qi = o_va + KV_A * HD
    o_ki = o_qi + H_IDX * HD
    o_wi = o_ki + HD
    o_qb = o_wi + H_IDX
    o_kb = o_qb + H_B * HD
    o_vb = o_kb + KV_B * HD
    o_qc = o_vb + KV_B * HD
    o_kc = o_qc + H_C * HD
    o_vc = o_kc + H_C * HD
    assert o_vc + H_C * HD == D_IN

    ctx = ExitStack()
    with ctx:
        def sb(name, shape, dt=F32, scope=ctx):
            return scope.enter_context(nc.sbuf_tensor(name, shape, dt))

        def sem(name):
            return ctx.enter_context(nc.semaphore(name))

        xT = sb("xT", [P, DT, NT])
        h_hi = sb("h_hi", [P, DT, NT], F32R)
        h_lo = sb("h_lo", [P, DT, NT], F32R)
        raw = [sb(f"raw{s}", [P, 16, P]) for s in range(2)]
        w_hi = [sb(f"w_hi{s}", [P, 16, P], F32R) for s in range(2)]
        w_lo = [sb(f"w_lo{s}", [P, 16, P], F32R) for s in range(2)]
        with ExitStack() as ffn_scope:
            gu_hi = sb("gu_hi", [P, thirds[0], NT], F32R, ffn_scope)
            gu_lo = sb("gu_lo", [P, thirds[0], NT], F32R, ffn_scope)
        o_hi = sb("o_hi", [P, 16, NT], F32R)
        o_lo = sb("o_lo", [P, 16, NT], F32R)
        ident = sb("ident", [P, P])
        mean_d = sb("mean_d", [P, P])
        mean_hd = sb("mean_hd", [P, P])
        mean_hd2 = sb("mean_hd2", [P, 2])
        eps = sb("eps", [P, 1])
        g_cols = sb("g_cols", [P, 3 * DT])
        qk_cols = sb("qk_cols", [P, 6])
        sink_rows = sb("sink_rows", [P, 2, 5])
        neg_sinks = sb("neg_sinks", [P, 2, 5])
        rstd = sb("rstd", [P, NT])
        sumsq = sb("sumsq", [P, NT])
        sqx = sb("sqx", [P, NT])
        sd_x = sb("sd_x", [P, NT])
        KEYS = T_P + PAST + T_S
        kt_a = sb("kt_a", [P, 2, KEYS])
        kt_b = sb("kt_b", [P, KEYS])
        kt_i = [sb(f"kt_i{c}", [P, KEYS]) for c in range(2)]
        kt_c = sb("kt_c", [P, KEYS])
        kc_cache = sb("kc_cache", [P, 5, P])
        v_a = sb("v_a", [P, 4, 2 * P])
        v_b = sb("v_b", [P, 4, P])
        with ExitStack() as scope:
            xrow = sb("xrow", [P, 3, D], F32, scope)
        with ExitStack() as scope:
            g_act = sb("g_act", [P, NT], F32, scope)
            g_sig = sb("g_sig", [P, NT], F32, scope)
            u_act = sb("u_act", [P, NT], F32, scope)
            gu = sb("gu", [P, NT], F32, scope)
            y_rows = sb("y_rows", [P, 2, 3, P], F32, scope)
        z_prep = sb("z_prep", [P, 10, NT])
        z_q = [sb(f"z_q{s}", [P, NT]) for s in range(2)]
        z_k = sb("z_k", [P, NT])
        z_v = sb("z_v", [P, NT])
        zw = z_v[0:H_IDX, :]
        q_n = [[sb(f"q_n{s}_{c}", [P, NT]) for c in range(2)] for s in range(2)]
        sq = sb("sq", [P, NT])
        sq_set = [z_prep[:, 4 + i, :] for i in range(3)]
        sd = sb("sd", [P, NT + 12])
        rinv = sb("rinv", [P, NT])
        v_c = sb("v_c", [P, 4, P])
        with ExitStack() as scope:
            flip = sb("flip", [P, P], F32, scope)
            gain_rows = sb("gain_rows", [3 * DT, P], F32, scope)
            qk_rows = sb("qk_rows", [6, P], F32, scope)
            t5_rows = sb("t5_rows", [T5_BUCKETS, H_A + H_B], F32, scope)
            hot = sb("hot", [T5_BUCKETS, VEC], F32, scope)
            c_rows = sb("c_rows", [P, 3, H_C], F32, scope)
            cache_rows = sb("cache_rows", [P, 9, P], F32, scope)
            vec_t5 = sb("vec_t5", [H_A + H_B, VEC], F32, scope)
            vec_c = sb("vec_c", [H_C, VEC], F32, scope)
        k_rows = sb("k_rows", [P, 3, P])
        s_buf = [sb(f"s_buf{s}", [P, 2, T_P]) for s in range(2)]
        p_t = [sb(f"p_t{s}", [P, 4, P]) for s in range(2)]
        bias_rev = [sb(f"bias_rev{s}", [P, 2, T_P]) for s in range(2)]
        idx_acc = [sb(f"idx_acc{r}", [P, n]) for r, n in enumerate((2 * P, P, PAST + T_S))]
        a_mask = [sb(f"a_mask{r}", [P, n]) for r, n in enumerate((2 * P, P, PAST + T_S))]
        nmax = [sb(f"nmax{s}", [P, 2]) for s in range(2)]
        snk = [sb(f"snk{s}", [P, 2]) for s in range(2)]
        esnk = [sb(f"esnk{s}", [P, 2]) for s in range(2)]
        esum = [sb(f"esum{s}", [P, 2]) for s in range(2)]
        einv = [sb(f"einv{s}", [P, 2]) for s in range(2)]
        q_scale = sb("q_scale", [P, 12])
        w_tok = sb("w_tok", [P, 3, H_IDX])
        top8 = sb("top8", [P, 8])
        CACHE_TILES = [(cache_rows[:, 0, :], kt_a[:, 0, T_P:T_P + PAST]), (cache_rows[:, 1, :], kt_a[:, 1, T_P:T_P + PAST]),
                       (cache_rows[:, 2, :], None), (cache_rows[:, 3, :], kt_b[:, T_P:T_P + PAST])]
        CACHE_TILES += [(cache_rows[:, 4 + i, :], kc_cache[:, i, :]) for i in range(5)]

        psum = [ctx.enter_context(nc.psum_tensor(f"bank{b}", [P, 512], F32)) for b in range(8)]
        bank_w = psum[0:2]
        bank_s = psum[2:4]
        bank_t = psum[4:6]
        bank_o = psum[6]
        bank_m = psum[7]

        vec_dram = nc.dram_tensor("bias_vectors", (H_A + H_B + H_C, VEC), F32, kind="Internal").ap()

        ld = [sem("strip_loaded0"), sem("strip_loaded1")]
        ld_wo = [sem("wo_strip_loaded0"), sem("wo_strip_loaded1")]
        hi_rdy = sem("w_hi_ready")
        lo_rdy = sem("w_lo_ready")
        used = sem("strip_multiplied")
        evac = sem("product_read")
        x_in = sem("x_loaded")
        small_in = sem("small_inputs_loaded")
        cache_in = sem("cache_rows_loaded")
        vcache_in = sem("v_cache_loaded")
        pool_built = sem("pool_constants_cleared")
        consts = sem("constants_built")
        start_tr = sem("start_transposed")
        start_cp = sem("start_copied")
        vec_out = sem("bias_vectors_stored")
        sqx_rdy = sem("x_squares_ready")
        acc_rdy = sem("x_squares_summed")
        hhi_rdy = sem("h_hi_ready")
        hlo_rdy = sem("h_lo_ready")
        rstd_rdy = sem("x_rstd_ready")
        sig_rdy = sem("silu_ready")
        gu_rdy = sem("gated_ready")
        guh_rdy = sem("gated_hi_ready")
        gul_rdy = sem("gated_lo_ready")
        m_done = sem("misc_bank_written")
        m_free = sem("misc_bank_read")
        sq_rdy = sem("squares_ready")
        rinv_rdy = sem("inverse_norm_ready")
        qk_rdy = sem("key_tile_normalized")
        set_sq = sem("set_squares_ready")
        kinv_rdy = sem("key_inverse_norm_ready")
        scale_rdy = sem("query_scales_ready")
        qn_half = sem("first_head_queries_placed")
        qn_rdy = sem("queries_placed")
        qk_done = sem("scores_done")
        s_add = sem("scores_biased")
        masked = sem("unselected_masked")
        mx_raw = sem("sink_max_step")
        sum_sunk = sem("sink_added")
        mx_rdy = sem("neg_max_ready")
        e_rdy = sem("exponentials_ready")
        r_rdy = sem("inverse_sums_ready")
        p_rdy = sem("probabilities_ready")
        t_done = sem("probabilities_transposed")
        c_done = sem("transposed_copied")
        pv_done = sem("unit_output_done")
        ohi_rdy = sem("output_hi_ready")
        olo_rdy = sem("output_lo_ready")
        bias_ld = [sem("bias_loaded0"), sem("bias_loaded1")]
        bias_rdy = sem("bias_ready")
        window_msk = sem("bias_window_masked")
        kc_rdy = sem("c_key_cache_placed")
        vc_ld = sem("c_value_cache_loaded")
        v_out = sem("v_rows_stored")
        k_out = sem("k_rows_stored")
        misc_out = sem("cache_tails_stored")
        iq_done = sem("index_products_done")
        irelu = sem("index_relu_done")
        iacc = sem("index_scores_summed")
        mask_rdy = sem("selection_ready")
        y_tr = sem("y_transposed")
        y_cp = sem("y_copied")
        y_out = [sem("y_stored0"), sem("y_stored1")]
        pe_passed = sem("narrow_product_begins")
        pool_passed = sem("pool_passed_wait")
        dve_link = sem("vector_step")

        block = ctx.enter_context(nc.Block())

        TOK = [slice(P, 2 * P), slice(0, P), slice(T_P, NT)]
        ROWS = [P, P, T_S]
        NKEY = [T_P, P, PAST + T_S]
        KEY0 = [0, 0, T_P]
        PREP = {"ka": (0, 2), "va": (2, 4), "qi": (4, 8), "kb": (8, 9), "vb": (9, 10)}
        CONSTS = 3

        def strip_no(ph, j, s):
            return j * 2 + (ph.n0 + s)

        def following(ph, j, s):
            if s == 0:
                return ph, j, 1
            if isinstance(j, int) and j == ph.strips // 2 - 1:
                return (ph.next, 0, 0) if ph.next else None
            return ph, j + 1, 0

        def bodies(eng, ph, body, peel_first=False, strips=2):
            count = ph.strips // strips
            start = 1 if peel_first else 0
            if peel_first:
                body(0)
            with eng.Fori(start, count - 1) as i:
                body(i)
            body(count - 1)

        idx_units = [(r, t) for r in range(3) for t in range(4)]
        PREP_ITEMS = {
            8: [("n", "ka0"), ("v", "va0")],
            9: [("n", "ka1"), ("v", "va1")],
            10: [("w",)] + [("i", u) for u in range(0, 4)],
            11: [("i", u) for u in range(4, 12)],
            12: [("n", "kb"), ("v", "vb"), ("t", 0)],
            13: [("k", "ka0"), ("t", 1)],
            14: [("k", "ka1"), ("t", 2)],
            15: [("k", "ki"), ("k", "kb"), ("s",)],
        }
        misc_no, norm_no, kout_no, vout_no = {}, {}, {}, {}
        at = 1 + 1
        for step in range(8, 16):
            for it in PREP_ITEMS[step]:
                if it[0] in "nvkws":
                    misc_no[it] = at
                    at += 1
                if it[0] == "n":
                    norm_no[it] = len(norm_no)
                if it[0] == "k":
                    kout_no[it] = len(kout_no)
                if it[0] == "v":
                    vout_no[it] = len(vout_no)
        KEY_NORMS = len(norm_no)
        MISC_CB, MISC_CB0 = 3, at
        MISC_A0 = MISC_CB0 + 4 * MISC_CB
        MISC_A1 = MISC_A0 + 3
        MISC_END = MISC_A1 + 2 * 2 + 1
        VOUT_PREP, KOUT_PREP = len(vout_no), len(kout_no)

        def norm_source(name):
            kt, z, g = {"ka0": (kt_a[:, 0, :], z_prep[:, 0, :], 1), "ka1": (kt_a[:, 1, :], z_prep[:, 1, :], 1),
                        "kb": (kt_b[:, :], z_prep[:, 8, :], 3), "kc": (kt_c[:, :], z_k[:, :], 5)}[name]
            return z, g, [(kt[:, 0:T_P], slice(0, T_P), slice(0, P)), (kt[:, T_P + PAST:KEYS], slice(T_P, NT), slice(0, P))]

        def scale_no(kind, b, p):
            return b + 1 if kind == "cb" else b * 2 + (p - 4)

        def set_squares(b, which):
            return b * 3 + (which + 1)

        def a_squares(b, p):
            return b * 2 + (5 + p + 1)

        def scale_col(p, r):
            return 4 * p + 2 * r if r < 2 else 8 + 2 * p

        @block.sync
        def _(sp):
            for t in range(2):
                sp.dma_start(xrow[:, t, :], xp[0, t * P:(t + 1) * P, :]).then_inc(x_in, 16)
            sp.dma_start(xrow[0:T_S, 2, :], xs[0]).then_inc(x_in, 16)

            def pieces(ph, j, s):
                half = [slice(0, 8), slice(8, ph.tiles)]
                m = ph.more
                if ph.name == "up":
                    w = (w_gate if s == 0 else w_up)[0, m["ffn"]].rearrange("(k p) n -> p k n", p=P)
                    col = bass.ds(j * P + m["f0"] * P, P)
                    return [(raw[s][:, k, :], w[:, k, col]) for k in half]
                if ph.name == "down":
                    f0, f1 = m["f0"], m["f0"] + m["size"]
                    w = w_down[0, m["ffn"], f0 * P:f1 * P].rearrange("(k p) n -> p k n", p=P)
                    col = bass.ds(j * 2 * P + s * P, P)
                    return [(raw[s][:, k, :], w[:, k, col]) for k in half]
                w = w_in[0].rearrange("(k p) n -> p k n", p=P)
                if ph.name == "prep":
                    if not isinstance(j, int) or j < 4:
                        col = bass.ds(j * 2 * P + (o_ka + s * P), P)
                        return [(raw[s][:, k, :], w[:, k, col]) for k in half]
                    if (j, s) == (4, 0):
                        return [(raw[s][:, :, c:c + HD], w[:, :, o_ki:o_ki + HD]) for c in (0, HD)]
                    if (j, s) == (4, 1):
                        return [(raw[s][:, k, 0:H_IDX], w[:, k, o_wi:o_wi + H_IDX]) for k in half]
                    col = slice(o_kb, o_kb + P) if s == 0 else slice(o_vb, o_vb + P)
                    return [(raw[s][:, k, :], w[:, k, col]) for k in half]
                raise AssertionError(ph.name)

            def w_in_cols(s, cols):
                w = w_in[0].rearrange("(k p) n -> p k n", p=P)
                if len(cols) == 1:
                    return [(raw[s][:, k, :], w[:, k, cols[0]]) for k in (slice(0, 8), slice(8, 16))]
                return [(raw[s][:, :, c * HD:(c + 1) * HD], w[:, :, cols[c]]) for c in range(2)]

            def load(ph, j, s, what=None):
                n = strip_no(ph, j, s)
                if not (isinstance(n, int) and n < 2):
                    sp.wait_ge(lo_rdy, n * 2 - 2)
                for dst, src in what or pieces(ph, j, s):
                    sp.dma_start(dst, src).then_inc(ld[s], 16)

            for ph in phases:
                if ph.name in ("up", "down"):
                    first = 1 if ph.n0 == 0 else 0
                    if first:
                        load(ph, 0, 0)
                        load(ph, 0, 1)
                    with sp.Fori(first, ph.strips // 2) as j:
                        load(ph, j, 0)
                        load(ph, j, 1)
                elif ph.name == "prep":
                    with sp.Fori(0, 4) as j:
                        load(ph, j, 0)
                        load(ph, j, 1)
                    for j in (4, 5):
                        load(ph, j, 0)
                        load(ph, j, 1)
                elif ph.name == "cb":
                    with sp.Fori(0, 5) as i:
                        load(ph, i * 2, 0, w_in_cols(0, [bass.ds(i * P + o_kc, P)]))
                        load(ph, i * 2, 1, w_in_cols(1, [bass.ds(i * P + o_qc, P)]))
                        load(ph, i * 2 + 1, 0, w_in_cols(0, [bass.ds(i * HD + o_qb, HD), bass.ds(i * HD + (o_qb + 5 * HD), HD)]))
                        load(ph, i * 2 + 1, 1, w_in_cols(1, [bass.ds(i * P + o_vc, P)]))
                elif ph.name == "a":
                    with sp.Fori(0, 3) as i:
                        for s in range(2):
                            c = o_qa + s * 6 * HD
                            load(ph, i, s, w_in_cols(s, [bass.ds(i * HD + c, HD), bass.ds(i * HD + (c + 3 * HD), HD)]))
                else:
                    wo = w_out[0]
                    with sp.Fori(0, ph.strips // 2) as j:
                        for s in range(2):
                            sp.wait_ge(lo_rdy, strip_no(ph, j, s) * 2 - 2)
                            col = bass.ds(j * 2 * P + s * P, P)
                            for g in range(2):
                                for c in range(2):
                                    r = (6 * g + 3 * c) * HD
                                    sp.dma_start(raw[s][c * HD:(c + 1) * HD, 3 * g:3 * g + 3, :],
                                                 wo[r:r + 3 * HD, col].rearrange("(k p) n -> p k n", p=HD)).then_inc(ld_wo[s], 16)
                            for c in range(2):
                                r = (H_A + 5 * c) * HD
                                sp.dma_start(raw[s][c * HD:(c + 1) * HD, 6:11, :],
                                             wo[r:r + 5 * HD, col].rearrange("(k p) n -> p k n", p=HD)).then_inc(ld_wo[s], 16)
                            r = (H_A + H_B) * HD
                            sp.dma_start(raw[s][:, 11:16, :],
                                         wo[r:r + 5 * P, col].rearrange("(k p) n -> p k n", p=P)).then_inc(ld_wo[s], 16)
        WO_LOADS = 7

        @block.tensor
        def _(pe):
            def products(ph, j, s, rhs, ks, n, first_k, last_k, when=None):
                for k in ks:
                    if when:
                        when(k)
                    hi, lo = rhs(k)
                    out = bank_w[s][:, 0:NT]
                    pe.matmul(out, w_hi[s][:, k, :], hi, start=(k == first_k), stop=False)
                    pe.matmul(out, w_hi[s][:, k, :], lo, start=False, stop=False)
                    mm = pe.matmul(out, w_lo[s][:, k, :], hi, start=False, stop=(k == last_k))
                return mm

            def strip(ph, j, s, rhs, when=None, part=(0, None)):
                n = strip_no(ph, j, s)
                a, b = part[0], part[1] or ph.tiles
                if a == 0 and not (isinstance(n, int) and n < 2):
                    pe.wait_ge(evac, n - 1)
                if a < 8:
                    if a == 0:
                        pe.wait_ge(lo_rdy, n * 2 + 1)
                    mm = products(ph, j, s, rhs, range(a, min(b, 8)), n, 0, ph.tiles - 1, when)
                if b > 8:
                    if a <= 8:
                        pe.wait_ge(lo_rdy, n * 2 + 2)
                    mm = products(ph, j, s, rhs, range(max(a, 8), b), n, 0, ph.tiles - 1, when)
                if b == ph.tiles:
                    mm.then_inc(used, 1)

            def narrow_strip(ph, j, s, rhs, m):
                n = strip_no(ph, j, s)
                pe.wait_ge(evac, n - 1)
                pe.wait_ge(lo_rdy, n * 2 + 2)
                out = bank_w[s][0:m, 0:NT]
                for k in range(ph.tiles):
                    hi, lo = rhs(k)
                    pe.matmul(bank_w[s][:, 0:NT], w_hi[s][:, k, :], hi, start=(k == 0), stop=False)
                    pe.matmul(bank_w[s][:, 0:NT], w_hi[s][:, k, :], lo, start=False, stop=False)
                    mm = pe.matmul(bank_w[s][:, 0:NT], w_lo[s][:, k, :], hi, start=False, stop=(k == ph.tiles - 1))
                mm.then_inc(used, 1)

            def h_rhs(k):
                return h_hi[:, k, :], h_lo[:, k, :]

            def gu_rhs(k):
                return gu_hi[:, k, :], gu_lo[:, k, :]

            def o_rhs(k):
                return o_hi[:, k, :], o_lo[:, k, :]

            def misc_begin(m):
                if not (isinstance(m, int) and m == 0):
                    pe.wait_ge(m_free, m)

            def x_norm(index):
                pe.wait_ge(acc_rdy, DT * (index + 1))
                misc_begin([0, 1, MISC_END][index])
                pe.matmul(bank_m[:, 0:NT], mean_d[:, :], sumsq[:, :], start=True, stop=True).then_inc(m_done, 1)

            def head_sum(m, q):
                pe.wait_ge(sq_rdy, q + 1)
                misc_begin(m)
                pe.matmul(bank_m[:, 0:NT], mean_hd[:, :], sq[:, :], start=True, stop=True).then_inc(m_done, 1)

            def set_sums(m, squares_done, keys, pairs):
                pe.wait_ge(set_sq, squares_done)
                misc_begin(m)
                if keys:
                    pe.matmul(bank_m[:, 0:NT], mean_hd[:, :], sq_set[0], start=True, stop=True)
                for p in pairs:
                    for r in range(3):
                        c = NT + scale_col(p, r)
                        mm = pe.matmul(bank_m[0:ROWS[r], c:c + 2], sq_set[1 + p][:, TOK[r]], mean_hd2[:, :], start=True, stop=True)
                mm.then_inc(m_done, 1)

            def turn_rows(m, tile, sample0):
                misc_begin(m)
                for t in range(2):
                    pe.transpose(bank_m[:, t * P:(t + 1) * P], tile[:, t * P:(t + 1) * P], ident[:, :])
                pe.transpose(bank_m[0:T_S, 2 * P:3 * P], tile[:, sample0:sample0 + T_S], ident[:, :]).then_inc(m_done, 1)

            def settled():
                pe.sem_inc(pe_passed, 1)

            def scores(U, r, b, q, kt):
                if not (isinstance(U, int) and U < 2):
                    pe.wait_ge(s_add, U - 1)
                out = bank_s[b]
                for c in range(2):
                    mm = pe.matmul(out[0:ROWS[r], c * NKEY[r]:(c + 1) * NKEY[r]], q[c][:, TOK[r]],
                                   kt[:, KEY0[r]:KEY0[r] + NKEY[r]], start=True, stop=True)
                mm.then_inc(qk_done, 1)

            def turn_p(U, r, b):
                pe.wait_ge(p_rdy, U + 1)
                if not (isinstance(U, int) and U < 2):
                    pe.wait_ge(c_done, U - 1)
                m = ROWS[r]
                if r == 2:
                    settled()
                for c in range(2):
                    if r < 2:
                        for kc in range(NKEY[r] // P):
                            o = (c * (NKEY[r] // P) + kc) * P
                            mm = pe.transpose(bank_t[b][:, o:o + P], s_buf[b][:, c, kc * P:(kc + 1) * P], ident[:, :])
                    else:
                        pe.transpose(bank_t[b][:, c * P:c * P + m], s_buf[b][0:m, c, 0:P], ident[0:m, 0:m])
                        mm = pe.transpose(bank_t[b][0:T_S, (2 + c) * P:(2 + c) * P + m], s_buf[b][0:m, c, P:P + T_S],
                                          ident[0:m, 0:m])
                mm.then_inc(t_done, 1)

            def out_v(U, r, b, pr, v):
                pe.wait_ge(c_done, U + 1)
                if r == 0 and not (isinstance(pr, int) and pr < 1):
                    pe.wait_ge(olo_rdy, pr)
                for c in range(2):
                    out = bank_o[c * HD:(c + 1) * HD, TOK[r]]
                    cols = slice(c * HD, (c + 1) * HD)
                    if r < 2:
                        nk = NKEY[r] // P
                        for kc in range(nk):
                            mm = pe.matmul(out, v[:, kc, cols], p_t[b][:, c * nk + kc, :], start=(kc == 0), stop=(kc == nk - 1))
                    else:
                        pe.matmul(out, v[:, 2, cols], p_t[b][:, c, 0:T_S], start=True, stop=False)
                        mm = pe.matmul(out, v[0:T_S, 3, cols], p_t[b][0:T_S, 2 + c, 0:T_S], start=False, stop=True)
                mm.then_inc(pv_done, 1)

            def attention(kind, body, turn, piece, sums):
                U, pr = body * 6, body * 2
                if kind == "cb":
                    kt, v = [kt_c, kt_b], [v_c, v_b]
                else:
                    kt, v = [kt_a[:, 0, :], kt_a[:, 1, :]], [v_a[:, :, 0:P], v_a[:, :, P:2 * P]]

                def sc(u):
                    p, r = divmod(u, 3)
                    if r == 0:
                        pe.wait_ge(qn_rdy, body * 2 + (p + 1))
                        if p == 0 and kind == "cb":
                            pe.wait_ge(qk_rdy, body + (KEY_NORMS + 1))
                    if u == 2 and kind == "cb":
                        pe.wait_ge(kc_rdy, body + 1)
                    scores(U + u, r, u % 2, q_n[p], kt[p])

                def tp(u):
                    turn_p(U + u, u % 3, u % 2)

                def pv(u):
                    p, r = divmod(u, 3)
                    if u == 0 and kind == "cb":
                        pe.wait_ge(m_free, turn + 1)
                        pe.wait_ge(vc_ld, body * 16 + 16)
                    out_v(U + u, r, u % 2, pr + p, v[p])

                for k in range(8):
                    piece(k)
                    if k == 0:
                        if kind == "cb":
                            turn_rows(turn, z_v, T_P)
                    if 2 <= k:
                        tp(k - 2)
                    if k < 6:
                        sc(k)
                    if k == 1 and kind == "cb":
                        turn_rows(turn + 1, kt_c, T_P + PAST)
                    if 3 <= k:
                        pv(k - 3)
                    if k in sums:
                        set_sums(*sums[k])
                    if k == 7:
                        pv(5)

            def prep_items(step):
                for it in PREP_ITEMS[step]:
                    if it[0] == "n":
                        head_sum(misc_no[it], norm_no[it])
                    elif it[0] == "v":
                        if it[1] == "vb":
                            pe.wait_ge(evac, phase["prep"].n0 + 12)
                            turn_rows(misc_no[it], z_prep[:, 9, :], T_P)
                        else:
                            pe.wait_ge(evac, phase["prep"].n0 + 4)
                            turn_rows(misc_no[it], z_prep[:, 2 + int(it[1][2]), :], T_P)
                    elif it[0] == "k":
                        kt = {"ka0": kt_a[:, 0, :], "ka1": kt_a[:, 1, :], "ki": kt_i[0], "kb": kt_b}[it[1]]
                        if it[1] != "ki":
                            pe.wait_ge(qk_rdy, norm_no[("n", it[1])] + 1)
                        turn_rows(misc_no[it], kt, T_P + PAST)
                    elif it[0] == "s":
                        set_sums(misc_no[it], set_squares(0, 2), True, (0, 1))
                    elif it[0] == "w":
                        misc_begin(misc_no[it])
                        pe.wait_ge(evac, phase["prep"].n0 + 10)
                        for t, (a, b) in enumerate(((0, P), (P, 2 * P), (2 * P, NT))):
                            mm = pe.transpose(bank_m[0:b - a, t * H_IDX:(t + 1) * H_IDX], zw[:, a:b], ident[0:H_IDX, 0:H_IDX])
                        mm.then_inc(m_done, 1)
                    elif it[0] == "i":
                        u = it[1]
                        r, t = idx_units[u]
                        pe.wait_ge(evac, phase["prep"].n0 + 9)
                        if u >= 2:
                            pe.wait_ge(irelu, u - 1)
                        for c in range(2):
                            mm = pe.matmul(bank_s[u % 2][0:ROWS[r], c * NKEY[r]:(c + 1) * NKEY[r]],
                                           z_prep[:, 4 + t, TOK[r]], kt_i[c][:, KEY0[r]:KEY0[r] + NKEY[r]],
                                           start=True, stop=True)
                        mm.then_inc(iq_done, 1)

            phase = {p.name: p for p in phases if p.name not in ("up", "down")}

            pe.wait_ge(consts, CONSTS)
            pe.wait_ge(small_in, 16 * 7)
            start_bank = [0]

            def start_slot():
                n = start_bank[0]
                start_bank[0] += 1
                if n >= 2:
                    pe.wait_ge(start_cp, n - 1)
                return bank_t[n % 2]

            b = start_slot()
            pe.transpose(b[:, 0:3 * DT], gain_rows[:, :], ident[0:3 * DT, 0:3 * DT])
            pe.transpose(b[:, 3 * DT:3 * DT + 6], qk_rows[:, :], ident[0:6, 0:6]).then_inc(start_tr, 1)
            pe.wait_ge(x_in, 48)
            for k in range(DT):
                b = start_slot()
                for t in range(2):
                    pe.transpose(b[:, t * P:(t + 1) * P], xrow[:, t, k * P:(k + 1) * P], ident[:, :])
                pe.transpose(b[:, T_P:NT], xrow[0:T_S, 2, k * P:(k + 1) * P], ident[0:T_S, 0:T_S]).then_inc(start_tr, 1)
            b = start_slot()
            pe.matmul(b[0:H_A + H_B, 0:VEC], t5_rows[:, :], hot[:, :],
                      start=True, stop=True).then_inc(start_tr, 1)
            b = start_slot()
            for blk in range(3):
                c0 = (2 - blk) * P
                mm = pe.matmul(b[0:H_C, c0:c0 + P], c_rows[:, blk, :], flip[:, :], start=True, stop=True)
            mm.then_inc(start_tr, 1)
            pe.wait_ge(cache_in, 16 * 5)
            for src, _ in CACHE_TILES:
                b = start_slot()
                pe.transpose(b[:, 0:P], src, ident[:, :]).then_inc(start_tr, 1)

            def h_when(index):
                def when(k):
                    pe.wait_ge(hlo_rdy, DT * index + k + 1)
                return when

            gated = 0
            for ph in phases:
                if ph.name == "up":
                    if ph.more["first"]:
                        index = 2 * ph.more["ffn"]
                        strip(ph, 0, 0, h_rhs, h_when(index))
                        x_norm(index)
                        strip(ph, 0, 1, h_rhs)
                    with pe.Fori(1 if ph.more["first"] else 0, ph.strips // 2) as j:
                        strip(ph, j, 0, h_rhs)
                        strip(ph, j, 1, h_rhs)
                elif ph.name == "down":
                    last = ph.tiles - 1

                    def gu_when(k, g=gated, last=last):
                        if k == 0:
                            pe.wait_ge(gul_rdy, g + last)
                        if k == last:
                            pe.wait_ge(gul_rdy, g + last + 1)
                    with pe.Fori(0, ph.strips // 2) as j:
                        strip(ph, j, 0, gu_rhs, gu_when)
                        strip(ph, j, 1, gu_rhs, gu_when)
                    gated += ph.tiles
                elif ph.name == "prep":
                    strip(ph, 0, 0, h_rhs, h_when(1))
                    x_norm(1)
                    strip(ph, 0, 1, h_rhs)
                    with pe.Fori(1, 4) as j:
                        strip(ph, j, 0, h_rhs)
                        strip(ph, j, 1, h_rhs)
                    strip(ph, 4, 0, h_rhs)
                    prep_items(8)
                    narrow_strip(ph, 4, 1, h_rhs, H_IDX)
                    prep_items(9)
                    strip(ph, 5, 0, h_rhs)
                    prep_items(10)
                    strip(ph, 5, 1, h_rhs)
                    prep_items(11)
                    pe.wait_ge(vcache_in, 32)
                elif ph.name == "cb":
                    for t in range(4):
                        strip(ph, t // 2, t % 2, h_rhs)
                        prep_items(12 + t)

                    def cb_body(i, ph=ph):
                        m = i * MISC_CB + (MISC_CB0 - MISC_CB)
                        pe.wait_ge(evac, i * 4 + ph.n0)
                        attention("cb", i - 1, m, lambda k: strip(ph, i * 2 + k // 4, k // 2 % 2, h_rhs, part=(k % 2 * 8, k % 2 * 8 + 8)),
                                  {6: (m + 2, set_squares(i, 2), True, (0, 1))})
                    cb_body(1)
                    with pe.Fori(2, 5) as i:
                        cb_body(i)
                elif ph.name == "a":
                    def a_body(i, ph=ph):
                        quarter = lambda k: strip(ph, i, k // 4, h_rhs, part=(k % 4 * 4, k % 4 * 4 + 4))
                        if isinstance(i, int):
                            pe.wait_ge(evac, ph.n0)
                            attention("cb", 4, MISC_A0, quarter, {6: (MISC_A0 + 2, a_squares(5, 0), False, (0,))})
                        else:
                            m = i * 2 + (MISC_A1 - 2)
                            attention("a", i + 4, None, quarter, {1: (m, a_squares(i + 4, 1), False, (1,)),
                                                                  6: (m + 1, a_squares(i + 5, 0), False, (0,))})
                    a_body(0)
                    with pe.Fori(1, 3) as i:
                        a_body(i)
                else:
                    order = [11, 12, 13, 14, 15, 6, 7, 8, 9, 10, 0, 3, 1, 4, 2, 5]

                    def wo(j, s, ks):
                        n = strip_no(ph, j, s)
                        if ks[0] == order[0]:
                            pe.wait_ge(evac, n - 1)
                            pe.wait_ge(lo_rdy, n * 2 + 2)
                        mm = products(ph, j, s, o_rhs, ks, n, order[0], order[-1])
                        if ks[-1] == order[-1]:
                            mm.then_inc(used, 1)

                    def piece(k):
                        if k == 0:
                            pe.wait_ge(olo_rdy, 10)
                        if k == 2:
                            pe.wait_ge(olo_rdy, 14)
                        for s in range(2):
                            a, b = (min(max(4 * x - 14 * s, 0), 14) for x in (k, k + 1))
                            if a < b:
                                wo(0, s, order[a:b])
                    attention("a", 7, None, piece, {1: (MISC_END - 1, a_squares(7, 1), False, (1,))})
                    pe.wait_ge(olo_rdy, 16)
                    wo(0, 0, order[14:16])
                    wo(0, 1, order[14:16])
                    with pe.Fori(1, ph.strips // 2) as j:
                        wo(j, 0, order)
                        wo(j, 1, order)
            for k in range(DT):
                pe.wait_ge(evac, phases[-1].n0 + k + 1)
                if k >= 2:
                    pe.wait_ge(y_cp, k - 1)
                for t in range(2):
                    pe.transpose(bank_t[k % 2][:, t * P:(t + 1) * P], xT[:, k, t * P:(t + 1) * P], ident[:, :])
                pe.transpose(bank_t[k % 2][0:T_S, 2 * P:3 * P], xT[:, k, T_P:NT], ident[:, :]).then_inc(y_tr, 1)

        PAIR_TILE = {"c": 11, "b": 6}
        START_COPIES = 1 + DT + 2 + 9

        def v_place(name):
            if name == "vb":
                cols = slice(0, P)
                flat = lambda t: t[0, 0].rearrange("t h d -> t (h d)")
                return v_b, cols, flat(pbv), flat(sbv)[P - T_S:P], 1
            t = int(name[2])
            cols = slice(t * P, (t + 1) * P)
            flat = lambda x: x[0, 0].rearrange("t h d -> t (h d)")[:, cols]
            return v_a, cols, flat(pav), flat(sav), 0

        def k_place(name):
            flat = lambda x: x[0, 0].rearrange("t h d -> t (h d)")
            if name == "ki":
                return paki[0, 0], saki[0, 0], 0, HD
            if name == "kb":
                return flat(pbk), flat(sbk)[P - T_S:P], 1, P
            cols = slice(int(name[2]) * P, (int(name[2]) + 1) * P)
            return flat(pak)[:, cols], flat(sak)[:, cols], 0, P

        @block.scalar
        def _(act):
            act.dma_start(gain_rows[:, :], gains[0].rearrange("g (k p) -> (g k) p", p=P)).then_inc(small_in, 16)
            for c in range(2):
                act.dma_start(qk_rows[:, c * HD:(c + 1) * HD], qk_norm[0]).then_inc(small_in, 16)
            act.dma_start(t5_rows[:, :], t5_bias).then_inc(small_in, 16)
            act.dma_start(hot[:, :], onehot).then_inc(small_in, 16)
            act.dma_start(c_rows[:, :, :], c_bias[0, 0:VEC].rearrange("(b p) h -> p b h", p=P)).then_inc(small_in, 16)
            act.dma_start(sink_rows[:, :, :].rearrange("p a b -> p (a b)"), bass.AP(sinks.tensor, 0, [[0, P], [1, H_B]])).then_inc(small_in, 16)
            act.dma_start(cache_rows[:, 0:2, :].rearrange("p t c -> p (t c)"), cak[0, 0].rearrange("t h d -> t (h d)")).then_inc(cache_in, 16)
            for c in range(2):
                act.dma_start(cache_rows[:, 2, c * HD:(c + 1) * HD], caki[0, 0]).then_inc(cache_in, 16)
            act.dma_start(cache_rows[:, 3, :], cbk[0, 0].rearrange("t h d -> t (h d)")).then_inc(cache_in, 16)
            act.dma_start(cache_rows[:, 4:9, :].rearrange("p t c -> p (t c)"), cck[0, 0].rearrange("t h d -> t (h d)")).then_inc(cache_in, 16)
            act.dma_start(v_a[:, 2, :], cav[0, 0].rearrange("t h d -> t (h d)")).then_inc(vcache_in, 16)
            act.dma_start(v_b[:, 2, :], cbv[0, 0].rearrange("t h d -> t (h d)")).then_inc(vcache_in, 16)

            def split(at, halves=(0, 1)):
                if at is None:
                    return
                ph, j, s = at
                n = strip_no(ph, j, s)
                if 0 in halves:
                    if ph.name == "wo":
                        act.wait_ge(ld_wo[s], j * (16 * WO_LOADS) + 16 * WO_LOADS)
                    else:
                        act.wait_ge(ld[s], j * 32 + (ph.ld0 * 32 + 32))
                    if not (isinstance(n, int) and n < 2):
                        act.wait_ge(used, n - 1)
                for half in halves:
                    k = (slice(0, 8), slice(8, ph.tiles))[half]
                    act.activation(w_hi[s][:, k, :], raw[s][:, k, :], ACT.Copy).then_inc(hi_rdy, 1)

            def h_tile(index, j):
                H = j + DT * index
                if not (isinstance(H, int) and H == 0):
                    act.wait_ge(acc_rdy, H)
                act.activation(sqx[:, :], xT[:, j, :], ACT.Square).then_inc(sqx_rdy, 1)
                act.activation(h_hi[:, j, :], xT[:, j, :], ACT.Copy, scale=g_cols[:, bass.ds(j + index * DT, 1)]).then_inc(hhi_rdy, 1)

            def x_norm(index):
                m = [0, 1, MISC_END][index]
                act.wait_ge(m_done, m + 1)
                if index:
                    act.wait_ge(rstd_rdy, index)
                act.activation(sd_x[:, :], bank_m[:, 0:NT], ACT.Sqrt, bias=eps[:, :]).then_inc(m_free, 1)

            def squares(z, n_done):
                act.wait_ge(evac, n_done)
                act.activation(sq[:, :], z, ACT.Square).then_inc(sq_rdy, 1)

            def deviation(m, q):
                act.wait_ge(m_done, m + 1)
                if not (isinstance(q, int) and q == 0):
                    act.wait_ge(rinv_rdy, q)
                act.activation(sd[:, 0:NT], bank_m[:, 0:NT], ACT.Sqrt, bias=eps[:, :]).then_inc(m_free, 1)

            def set_deviation(m, b, keys, pairs):
                act.wait_ge(m_done, m + 1)
                if keys:
                    if not (isinstance(b, int) and b == 0):
                        act.wait_ge(kinv_rdy, b)
                    else:
                        act.wait_ge(rinv_rdy, KEY_NORMS)
                else:
                    act.wait_ge(scale_rdy, scale_no("a", b, pairs[0]) - 1)
                    if isinstance(b, int):
                        act.wait_ge(kinv_rdy, 5)
                c0, c1 = NT + 4 * pairs[0], NT + 4 * pairs[-1] + 4
                act.activation(sd[:, 0 if keys else c0:c1], bank_m[:, 0 if keys else c0:c1], ACT.Sqrt, bias=eps[:, :])
                c0, c1 = NT + 8 + 2 * pairs[0], NT + 8 + 2 * pairs[-1] + 2
                act.activation(sd[0:T_S, c0:c1], bank_m[0:T_S, c0:c1], ACT.Sqrt, bias=eps[0:T_S, :]).then_inc(m_free, 1)

            def place_v(m, v, cols):
                act.wait_ge(m_done, m + 1)
                act.activation(v[:, 0:2, cols], bank_m[:, 0:2 * P].rearrange("p (t c) -> p t c", t=2), ACT.Copy)
                act.activation(v[0:T_S, 3, cols], bank_m[0:T_S, 2 * P:3 * P], ACT.Copy).then_inc(m_free, 1)

            def place_k(m, kout):
                act.wait_ge(m_done, m + 1)
                if not (isinstance(kout, int) and kout == 0):
                    act.wait_ge(k_out, kout * 32)
                act.activation(k_rows[:, 0:2, :], bank_m[:, 0:2 * P].rearrange("p (t c) -> p t c", t=2), ACT.Copy)
                act.activation(k_rows[0:T_S, 2, :], bank_m[0:T_S, 2 * P:3 * P], ACT.Copy).then_inc(m_free, 1)

            def exps(U, u, sink):
                b, r = u % 2, u % 3
                m, n = ROWS[r], NKEY[r]
                act.wait_ge(mx_rdy, U + u + 1)
                for c in range(2):
                    a = act.activation(s_buf[b][0:m, c, 0:n], s_buf[b][0:m, c, 0:n], ACT.Exp, bias=nmax[b][0:m, c:c + 1],
                                       accum_out=esum[b][0:m, c:c + 1])
                if sink:
                    a = act.activation(esnk[b][0:m, :], snk[b][0:m, :], ACT.Exp)
                a.then_inc(e_rdy, 1)

            def copy_t(U, u):
                b, r = u % 2, u % 3
                act.wait_ge(t_done, U + u + 1)
                if not (isinstance(U, int) and U + u < 2):
                    act.wait_ge(pv_done, U + (u - 1))
                pt = bank_t[b][:, :].rearrange("p (t c) -> p t c", t=4)
                if r < 2:
                    k = 4 - 2 * r
                    a = act.activation(p_t[b][:, 0:k, :], pt[:, 0:k, :], ACT.Copy)
                else:
                    act.activation(p_t[b][:, 0:2, 0:T_S], pt[:, 0:2, 0:T_S], ACT.Copy)
                    a = act.activation(p_t[b][0:T_S, 2:4, 0:T_S], pt[0:T_S, 2:4, 0:T_S], ACT.Copy)
                a.then_inc(c_done, 1)

            def out_hi(U, p, tile):
                act.wait_ge(pv_done, U + (3 * p + 3))
                act.activation(o_hi[:, tile, :], bank_o[:, 0:NT], ACT.Copy).then_inc(ohi_rdy, 1)

            def prep_items(step):
                for it in PREP_ITEMS[step]:
                    if it[0] == "n":
                        z, done = {"ka0": (0, 1), "ka1": (1, 2), "kb": (8, 11)}[it[1]]
                        squares(z_prep[:, z, :], phase["prep"].n0 + done)
                        deviation(misc_no[it], norm_no[it])
                    elif it[0] == "v":
                        v, cols, _, _, _ = v_place(it[1])
                        place_v(misc_no[it], v, cols)
                    elif it[0] == "k":
                        place_k(misc_no[it], kout_no[it])
                    elif it[0] == "s":
                        set_deviation(misc_no[it], 0, True, (0, 1))
                    elif it[0] == "w":
                        act.wait_ge(m_done, misc_no[it] + 1)
                        act.activation(w_tok[:, 0:2, :], bank_m[:, 0:2 * H_IDX].rearrange("p (t c) -> p t c", t=2), ACT.Copy)
                        act.activation(w_tok[0:T_S, 2, :], bank_m[0:T_S, 2 * H_IDX:3 * H_IDX], ACT.Copy).then_inc(m_free, 1)
                    elif it[0] == "i":
                        u = it[1]
                        r, _ = idx_units[u]
                        act.wait_ge(iq_done, u + 1)
                        if u >= 2:
                            act.wait_ge(iacc, 2 * u - 2)
                        m, n = ROWS[r], NKEY[r]
                        act.activation(s_buf[u % 2][0:m, :, 0:n], bank_s[u % 2][0:m, 0:2 * n].rearrange("p (c k) -> p c k", c=2),
                                       ACT.Relu).then_inc(irelu, 1)

            def attention(body, kind, turn, split_half, tiles, sums):
                U = body * 6
                split_half(0)
                for k in range(8):
                    if k == 0 and kind == "cb":
                        act.wait_ge(v_out, body * 32 + VOUT_PREP * 32)
                        if not (isinstance(body, int) and body == 0):
                            act.wait_ge(pv_done, U)
                        place_v(turn, v_c, slice(0, P))
                    if k == 1 and kind == "cb":
                        place_k(turn + 1, body + KOUT_PREP)
                    if k in sums and k < 6:
                        set_deviation(*sums[k])
                    if k == 6:
                        out_hi(U, 0, tiles[0])
                    if 2 <= k:
                        copy_t(U, k - 2)
                    if k < 7:
                        split_half(k + 1)
                    if k < 6:
                        exps(U, k, kind == "cb" and k >= 3)
                    if k in sums and k >= 6:
                        set_deviation(*sums[k])
                out_hi(U, 1, tiles[1])

            phase = {p.name: p for p in phases if p.name not in ("up", "down")}

            split((phases[0], 0, 0))
            for j in range(DT):
                act.wait_ge(start_cp, 2 + j)
                h_tile(0, j)

            for ph in phases:
                if ph.name == "up":
                    F0 = sum(p.more["size"] for p in phases[:phases.index(ph)] if p.name == "up")

                    def body(j, ph=ph, F0=F0):
                        F = j + F0
                        n = strip_no(ph, j, 0)
                        split(following(ph, j, 0))
                        if ph.more["first"] and isinstance(j, int) and j == 0:
                            x_norm(2 * ph.more["ffn"])
                        act.wait_ge(evac, n + 1)
                        if not (isinstance(F, int) and F == 0):
                            act.wait_ge(gu_rdy, F)
                        act.activation(g_sig[:, :], g_act[:, :], ACT.Silu).then_inc(sig_rdy, 1)
                        split(following(ph, j, 1))
                        act.wait_ge(gu_rdy, F + 1)
                        act.activation(gu_hi[:, j, :], gu[:, :], ACT.Copy).then_inc(guh_rdy, 1)
                    bodies(act, ph, body, peel_first=ph.more["first"])
                elif ph.name == "down" or ph.name == "wo":
                    index = 1 if ph.name == "down" else 2
                    h_after = ph.name == "wo" or (ph.more["last"] and ph.more["ffn"] == 0)

                    def body(j, ph=ph, index=index, h_after=h_after):
                        for s in range(2):
                            if ph.name == "wo" and isinstance(j, int) and j == 0:
                                if s == 0:
                                    split(following(ph, 0, 0))
                                    attend_tail()
                                else:
                                    split(following(ph, 0, 1))
                            else:
                                split(following(ph, j, s))
                            if h_after:
                                act.wait_ge(evac, strip_no(ph, j, s) + 1)
                                h_tile(index, j * 2 + s)

                    def attend_tail():
                        attention(7, "a", None, lambda k: None, (2, 5), {1: (MISC_END - 1, 7, False, (1,))})
                    bodies(act, ph, body, peel_first=ph.name == "wo")
                elif ph.name == "prep":
                    def body(j, ph=ph):
                        split(following(ph, j, 0))
                        if isinstance(j, int) and j == 0:
                            x_norm(1)
                        split(following(ph, j, 1))
                    body(0)
                    with act.Fori(1, 4) as j:
                        body(j)
                    for t in range(4):
                        split(following(ph, 4 + t // 2, t % 2))
                        prep_items(8 + t)
                elif ph.name == "cb":
                    for t in range(4):
                        split(following(ph, t // 2, t % 2))
                        prep_items(12 + t)

                    def body(i, ph=ph):
                        m = i * MISC_CB + (MISC_CB0 - MISC_CB)
                        order = [(ph, i * 2, 1), (ph, i * 2 + 1, 0), (ph, i * 2 + 1, 1),
                                 (ph, i * 2 + 2, 0) if not isinstance(i, int) or i < 4 else (ph.next, 0, 0)]
                        attention(i - 1, "cb", m, lambda k: split(order[k // 2], (k % 2,)),
                                  (i + (PAIR_TILE["c"] - 1), i + (PAIR_TILE["b"] - 1)), {6: (m + 2, i, True, (0, 1))})
                    body(1)
                    with act.Fori(2, 4) as i:
                        body(i)
                    body(4)
                elif ph.name == "a":
                    def body(i, ph=ph):
                        order = [(ph, i, 1), following(ph, i, 1)]
                        split_half = lambda k: split(order[k // 4], (k // 2 % 2,)) if k % 2 == 0 else None
                        if i == 0:
                            attention(4, "cb", MISC_A0, split_half, (PAIR_TILE["c"] + 4, PAIR_TILE["b"] + 4),
                                      {6: (MISC_A0 + 2, 5, False, (0,))})
                        else:
                            m = i * 2 + (MISC_A1 - 2)
                            attention(i + 4, "a", None, split_half, (i - 1, i + 2),
                                      {1: (m, i + 4, False, (1,)), 6: (m + 1, i + 5, False, (0,))})
                    body(0), body(1), body(2)
            yp_t, ys_t = yp[0].rearrange("(t p) c -> p t c", p=P), ys[0]
            for k in range(DT):
                act.wait_ge(y_cp, k + 1)
                act.dma_start(yp_t[:, :, k * P:(k + 1) * P], y_rows[:, k % 2, 0:2, :]).then_inc(y_out[k % 2], 16)
                act.dma_start(ys_t[:, k * P:(k + 1) * P], y_rows[0:T_S, k % 2, 2, :]).then_inc(y_out[k % 2], 16)
            for stored in y_out:
                act.wait_ge(stored, DT // 2 * 32)

        @block.vector
        def _(dve):
            steps = [0]

            def link(ins):
                steps[0] += 1
                ins.then_inc(dve_link, 1)
                dve.wait_ge(dve_link, steps[0])

            def split(at, halves=(0, 1)):
                if at is None:
                    return
                ph, j, s = at
                n = strip_no(ph, j, s)
                for half in halves:
                    k = (slice(0, 8), slice(8, ph.tiles))[half]
                    dve.wait_ge(hi_rdy, n * 2 + (half + 1))
                    dve.tensor_tensor(w_lo[s][:, k, :], raw[s][:, k, :], w_hi[s][:, k, :].bitcast(F32), ALU.subtract)\
                       .then_inc(lo_rdy, 1)

            def h_tile(index, j):
                H = j + DT * index
                dve.wait_ge(sqx_rdy, H + 1)
                if not (isinstance(H, int) and H == 0):
                    dve.wait_ge(acc_rdy, H)
                dve.tensor_tensor(sumsq[:, :], sumsq[:, :], sqx[:, :], ALU.add).then_inc(acc_rdy, 1)
                dve.wait_ge(hhi_rdy, H + 1)
                dve.scalar_tensor_tensor(h_lo[:, j, :], xT[:, j, :], g_cols[:, bass.ds(j + index * DT, 1)],
                                         h_hi[:, j, :].bitcast(F32), ALU.mult, ALU.subtract).then_inc(hlo_rdy, 1)

            def x_norm(index, n):
                m = [0, 1, MISC_END][index]
                dve.wait_ge(m_free, m + 1)
                if n:
                    dve.wait_ge(evac, n)
                dve.reciprocal(rstd[:, :], sd_x[:, :]).then_inc(rstd_rdy, 1)
                dve.wait_ge(rstd_rdy, index + 1)

            def read(n, s, dst, rows=slice(0, P), cols=slice(0, NT)):
                dve.wait_ge(used, n + 1)
                return dve.tensor_tensor(dst, bank_w[s][rows, cols], rstd[rows, cols], ALU.mult)

            def finish(name, m, q, gain):
                z, _, places = norm_source(name)
                dve.wait_ge(m_free, m + 1)
                if not (isinstance(q, int) and q == 0):
                    dve.wait_ge(qk_rdy, q)
                dve.reciprocal(rinv[:, :], sd[:, 0:NT]).then_inc(rinv_rdy, 1)
                dve.wait_ge(rinv_rdy, q + 1)
                for dst, cols, rows in places:
                    ins = dve.scalar_tensor_tensor(dst, z[rows, cols], qk_cols[rows, gain:gain + 1], rinv[rows, cols], ALU.mult, ALU.mult)
                ins.then_inc(qk_rdy, 1)

            def set_inverses(m, b, keys, pairs):
                dve.wait_ge(m_free, m + 1)
                c0, c1 = 4 * pairs[0], 4 * pairs[-1] + 4
                dve.reciprocal(q_scale[:, c0:c1], sd[:, NT + c0:NT + c1])
                c0, c1 = 8 + 2 * pairs[0], 8 + 2 * pairs[-1] + 2
                dve.reciprocal(q_scale[0:T_S, c0:c1], sd[0:T_S, NT + c0:NT + c1]).then_inc(scale_rdy, 1)
                if keys:
                    dve.reciprocal(rinv[:, :], sd[:, 0:NT]).then_inc(kinv_rdy, 1)
                    dve.wait_ge(kinv_rdy, b + 1)
                    if not (isinstance(b, int) and b == 0):
                        dve.wait_ge(qk_done, b * 6 - 3)
                    z, _, places = norm_source("kc")
                    for dst, cols, rows in places:
                        ins = dve.scalar_tensor_tensor(dst, z[rows, cols], qk_cols[rows, 5:6], rinv[rows, cols], ALU.mult, ALU.mult)
                    ins.then_inc(qk_rdy, 1)

            def smax(kind, body, u):
                U = body * 6
                b, r, p = u % 2, u % 3, u // 3
                m, n = ROWS[r], NKEY[r]
                dve.wait_ge(qk_done, U + (u + 1))
                if not (isinstance(U, int) and U + u < 2):
                    dve.wait_ge(t_done, U + (u - 1))
                if r == 0:
                    if kind == "cb":
                        dve.wait_ge(bias_rdy, body * 2 + (p + 1))
                    else:
                        dve.wait_ge(bias_ld[p], body * 16 + 16)
                rev = [slice(None, None, -1), slice(P - 1, None, -1), slice(T_P - 1, T_P - 1 - n, -1)][r]
                s = s_buf[b][0:m, :, 0:n]
                if r == 0:
                    dve.wait_ge(scale_rdy, scale_no(kind, body, p))
                for c in range(2):
                    x = scale_col(p, r) + c
                    ins = dve.scalar_tensor_tensor(s_buf[b][0:m, c, 0:n], bank_s[b][0:m, c * n:(c + 1) * n], q_scale[0:m, x:x + 1],
                                                   bias_rev[p][0:m, c, rev], ALU.mult, ALU.add)
                ins.then_inc(s_add, 1)
                dve.wait_ge(s_add, U + (u + 1))
                if kind == "a":
                    mask = a_mask[r][0:m, :]
                    for c in range(2):
                        ins = dve.tensor_tensor(s_buf[b][0:m, c, 0:n], s_buf[b][0:m, c, 0:n], mask, ALU.add)
                    ins.then_inc(masked, 1)
                    dve.wait_ge(masked, body * 6 + (u - 29))
                sink = kind == "cb" and p == 1
                red = dve.tensor_reduce(nmax[b][0:m, :], s, AX_X, ALU.max, negate=True)
                if not sink:
                    red.then_inc(mx_rdy, 1)
                else:
                    c0 = body * 6 + 2 * r
                    ns = neg_sinks[0:m, :, body]
                    red.then_inc(mx_raw, 1)
                    dve.wait_ge(mx_raw, c0 + 1)
                    dve.tensor_tensor(nmax[b][0:m, :], nmax[b][0:m, :], ns, ALU.min).then_inc(mx_raw, 1)
                    dve.wait_ge(mx_raw, c0 + 2)
                    dve.tensor_tensor(snk[b][0:m, :], nmax[b][0:m, :], ns, ALU.subtract).then_inc(mx_rdy, 1)

            def inverse(kind, body, u):
                b, r, p = u % 2, u % 3, u // 3
                m = ROWS[r]
                dve.wait_ge(e_rdy, body * 6 + (u + 1))
                if kind == "cb" and p == 1:
                    dve.tensor_tensor(esum[b][0:m, :], esum[b][0:m, :], esnk[b][0:m, :], ALU.add).then_inc(sum_sunk, 1)
                    dve.wait_ge(sum_sunk, body * 3 + (r + 1))
                dve.reciprocal(einv[b][0:m, :], esum[b][0:m, :]).then_inc(r_rdy, 1)
                dve.wait_ge(r_rdy, body * 6 + (u + 1))
                n = NKEY[r]
                for c in range(2):
                    ins = dve.tensor_scalar(s_buf[b][0:m, c, 0:n], s_buf[b][0:m, c, 0:n], einv[b][0:m, c:c + 1], None, ALU.mult)
                ins.then_inc(p_rdy, 1)

            def out_lo(body, p, tile):
                dve.wait_ge(ohi_rdy, body * 2 + (p + 1))
                dve.tensor_tensor(o_lo[:, tile, :], bank_o[:, 0:NT], o_hi[:, tile, :].bitcast(F32), ALU.subtract).then_inc(olo_rdy, 1)

            def attention(body, kind, split_half, reads, tiles, sums):
                split_half(0)
                for k in range(8):
                    if k < 6:
                        smax(kind, body, k)
                    if k == 6:
                        out_lo(body, 0, tiles[0])
                    if k == 7 and 7 in sums:
                        set_inverses(*sums[7])
                    if k in reads:
                        reads[k]()
                    if k < 7:
                        split_half(k + 1)
                    if k < 6:
                        inverse(kind, body, k)
                    if k in sums and k < 7:
                        set_inverses(*sums[k])
                out_lo(body, 1, tiles[1])

            def prep_items(step):
                for it in PREP_ITEMS[step]:
                    if it[0] == "n":
                        gain = {"ka0": 1, "ka1": 1, "kb": 3}[it[1]]
                        finish(it[1], misc_no[it], norm_no[it], gain)
                    elif it[0] == "s":
                        set_inverses(misc_no[it], 0, True, (0, 1))
                    elif it[0] == "i":
                        u = it[1]
                        r, t = idx_units[u]
                        m, n = ROWS[r], NKEY[r]
                        dve.wait_ge(irelu, u + 1)
                        if u == 0:
                            dve.wait_ge(m_free, misc_no[("w",)] + 1)
                        for c in range(2):
                            w = w_tok[0:m, [1, 0, 2][r], 2 * t + c:2 * t + c + 1]
                            acc = idx_acc[r][0:m, :]
                            if t == 0 and c == 0:
                                ins = dve.tensor_scalar(acc, s_buf[u % 2][0:m, c, 0:n], w, None, ALU.mult)
                            else:
                                dve.wait_ge(iacc, 2 * u + c)
                                ins = dve.scalar_tensor_tensor(acc, s_buf[u % 2][0:m, c, 0:n], w, acc, ALU.mult, ALU.add)
                            ins.then_inc(iacc, 1)
                    elif it[0] == "t":
                        r = it[1]
                        m, n = ROWS[r], NKEY[r]
                        acc = idx_acc[r][0:m, :]
                        dve.wait_ge(iacc, 8 * (r + 1))
                        link(dve.tensor_scalar(acc, acc, IDX_SCALE, None, ALU.mult))
                        if r < 2:
                            link(dve.memset(idx_acc[r][0:CHUNK, n - CHUNK:n], NEG))
                        for _ in range((K_P if r < 2 else K_S) // 8):
                            link(dve.max(top8[0:m, :], acc))
                            link(dve.match_replace(acc, top8[0:m, :], acc, TAKEN))
                        dve.tensor_scalar(a_mask[r][0:m, :], acc, TAKEN / 2, NEG, ALU.is_gt, ALU.mult).then_inc(mask_rdy, 1)

            for tile, value in ((sumsq[:, :], 0.0), (mean_d[:, :], 1.0 / D), (eps[:, :], EPS), (mean_hd[:, :], 0.0),
                                (mean_hd[0:HD, 0:HD], 1.0 / HD), (mean_hd2[:, :], 0.0), (mean_hd2[0:HD, 0:1], 1.0 / HD),
                                (mean_hd2[HD:P, 1:2], 1.0 / HD)):
                link(dve.memset(tile, value))
            dve.wait_ge(consts, 2)
            dve.memset(mean_hd[HD:P, HD:P], 1.0 / HD).then_inc(consts, 1)
            split((phases[0], 0, 0))
            n = 0

            def start_copy(dst, src_cols, rows=P):
                nonlocal n
                dve.wait_ge(start_tr, n + 1)
                dve.tensor_copy(dst, bank_t[n % 2][0:rows, src_cols]).then_inc(start_cp, 1)
                n += 1
            dve.wait_ge(start_tr, 1)
            dve.tensor_copy(g_cols[:, :], bank_t[0][:, 0:3 * DT])
            dve.tensor_copy(qk_cols[:, :], bank_t[0][:, 3 * DT:3 * DT + 6]).then_inc(start_cp, 1)
            n = 1
            for j in range(DT):
                start_copy(xT[:, j, :], slice(0, NT))
                dve.wait_ge(start_cp, n)
                h_tile(0, j)
            start_copy(vec_t5[:, :], slice(0, VEC), H_A + H_B)
            start_copy(vec_c[:, :], slice(0, VEC), H_C)
            for c in range(2):
                link(dve.memset(kt_i[c][(1 - c) * HD:(2 - c) * HD, :], 0.0))
            for _, dst in CACHE_TILES:
                if dst is None:
                    dve.wait_ge(start_tr, n + 1)
                    dve.tensor_copy(kt_i[0][0:HD, T_P:T_P + PAST], bank_t[n % 2][0:HD, 0:P])
                    dve.tensor_copy(kt_i[1][HD:P, T_P:T_P + PAST], bank_t[n % 2][HD:P, 0:P]).then_inc(start_cp, 1)
                    n += 1
                else:
                    start_copy(dst, slice(0, P))
            dve.wait_ge(small_in, 16 * 7)
            link(dve.tensor_scalar(neg_sinks[:, :, :].rearrange("p a b -> p (a b)"), sink_rows[:, :, :].rearrange("p a b -> p (a b)"),
                                   -1.0, None, ALU.mult))

            for ph in phases:
                if ph.name == "up":
                    F0 = sum(p.more["size"] for p in phases[:phases.index(ph)] if p.name == "up")

                    def body(j, ph=ph, F0=F0):
                        F = j + F0
                        n = strip_no(ph, j, 0)
                        later = not (isinstance(F, int) and F == 0)
                        split(following(ph, j, 0))
                        if ph.more["first"] and isinstance(j, int) and j == 0:
                            x_norm(2 * ph.more["ffn"], ph.n0)
                        if later:
                            dve.wait_ge(sig_rdy, F)
                        read(n, 0, g_act[:, :]).then_inc(evac, 1)
                        split(following(ph, j, 1))
                        if later:
                            dve.wait_ge(gu_rdy, F)
                        read(n + 1, 1, u_act[:, :]).then_inc(evac, 1)
                        dve.wait_ge(evac, n + 2)
                        dve.wait_ge(sig_rdy, F + 1)
                        if later:
                            dve.wait_ge(gul_rdy, F)
                            dve.wait_ge(guh_rdy, F)
                        dve.tensor_tensor(gu[:, :], g_sig[:, :], u_act[:, :], ALU.mult).then_inc(gu_rdy, 1)
                        dve.wait_ge(gu_rdy, F + 1)
                        dve.wait_ge(guh_rdy, F + 1)
                        dve.tensor_tensor(gu_lo[:, j, :], gu[:, :], gu_hi[:, j, :].bitcast(F32), ALU.subtract).then_inc(gul_rdy, 1)
                    bodies(dve, ph, body, peel_first=ph.more["first"])
                elif ph.name in ("down", "wo"):
                    index = 1 if ph.name == "down" else 2
                    factor = 0.5 if ph.name == "down" else 1.0
                    h_after = ph.name == "wo" or (ph.more["last"] and ph.more["ffn"] == 0)
                    done = 1 if ph.name == "down" and ph.more["ffn"] == 0 else 2 if ph.name == "wo" else 3
                    dve.wait_ge(hlo_rdy, DT * done)
                    if h_after:
                        dve.wait_ge(m_done, [0, 1, 2][index])
                        link(dve.memset(sumsq[:, :], 0.0))

                    def body(j, ph=ph, index=index, factor=factor, h_after=h_after):
                        for s in range(2):
                            n = strip_no(ph, j, s)
                            split(following(ph, j, s))
                            if ph.name == "wo" and isinstance(j, int) and j == 0 and s == 0:
                                attend_tail()
                            dve.wait_ge(used, n + 1)
                            dve.wait_ge(evac, n)
                            d = j * 2 + s
                            dve.scalar_tensor_tensor(xT[:, d, :], bank_w[s][:, 0:NT], factor, xT[:, d, :], ALU.mult, ALU.add)\
                               .then_inc(evac, 1)
                            if h_after:
                                dve.wait_ge(evac, n + 1)
                                h_tile(index, d)

                    def attend_tail():
                        attention(7, "a", lambda k: None, {}, (2, 5), {1: (MISC_END - 1, 7, False, (1,))})
                    bodies(dve, ph, body, peel_first=ph.name == "wo")
                elif ph.name == "prep":
                    def body(j, ph=ph):
                        n = strip_no(ph, j, 0)
                        split(following(ph, j, 0))
                        if isinstance(j, int) and j == 0:
                            x_norm(1, ph.n0)
                            for s in range(2):
                                for c in range(2):
                                    link(dve.memset(q_n[s][c][(1 - c) * HD:(2 - c) * HD, :], 0.0))
                        read(n, 0, z_prep[:, j * 2, :]).then_inc(evac, 1)
                        split(following(ph, j, 1))
                        read(n + 1, 1, z_prep[:, j * 2 + 1, :]).then_inc(evac, 1)
                    body(0)
                    with dve.Fori(1, 4) as j:
                        body(j)
                    n = ph.n0 + 8
                    split(following(ph, 4, 0))
                    for c in range(2):
                        part = slice(c * HD, (c + 1) * HD)
                        read(n, 0, kt_i[c][part, 0:T_P], rows=part, cols=slice(0, T_P))
                        ins = read(n, 0, kt_i[c][part, T_P + PAST:KEYS], rows=part, cols=slice(T_P, NT))
                    ins.then_inc(evac, 1)
                    dve.wait_ge(evac, n + 1)
                    prep_items(8)
                    split(following(ph, 4, 1))
                    read(n + 1, 1, zw[:, :], rows=slice(0, H_IDX)).then_inc(evac, 1)
                    prep_items(9)
                    split(following(ph, 5, 0))
                    read(n + 2, 0, z_prep[:, 8, :]).then_inc(evac, 1)
                    prep_items(10)
                    split(following(ph, 5, 1))
                    read(n + 3, 1, z_prep[:, 9, :]).then_inc(evac, 1)
                    prep_items(11)
                elif ph.name == "cb":
                    zs = [z_k, z_q[0], z_q[1], z_v]
                    for t in range(4):
                        split(following(ph, t // 2, t % 2))
                        read(ph.n0 + t, t % 2, zs[t][:, :]).then_inc(evac, 1)
                        dve.wait_ge(evac, ph.n0 + t + 1)
                        prep_items(12 + t)

                    def body(i, ph=ph):
                        n = i * 4 + ph.n0
                        m = i * MISC_CB + (MISC_CB0 - MISC_CB)
                        order = [(ph, i * 2, 1), (ph, i * 2 + 1, 0), (ph, i * 2 + 1, 1),
                                 (ph, i * 2 + 2, 0) if not isinstance(i, int) or i < 4 else (ph.next, 0, 0)]

                        def whole(t):
                            if t == 0:
                                dve.wait_ge(qk_rdy, i + KEY_NORMS)
                            elif t < 3:
                                dve.wait_ge(qn_rdy, i * 2 + (t - 2))
                            else:
                                dve.wait_ge(m_done, m + 1)
                            read(n + t, t % 2, zs[t][:, :]).then_inc(evac, 1)
                        attention(i - 1, "cb", lambda k: split(order[k // 2], (k % 2,)),
                                  {2 * t + 1: (lambda t=t: whole(t)) for t in range(4)},
                                  (i + (PAIR_TILE["c"] - 1), i + (PAIR_TILE["b"] - 1)), {7: (m + 2, i, True, (0, 1))})
                    body(1)
                    with dve.Fori(2, 4) as i:
                        body(i)
                    body(4)
                elif ph.name == "a":
                    dve.wait_ge(mask_rdy, 3)

                    def body(i, ph=ph):
                        n = i * 2 + ph.n0
                        order = [(ph, i, 1), following(ph, i, 1)]
                        split_half = lambda k: split(order[k // 4], (k // 2 % 2,)) if k % 2 == 0 else None

                        def whole(t):
                            dve.wait_ge(qn_rdy, i * 2 + (9 + t))
                            read(n + t, t, z_q[t][:, :]).then_inc(evac, 1)
                        reads = {3: lambda: whole(0), 7: lambda: whole(1)}
                        if i == 0:
                            attention(4, "cb", split_half, reads, (PAIR_TILE["c"] + 4, PAIR_TILE["b"] + 4),
                                      {7: (MISC_A0 + 2, 5, False, (0,))})
                        else:
                            m = i * 2 + (MISC_A1 - 2)
                            attention(i + 4, "a", split_half, reads, (i - 1, i + 2),
                                      {1: (m, i + 4, False, (1,)), 7: (m + 1, i + 5, False, (0,))})
                    body(0), body(1), body(2)
            for k in range(DT):
                dve.wait_ge(y_tr, k + 1)
                if k >= 2:
                    dve.wait_ge(y_out[k % 2], 32 * (k // 2))
                dve.tensor_copy(y_rows[:, k % 2, 0:2, :], bank_t[k % 2][:, 0:2 * P].rearrange("p (t c) -> p t c", t=2))
                dve.tensor_copy(y_rows[0:T_S, k % 2, 2, :], bank_t[k % 2][0:T_S, 2 * P:3 * P]).then_inc(y_cp, 1)

        @block.gpsimd
        def _(pool):
            pool.memset(ident[:, :], 0.0).then_inc(pool_built, 1)
            pool.wait_ge(pool_built, 1)
            pool.memset(flip[:, :], 0.0).then_inc(pool_built, 1)
            pool.wait_ge(pool_built, 2)
            pool.affine_select(out=ident[:, :], in_=ident[:, :], compare_op=ALU.not_equal, fill=1.0, base=0,
                               pattern=[[-1, P]], channel_multiplier=1).then_inc(consts, 1)
            pool.wait_ge(consts, 1)
            pool.affine_select(out=flip[:, :], in_=flip[:, :], compare_op=ALU.not_equal, fill=1.0, base=1 - P,
                               pattern=[[1, P]], channel_multiplier=1).then_inc(consts, 1)
            pool.wait_ge(consts, 2)

            def settled():
                pool.sem_inc(pool_passed, 1)

            for src, dst in ((cbk, sbk), (cbv, sbv), (cck, sck), (ccv, scv)):
                pool.dma_start(dst[0, 0, 0:P - T_S], src[0, 0, T_S:P]).then_inc(misc_out, 16)
            pool.wait_ge(start_cp, 1 + DT + 2)
            pool.dma_start(vec_dram[0:H_A + H_B, :], vec_t5[:, :]).then_inc(vec_out, 16)
            pool.dma_start(vec_dram[H_A + H_B:H_A + H_B + H_C, :], vec_c[:, :]).then_inc(vec_out, 16)
            pool.wait_ge(vec_out, 32)

            def windows(first, step, count, apart):
                return bass.AP(vec_dram.tensor, first * VEC, [[step * VEC, count], [1, P], [apart * VEC, 2], [1, T_P]])
            win = {"c": windows(H_A + H_B, 2, 5, 1), "b": windows(H_A, 1, 5, 5),
                   "a0": windows(0, 1, 3, 3), "a1": windows(6, 1, 3, 3)}

            def load_bias(kind, at, p, body):
                if not (isinstance(body, int) and body == 0):
                    pool.wait_ge(s_add, body * 6 + (3 * p - 3))
                    settled()
                pool.dma_start(bias_rev[p][:, :, :], win[kind][at]).then_inc(bias_ld[p], 16)
                if kind in "bc":
                    pool.wait_ge(bias_ld[p], body * 16 + 16)
                    settled()
                    if kind == "b":
                        pool.memset(bias_rev[p][CHUNK:P, :, T_P - CHUNK:T_P], NEG).then_inc(window_msk, 1)
                        pool.wait_ge(window_msk, body + 1)
                        settled()
                    pool.memset(bias_rev[p][0:CHUNK, :, 0:CHUNK], NEG).then_inc(bias_rdy, 1)
                    pool.wait_ge(bias_rdy, body * 2 + (p + 1))
                    settled()

            def place_c_cache(i):
                pool.tensor_copy(kt_c[:, T_P:T_P + PAST], kc_cache[:, i, :]).then_inc(kc_rdy, 1)
                pool.wait_ge(kc_rdy, i + 1)
                settled()
                pool.dma_start(v_c[:, 2, :], ccv_t[:, bass.ds(i * P, P)]).then_inc(vc_ld, 16)

            ccv_t = ccv[0, 0].rearrange("t h d -> t (h d)")

            def place_q(b, p, n_done, number, gain):
                z, c0 = z_q[p], [slice(0, HD), slice(HD, P)]
                square(z, 1 + p, n_done, number)
                if not (isinstance(b, int) and b == 0):
                    pool.wait_ge(qk_done, b * 6 + (3 * p - 3))
                    settled()
                for c, done in enumerate((qn_half, qn_rdy)):
                    pool.tensor_scalar(q_n[p][c][c0[c], :], z[c0[c], :], qk_cols[c0[c], gain:gain + 1], ATTN_SCALE,
                                       ALU.mult, ALU.mult).then_inc(done, 1)
                    pool.wait_ge(done, b * 2 + (p + 1))
                    settled()

            def square(z, which, n_done, number):
                pool.wait_ge(evac, n_done)
                settled()
                pool.tensor_tensor(sq_set[which], z[:, :], z[:, :], ALU.mult).then_inc(set_sq, 1)
                pool.wait_ge(set_sq, number)
                settled()

            def store_v(m, v, cols, prompt, sample, first):
                pool.wait_ge(m_free, m + 1)
                settled()
                pool.dma_start(prompt.rearrange("(t p) c -> p t c", p=P), v[:, first:2, cols]).then_inc(v_out, 16)
                pool.dma_start(sample, v[0:T_S, 3, cols]).then_inc(v_out, 16)

            def store_k(m, prompt, sample, first, width):
                pool.wait_ge(m_free, m + 1)
                settled()
                pool.dma_start(prompt.rearrange("(t p) c -> p t c", p=P), k_rows[:, first:2, 0:width]).then_inc(k_out, 16)
                pool.dma_start(sample, k_rows[0:T_S, 2, 0:width]).then_inc(k_out, 16)

            flat = lambda x: x[0, 0].rearrange("t h d -> t (h d)")

            def store_c(m, i):
                cols = bass.ds(i * P, P)
                store_v(m, v_c, slice(0, P), flat(pcv)[:, cols], flat(scv)[P - T_S:P, cols], 0)
                store_k(m + 1, flat(pck)[:, cols], flat(sck)[P - T_S:P, cols], 0, P)

            prep = next(p for p in phases if p.name == "prep")
            pool.wait_ge(evac, prep.n0 + 1)
            load_bias("c", 0, 0, 0)
            load_bias("b", 0, 1, 0)
            place_c_cache(0)
            cb = next(p for p in phases if p.name == "cb")
            a_ph = next(p for p in phases if p.name == "a")
            for step in range(8, 16):
                if step == 13:
                    square(z_k, 0, cb.n0 + 1, set_squares(0, 0))
                if step == 14:
                    place_q(0, 0, cb.n0 + 2, set_squares(0, 1), 4)
                if step == 15:
                    place_q(0, 1, cb.n0 + 3, set_squares(0, 2), 2)
                for it in PREP_ITEMS[step]:
                    if it[0] == "v":
                        store_v(misc_no[it], *v_place(it[1]))
                    if it[0] == "k":
                        store_k(misc_no[it], *k_place(it[1]))

            def attend(body, nxt, at, turn, project):
                U, b = body * 6, body + 1
                if project == "cb":
                    square(z_k, 0, b * 4 + (cb.n0 + 1), set_squares(b, 0))
                if turn is not None:
                    store_c(turn, body)
                if nxt:
                    load_bias(nxt[0], at, 0, b)
                if project == "cb":
                    place_q(b, 0, b * 4 + (cb.n0 + 2), set_squares(b, 1), 4)
                    place_q(b, 1, b * 4 + (cb.n0 + 3), set_squares(b, 2), 2)
                elif project == "a":
                    place_q(b, 0, b * 2 + (a_ph.n0 - 10 + 1), a_squares(b, 0), 0)
                if nxt and nxt[0] == "c":
                    pool.wait_ge(pv_done, U + 3)
                    settled()
                    place_c_cache(at)
                if nxt:
                    load_bias(nxt[1], at, 1, b)
                if project == "a":
                    place_q(b, 1, b * 2 + (a_ph.n0 - 10 + 2), a_squares(b, 1), 0)

            attend(0, ("c", "b"), 1, MISC_CB0, "cb")
            with pool.Fori(1, 4) as i:
                attend(i, ("c", "b"), i + 1, i * MISC_CB + MISC_CB0, "cb")
            attend(4, ("a0", "a1"), 0, MISC_A0, "a")
            with pool.Fori(5, 7) as i:
                attend(i, ("a0", "a1"), i - 4, None, "a")
            pool.wait_ge(misc_out, 64)
            pool.wait_ge(v_out, 32 * (VOUT_PREP + 5))
            pool.wait_ge(k_out, 32 * (KOUT_PREP + 5))


_INS = ["x_prompt", "x_sample", "cache_a_k", "cache_a_v", "cache_a_kidx", "cache_b_k", "cache_b_v", "cache_c_k", "cache_c_v",
        "w_in", "w_out", "qk_norm", "sinks", "c_rel_bias", "t5_rel_bias", "norm_gains", "w_ffn_gate", "w_ffn_up", "w_ffn_down"]


def kernel(**inputs):
    import concourse.bacc as bacc
    from concourse.bass_utils import run_bass_kernel_spmd

    nc = bacc.Bacc("TRN2", target_bir_lowering=False, num_devices=1)
    arrays, args = {}, []

    def add_input(name, a):
        a = np.ascontiguousarray(a)
        arrays[f"in_{name}"] = a
        args.append(nc.dram_tensor(f"in_{name}", a.shape, mybir.dt.from_np(a.dtype), kind="ExternalInput").ap())

    for name in _INS:
        add_input(name, inputs[name])
    add_input("t5_onehot", t5_onehot())
    shape = {name: tuple(inputs[name].shape) for name in _INS}
    depth, batch, past = shape["cache_a_k"][:3]
    seq, dec = shape["x_prompt"][1], shape["x_sample"][1]
    window = shape["cache_b_k"][2]
    outs = [shape["x_prompt"], shape["x_sample"], (depth, batch, seq, KV_A, HD), (depth, batch, seq, KV_A, HD),
            (depth, batch, seq, HD), (depth, batch, window, KV_B, HD), (depth, batch, window, KV_B, HD),
            (depth, batch, seq, H_C, HD), (depth, batch, seq, H_C, HD),
            (depth, batch, dec, KV_A, HD), (depth, batch, dec, KV_A, HD), (depth, batch, dec, HD),
            shape["cache_b_k"], shape["cache_b_v"], shape["cache_c_k"], shape["cache_c_v"]]
    for i, s in enumerate(outs):
        args.append(nc.dram_tensor(f"out_{i}", s, F32, kind="ExternalOutput").ap())
    encoder_step(nc, *args)
    r = run_bass_kernel_spmd(nc, [arrays], core_ids=[0])
    return tuple(r.results[0][f"out_{i}"] for i in range(len(outs)))
```

```python
from contextlib import ExitStack

import numpy as np

import concourse.bass as bass
from concourse import mybir

ALU = mybir.AluOpType
ACT = mybir.ActivationFunctionType
AX_X = mybir.AxisListType.X
F32 = mybir.dt.float32
F32R = mybir.dt.float32r

P = 128
HD = 64
CHUNK = 64
H_A, KV_A, H_IDX, H_B, KV_B, H_C = 12, 4, 8, 10, 2, 10
T5_BUCKETS, T5_MAX_DIST, C_MAX_REL = 32, 1024, 256
EPS = 1e-6
NEG = -1e30
TAKEN = -3e38
ATTN_SCALE = HD ** -0.5
IDX_SCALE = (H_IDX * HD) ** -0.5
VEC = 3 * P


def t5_onehot():
    nb = T5_BUCKETS // 2
    exact = nb // 2
    rel = 127 - np.arange(VEC)
    n = np.abs(rel)
    nf = np.maximum(n, exact).astype(np.float32)
    large = exact + (np.log(nf / np.float32(exact)) / np.float32(np.log(T5_MAX_DIST / exact))
                     * np.float32(nb - exact)).astype(np.int32)
    bucket = np.where(rel > 0, nb, 0) + np.where(n < exact, n, np.minimum(large, nb - 1))
    return (np.arange(T5_BUCKETS)[:, None] == bucket[None, :]).astype(np.float32)


class Phase:

    def __init__(self, name, strips, tiles, n0, ld0, **more):
        self.name, self.strips, self.tiles, self.n0, self.ld0 = name, strips, tiles, n0, ld0
        self.more = more


def plan_phases(d_tiles, f_tiles):
    phases, n, ld = [], 0, 0
    thirds = [f_tiles - 2 * (f_tiles // 3), f_tiles // 3, f_tiles // 3]

    def add(name, strips, tiles, **more):
        nonlocal n, ld
        phases.append(Phase(name, strips, tiles, n, 0 if name == "wo" else ld, **more))
        n += strips
        ld += 0 if name == "wo" else strips // 2

    for ffn in range(2):
        f0 = 0
        for t, size in enumerate(thirds):
            add("up", 2 * size, d_tiles, ffn=ffn, f0=f0, size=size, first=t == 0)
            add("down", d_tiles, size, ffn=ffn, f0=f0, size=size, last=t == 2)
            f0 += size
        if ffn == 0:
            add("prep", 12, d_tiles)
            add("cb", 20, d_tiles)
            add("a", 6, d_tiles)
            add("wo", d_tiles, 16)
    for a, b in zip(phases, phases[1:]):
        a.next = b
    phases[-1].next = None
    return phases


def encoder_step(nc, xp, xs, cak, cav, caki, cbk, cbv, cck, ccv, w_in, w_out, qk_norm, sinks, c_bias, t5_bias,
                 gains, w_gate, w_up, w_down, onehot,
                 yp, ys, pak, pav, paki, pbk, pbv, pck, pcv, sak, sav, saki, sbk, sbv, sck, scv):
    T_P, D = xp.shape[1:]
    T_S = xs.shape[1]
    PAST = cak.shape[2]
    D_IN = w_in.shape[2]
    D_FF = w_gate.shape[3]
    NT = T_P + T_S
    DT, FT = D // P, D_FF // P
    assert T_P == 2 * P and T_S == 32 and PAST == P and w_out.shape[1] == 16 * P
    assert cbk.shape[2] == P and cck.shape[2] == P
    K_P, K_S = T_P // 4, (PAST + T_S) // 4
    phases = plan_phases(DT, FT)
    thirds = [p.more["size"] for p in phases if p.name == "up"][:3]

    o_qa = 0
    o_ka = o_qa + H_A * HD
    o_va = o_ka + KV_A * HD
    o_qi = o_va + KV_A * HD
    o_ki = o_qi + H_IDX * HD
    o_wi = o_ki + HD
    o_qb = o_wi + H_IDX
    o_kb = o_qb + H_B * HD
    o_vb = o_kb + KV_B * HD
    o_qc = o_vb + KV_B * HD
    o_kc = o_qc + H_C * HD
    o_vc = o_kc + H_C * HD
    assert o_vc + H_C * HD == D_IN

    ctx = ExitStack()
    with ctx:
        def sb(name, shape, dt=F32, scope=ctx):
            return scope.enter_context(nc.sbuf_tensor(name, shape, dt))

        def sem(name):
            return ctx.enter_context(nc.semaphore(name))

        xT = sb("xT", [P, DT, NT])
        h_hi = sb("h_hi", [P, DT, NT], F32R)
        h_lo = sb("h_lo", [P, DT, NT], F32R)
        raw = [sb(f"raw{s}", [P, 16, P]) for s in range(2)]
        w_hi = [sb(f"w_hi{s}", [P, 16, P], F32R) for s in range(2)]
        w_lo = [sb(f"w_lo{s}", [P, 16, P], F32R) for s in range(2)]
        with ExitStack() as ffn_scope:
            gu_hi = sb("gu_hi", [P, thirds[0], NT], F32R, ffn_scope)
            gu_lo = sb("gu_lo", [P, thirds[0], NT], F32R, ffn_scope)
        o_hi = sb("o_hi", [P, 16, NT], F32R)
        o_lo = sb("o_lo", [P, 16, NT], F32R)
        ident = sb("ident", [P, P])
        mean_d = sb("mean_d", [P, P])
        mean_hd = sb("mean_hd", [P, P])
        mean_hd2 = sb("mean_hd2", [P, 2])
        eps = sb("eps", [P, 1])
        g_cols = sb("g_cols", [P, 3 * DT])
        qk_cols = sb("qk_cols", [P, 6])
        sink_rows = sb("sink_rows", [P, 2, 5])
        neg_sinks = sb("neg_sinks", [P, 2, 5])
        rstd = sb("rstd", [P, NT])
        sumsq = sb("sumsq", [P, NT])
        sqx = sb("sqx", [P, NT])
        sd_x = sb("sd_x", [P, NT])
        KEYS = T_P + PAST + T_S
        kt_a = sb("kt_a", [P, 2, KEYS])
        kt_b = sb("kt_b", [P, KEYS])
        kt_i = sb("kt_i", [P, KEYS])
        kt_c = sb("kt_c", [P, KEYS])
        kc_cache = sb("kc_cache", [P, 5, P])
        v_a = sb("v_a", [P, 4, 2 * P])
        v_b = sb("v_b", [P, 4, P])
        with ExitStack() as scope:
            xrow = sb("xrow", [P, 3, D], F32, scope)
        with ExitStack() as scope:
            g_act = sb("g_act", [P, NT], F32, scope)
            g_sig = sb("g_sig", [P, NT], F32, scope)
            u_act = sb("u_act", [P, NT], F32, scope)
            gu = sb("gu", [P, NT], F32, scope)
            y_t = [sb(f"y_t{s}", [P, NT], F32, scope) for s in range(2)]
            y_rows = sb("y_rows", [P, 2, 3, P], F32, scope)
        z_prep = sb("z_prep", [P, 10, NT])
        z_q = [sb(f"z_q{s}", [P, NT]) for s in range(2)]
        z_k = sb("z_k", [P, NT])
        z_v = sb("z_v", [P, NT])
        zw = z_v[0:H_IDX, :]
        q_n = [sb(f"q_n{s}", [P, NT]) for s in range(2)]
        sq = sb("sq", [P, NT])
        sq_set = [z_prep[:, 4 + i, :] for i in range(3)]
        sd = sb("sd", [P, NT + 12])
        rinv = sb("rinv", [P, NT])
        v_c = sb("v_c", [P, 4, P])
        k_rows = sb("k_rows", [P, 3, P])
        with ExitStack() as scope:
            flip = sb("flip", [P, P], F32, scope)
            gain_rows = sb("gain_rows", [3 * DT, P], F32, scope)
            qk_rows = sb("qk_rows", [6, P], F32, scope)
            t5_rows = sb("t5_rows", [T5_BUCKETS, H_A + H_B], F32, scope)
            hot = sb("hot", [T5_BUCKETS, VEC], F32, scope)
            c_rows = sb("c_rows", [P, 3, H_C], F32, scope)
            cache_rows = sb("cache_rows", [P, 9, P], F32, scope)
            vec_t5 = sb("vec_t5", [H_A + H_B, VEC], F32, scope)
            vec_c = sb("vec_c", [H_C, VEC], F32, scope)
        s_buf = [sb(f"s_buf{s}", [P, 2, T_P]) for s in range(2)]
        p_t = [sb(f"p_t{s}", [P, 4, P]) for s in range(2)]
        bias_rev = [sb(f"bias_rev{s}", [P, 2, T_P]) for s in range(2)]
        idx_acc = [sb(f"idx_acc{r}", [P, n]) for r, n in enumerate((2 * P, P, PAST + T_S))]
        a_mask = [sb(f"a_mask{r}", [P, n]) for r, n in enumerate((2 * P, P, PAST + T_S))]
        nmax = [sb(f"nmax{s}", [P, 2]) for s in range(2)]
        snk = [sb(f"snk{s}", [P, 2]) for s in range(2)]
        esnk = [sb(f"esnk{s}", [P, 2]) for s in range(2)]
        esum = [sb(f"esum{s}", [P, 2]) for s in range(2)]
        einv = [sb(f"einv{s}", [P, 2]) for s in range(2)]
        q_scale = sb("q_scale", [P, 12])
        w_tok = sb("w_tok", [P, 3, H_IDX])
        top8 = sb("top8", [P, 8])
        CACHE_TILES = [(cache_rows[:, 0, :], kt_a[:, 0, T_P:T_P + PAST]), (cache_rows[:, 1, :], kt_a[:, 1, T_P:T_P + PAST]),
                       (cache_rows[:, 2, :], kt_i[:, T_P:T_P + PAST]), (cache_rows[:, 3, :], kt_b[:, T_P:T_P + PAST])]
        CACHE_TILES += [(cache_rows[:, 4 + i, :], kc_cache[:, i, :]) for i in range(5)]

        psum = [ctx.enter_context(nc.psum_tensor(f"bank{b}", [P, 512], F32)) for b in range(8)]
        bank_w = psum[0:2]
        bank_s = psum[2:4]
        bank_t = psum[4:6]
        bank_o = psum[6]
        bank_m = psum[7]

        vec_dram = nc.dram_tensor("bias_vectors", (H_A + H_B + H_C, VEC), F32, kind="Internal").ap()

        ld = [sem("strip_loaded0"), sem("strip_loaded1")]
        ld_wo = [sem("wo_strip_loaded0"), sem("wo_strip_loaded1")]
        hi_rdy = sem("w_hi_ready")
        lo_rdy = sem("w_lo_ready")
        used = sem("strip_multiplied")
        evac = sem("product_read")
        part_used = sem("wo_strip_half_multiplied")
        x_in = [sem(f"x_loaded{c}") for c in range(4)]
        xs_in = sem("x_sample_loaded")
        gains_in = sem("gains_loaded")
        small_in = sem("small_inputs_loaded")
        cache_in = sem("cache_rows_loaded")
        vcache_in = sem("v_cache_loaded")
        pool_built = sem("pool_constants_cleared")
        consts = sem("constants_built")
        start_tr = sem("start_transposed")
        start_cp = sem("start_copied")
        vec_out = sem("bias_vectors_stored")
        x_sq = sem("first_x_squares_ready")
        sqx_rdy = sem("x_squares_ready")
        acc_rdy = sem("x_squares_summed")
        hhi_rdy = sem("h_hi_ready")
        hlo_rdy = sem("h_lo_ready")
        rstd_rdy = sem("x_rstd_ready")
        sig_rdy = sem("silu_ready")
        gu_rdy = sem("gated_ready")
        guh_rdy = sem("gated_hi_ready")
        gul_rdy = sem("gated_lo_ready")
        m_done = sem("misc_bank_written")
        m_free = sem("misc_bank_read")
        sq_rdy = sem("squares_ready")
        rinv_rdy = sem("inverse_norm_ready")
        qk_rdy = sem("key_tile_normalized")
        set_sq = sem("set_squares_ready")
        kinv_rdy = sem("key_inverse_norm_ready")
        scale_rdy = sem("query_scales_ready")
        qn_rdy = sem("queries_placed")
        qk_done = sem("scores_done")
        s_add = sem("scores_biased")
        mx_raw = sem("sink_max_step")
        sum_sunk = sem("sink_added")
        mx_rdy = sem("neg_max_ready")
        e_rdy = sem("exponentials_ready")
        r_rdy = sem("inverse_sums_ready")
        p_rdy = sem("probabilities_ready")
        t_done = sem("probabilities_transposed")
        c_done = sem("transposed_copied")
        pv_done = sem("unit_output_done")
        ohi_rdy = sem("output_hi_ready")
        olo_rdy = sem("output_lo_ready")
        bias_ld = [sem("bias_loaded0"), sem("bias_loaded1")]
        bias_rdy = sem("bias_ready")
        window_msk = sem("bias_window_masked")
        kc_rdy = sem("c_key_cache_placed")
        vc_ld = sem("c_value_cache_loaded")
        v_out = sem("v_rows_stored")
        k_out = sem("k_rows_stored")
        misc_out = sem("cache_tails_stored")
        iq_done = sem("index_products_done")
        irelu = sem("index_relu_done")
        iacc = sem("index_scores_summed")
        mask_rdy = sem("selection_ready")
        y_tr = sem("y_transposed")
        y_cp = sem("y_copied")
        y_out = [sem("y_stored0"), sem("y_stored1")]
        pe_passed = sem("narrow_product_begins")
        pool_passed = sem("pool_passed_wait")
        dve_link = sem("vector_step")

        block = ctx.enter_context(nc.Block())

        TOK = [slice(P, 2 * P), slice(0, P), slice(T_P, NT)]
        ROWS = [P, P, T_S]
        NKEY = [T_P, P, PAST + T_S]
        KEY0 = [0, 0, T_P]
        CONSTS = 3

        def strip_no(ph, j, s):
            return j * 2 + (ph.n0 + s)

        def half_tiles(ph, half):
            return (slice(0, 8), slice(8, ph.tiles))[half ^ (ph.name == "wo")]

        def following(ph, j, s):
            if s == 0:
                return ph, j, 1
            if isinstance(j, int) and j == ph.strips // 2 - 1:
                return (ph.next, 0, 0) if ph.next else None
            return ph, j + 1, 0

        def bodies(eng, ph, body, peel_first=False, strips=2):
            count = ph.strips // strips
            start = 1 if peel_first else 0
            if peel_first:
                body(0)
            with eng.Fori(start, count - 1) as i:
                body(i)
            body(count - 1)

        idx_units = [(r, t) for r in range(3) for t in range(4)]
        PREP_ITEMS = {
            5: [("w",), ("i", 0)],
            6: [("i", 1), ("i", 2), ("i", 3)],
            7: [("i", 4), ("i", 5), ("i", 6)],
            8: [("n", "ka0"), ("i", 7), ("i", 8), ("i", 9)],
            9: [("n", "ka1"), ("i", 10), ("i", 11), ("t", 0, 0, 2)],
            10: [("v", "va0"), ("k", "ka0"), ("t", 0, 2, 5)],
            11: [("v", "va1"), ("k", "ka1"), ("t", 0, 5, 8)],
            12: [("n", "kb"), ("v", "vb"), ("t", 1, 0, 2)],
            13: [("k", "kb"), ("t", 1, 2, 6)],
            14: [("k", "ki"), ("t", 1, 6, 8), ("t", 2, 0, 2)],
            15: [("s",)],
        }
        misc_no, norm_no, kout_no, vout_no = {}, {}, {}, {}
        at = 1 + 1
        for step in range(5, 16):
            for it in PREP_ITEMS[step]:
                if it[0] in "nvkws":
                    misc_no[it] = at
                    at += 1
                if it[0] == "n":
                    norm_no[it] = len(norm_no)
                if it[0] == "k":
                    kout_no[it] = len(kout_no)
                if it[0] == "v":
                    vout_no[it] = len(vout_no)
        KEY_NORMS = len(norm_no)
        MISC_CB, MISC_CB0 = 3, at
        MISC_A0 = MISC_CB0 + 4 * MISC_CB
        MISC_A1 = MISC_A0 + 3
        MISC_END = MISC_A1 + 2 * 2 + 1
        VOUT_PREP, KOUT_PREP = len(vout_no), len(kout_no)

        def norm_source(name):
            kt, z, g = {"ka0": (kt_a[:, 0, :], z_prep[:, 0, :], 1), "ka1": (kt_a[:, 1, :], z_prep[:, 1, :], 1),
                        "kb": (kt_b[:, :], z_prep[:, 8, :], 3), "kc": (kt_c[:, :], z_k[:, :], 5)}[name]
            return z, g, [(kt[:, 0:T_P], slice(0, T_P), slice(0, P)), (kt[:, T_P + PAST:KEYS], slice(T_P, NT), slice(0, P))]

        def scale_no(kind, b, p):
            return b + 1 if kind == "cb" else b * 2 + (p - 4)

        def set_squares(b, which):
            return b * 3 + (which + 1)

        def a_squares(b, p):
            return b * 2 + (5 + p + 1)

        def scale_col(p, r):
            return 4 * p + 2 * r if r < 2 else 8 + 2 * p

        @block.sync
        def _(sp):
            sp.dma_start(xrow[0:T_S, 2, :], xs[0]).then_inc(xs_in, 16)

            def load_x(c):
                cols = slice(c * D // 4, (c + 1) * D // 4)
                sp.dma_start(xrow[:, 0:2, cols], xp[0, :, cols].rearrange("(t p) c -> p t c", p=P)).then_inc(x_in[c], 16)

            def pieces(ph, j, s):
                half = [slice(0, 8), slice(8, ph.tiles)]
                m = ph.more
                if ph.name == "up":
                    w = (w_gate if s == 0 else w_up)[0, m["ffn"]].rearrange("(k p) n -> p k n", p=P)
                    col = bass.ds(j * P + m["f0"] * P, P)
                    return [(raw[s][:, k, :], w[:, k, col]) for k in half]
                if ph.name == "down":
                    f0, f1 = m["f0"], m["f0"] + m["size"]
                    w = w_down[0, m["ffn"], f0 * P:f1 * P].rearrange("(k p) n -> p k n", p=P)
                    col = bass.ds(j * 2 * P + s * P, P)
                    return [(raw[s][:, k, :], w[:, k, col]) for k in half]
                w = w_in[0].rearrange("(k p) n -> p k n", p=P)
                if ph.name == "prep":
                    if j < 2 or 3 <= j < 5:
                        col = (o_qi, o_ka)[j > 2] + (j * 2 - (0, 6)[j > 2] + s) * P
                        return [(raw[s][:, k, :], w[:, k, col:col + P]) for k in half]
                    if (j, s) == (2, 0):
                        return [(raw[s][:, :, c:c + HD], w[:, :, o_ki:o_ki + HD]) for c in (0, HD)]
                    if (j, s) == (2, 1):
                        return [(raw[s][:, k, 0:H_IDX], w[:, k, o_wi:o_wi + H_IDX]) for k in half]
                    col = slice(o_kb, o_kb + P) if s == 0 else slice(o_vb, o_vb + P)
                    return [(raw[s][:, k, :], w[:, k, col]) for k in half]
                raise AssertionError(ph.name)

            def w_in_cols(s, cols):
                w = w_in[0].rearrange("(k p) n -> p k n", p=P)
                if len(cols) == 1:
                    return [(raw[s][:, k, :], w[:, k, cols[0]]) for k in (slice(0, 8), slice(8, 16))]
                return [(raw[s][:, :, c * HD:(c + 1) * HD], w[:, :, cols[c]]) for c in range(2)]

            def load(ph, j, s, what=None):
                n = strip_no(ph, j, s)
                if not (isinstance(n, int) and n < 2):
                    sp.wait_ge(lo_rdy, n * 2 - 2)
                for dst, src in what or pieces(ph, j, s):
                    sp.dma_start(dst, src).then_inc(ld[s], 16)

            for ph in phases:
                if ph.name in ("up", "down"):
                    first = 1 if ph.n0 == 0 else 0
                    if first:
                        load_x(0)
                        load_x(1)
                        for half, c in zip(pieces(ph, 0, 0), (2, 3)):
                            load(ph, 0, 0, [half])
                            load_x(c)
                        load(ph, 0, 1)
                        for c in range(2):
                            sp.dma_start(qk_rows[:, c * HD:(c + 1) * HD], qk_norm[0]).then_inc(small_in, 16)
                        sp.dma_start(t5_rows[:, :], t5_bias).then_inc(small_in, 16)
                        sp.dma_start(hot[:, :], onehot).then_inc(small_in, 16)
                        sp.dma_start(c_rows[:, :, :], c_bias[0, 0:VEC].rearrange("(b p) h -> p b h", p=P)).then_inc(small_in, 16)
                        sp.dma_start(sink_rows[:, :, :].rearrange("p a b -> p (a b)"), bass.AP(sinks.tensor, 0, [[0, P], [1, H_B]])).then_inc(small_in, 16)
                        sp.dma_start(cache_rows[:, 0:2, :].rearrange("p t c -> p (t c)"), cak[0, 0].rearrange("t h d -> t (h d)")).then_inc(cache_in, 16)
                        for c in range(2):
                            sp.dma_start(cache_rows[:, 2, c * HD:(c + 1) * HD], caki[0, 0]).then_inc(cache_in, 16)
                        sp.dma_start(cache_rows[:, 3, :], cbk[0, 0].rearrange("t h d -> t (h d)")).then_inc(cache_in, 16)
                        sp.dma_start(cache_rows[:, 4:9, :].rearrange("p t c -> p (t c)"), cck[0, 0].rearrange("t h d -> t (h d)")).then_inc(cache_in, 16)
                        sp.dma_start(v_a[:, 2, :], cav[0, 0].rearrange("t h d -> t (h d)")).then_inc(vcache_in, 16)
                        sp.dma_start(v_b[:, 2, :], cbv[0, 0].rearrange("t h d -> t (h d)")).then_inc(vcache_in, 16)
                    with sp.Fori(first, ph.strips // 2) as j:
                        load(ph, j, 0)
                        load(ph, j, 1)
                elif ph.name == "prep":
                    for j in range(6):
                        load(ph, j, 0)
                        load(ph, j, 1)
                elif ph.name == "cb":
                    with sp.Fori(0, 5) as i:
                        load(ph, i * 2, 0, w_in_cols(0, [bass.ds(i * P + o_kc, P)]))
                        load(ph, i * 2, 1, w_in_cols(1, [bass.ds(i * P + o_qc, P)]))
                        load(ph, i * 2 + 1, 0, w_in_cols(0, [bass.ds(i * HD + o_qb, HD), bass.ds(i * HD + (o_qb + 5 * HD), HD)]))
                        load(ph, i * 2 + 1, 1, w_in_cols(1, [bass.ds(i * P + o_vc, P)]))
                elif ph.name == "a":
                    with sp.Fori(0, 3) as i:
                        for s in range(2):
                            c = o_qa + s * 6 * HD
                            load(ph, i, s, w_in_cols(s, [bass.ds(i * HD + c, HD), bass.ds(i * HD + (c + 3 * HD), HD)]))
                else:
                    wo = w_out[0]
                    with sp.Fori(0, ph.strips // 2) as j:
                        for s in range(2):
                            sp.wait_ge(lo_rdy, strip_no(ph, j, s) * 2 - 2)
                            col = bass.ds(j * 2 * P + s * P, P)
                            for g in range(2):
                                for c in range(2):
                                    r = (6 * g + 3 * c) * HD
                                    sp.dma_start(raw[s][c * HD:(c + 1) * HD, 3 * g:3 * g + 3, :],
                                                 wo[r:r + 3 * HD, col].rearrange("(k p) n -> p k n", p=HD)).then_inc(ld_wo[s], 16)
                            for c in range(2):
                                r = (H_A + 5 * c) * HD
                                sp.dma_start(raw[s][c * HD:(c + 1) * HD, 6:11, :],
                                             wo[r:r + 5 * HD, col].rearrange("(k p) n -> p k n", p=HD)).then_inc(ld_wo[s], 16)
                            r = (H_A + H_B) * HD
                            sp.dma_start(raw[s][:, 11:16, :],
                                         wo[r:r + 5 * P, col].rearrange("(k p) n -> p k n", p=P)).then_inc(ld_wo[s], 16)
        WO_LOADS = 7

        @block.tensor
        def _(pe):
            def products(ph, j, s, rhs, ks, n, first_k, last_k, when=None):
                for k in ks:
                    if when:
                        when(k)
                    hi, lo = rhs(k)
                    out = bank_w[s][:, 0:NT]
                    pe.matmul(out, w_hi[s][:, k, :], hi, start=(k == first_k), stop=False)
                    pe.matmul(out, w_hi[s][:, k, :], lo, start=False, stop=False)
                    mm = pe.matmul(out, w_lo[s][:, k, :], hi, start=False, stop=(k == last_k))
                return mm

            def strip(ph, j, s, rhs, when=None, part=(0, None)):
                n = strip_no(ph, j, s)
                a, b = part[0], part[1] or ph.tiles
                if a == 0 and not (isinstance(n, int) and n < 2):
                    pe.wait_ge(evac, n - 1)
                if a < 8:
                    if a == 0:
                        pe.wait_ge(lo_rdy, n * 2 + 1)
                    mm = products(ph, j, s, rhs, range(a, min(b, 8)), n, 0, ph.tiles - 1, when)
                if b > 8:
                    if a <= 8:
                        pe.wait_ge(lo_rdy, n * 2 + 2)
                    mm = products(ph, j, s, rhs, range(max(a, 8), b), n, 0, ph.tiles - 1, when)
                if b == ph.tiles:
                    mm.then_inc(used, 1)

            def h_rhs(k):
                return h_hi[:, k, :], h_lo[:, k, :]

            def gu_rhs(k):
                return gu_hi[:, k, :], gu_lo[:, k, :]

            def o_rhs(k):
                return o_hi[:, k, :], o_lo[:, k, :]

            def misc_begin(m):
                if not (isinstance(m, int) and m == 0):
                    pe.wait_ge(m_free, m)

            def x_norm(index):
                pe.wait_ge(acc_rdy, DT * (index + 1))
                misc_begin([0, 1, MISC_END][index])
                pe.matmul(bank_m[:, 0:NT], mean_d[:, :], sumsq[:, :], start=True, stop=True).then_inc(m_done, 1)

            def head_sum(m, q):
                pe.wait_ge(sq_rdy, q + 1)
                misc_begin(m)
                pe.matmul(bank_m[:, 0:NT], mean_hd[:, :], sq[:, :], start=True, stop=True).then_inc(m_done, 1)

            def set_sums(m, squares_done, keys, pairs):
                pe.wait_ge(set_sq, squares_done)
                misc_begin(m)
                if keys:
                    pe.matmul(bank_m[:, 0:NT], mean_hd[:, :], sq_set[0], start=True, stop=True)
                for p in pairs:
                    for r in range(3):
                        c = NT + scale_col(p, r)
                        mm = pe.matmul(bank_m[0:ROWS[r], c:c + 2], sq_set[1 + p][:, TOK[r]], mean_hd2[:, :], start=True, stop=True)
                mm.then_inc(m_done, 1)

            def turn_rows(m, tile, sample0):
                misc_begin(m)
                for t in range(2):
                    pe.transpose(bank_m[:, t * P:(t + 1) * P], tile[:, t * P:(t + 1) * P], ident[:, :])
                pe.transpose(bank_m[0:T_S, 2 * P:3 * P], tile[:, sample0:sample0 + T_S], ident[:, :]).then_inc(m_done, 1)

            def settled():
                pe.sem_inc(pe_passed, 1)

            def scores(U, r, b, q, kt):
                if not (isinstance(U, int) and U < 1):
                    pe.wait_ge(s_add, U)
                if r == 2:
                    settled()
                for c in range(2):
                    half = slice(c * HD, (c + 1) * HD)
                    mm = pe.matmul(bank_s[c][0:ROWS[r], 0:NKEY[r]], q[half, TOK[r]],
                                   kt[half, KEY0[r]:KEY0[r] + NKEY[r]], start=True, stop=True)
                mm.then_inc(qk_done, 1)

            def turn_p(U, r, b):
                pe.wait_ge(p_rdy, U + 1)
                if not (isinstance(U, int) and U < 2):
                    pe.wait_ge(c_done, U - 1)
                m = ROWS[r]
                if r == 2:
                    settled()
                for c in range(2):
                    if r < 2:
                        for kc in range(NKEY[r] // P):
                            o = (c * (NKEY[r] // P) + kc) * P
                            mm = pe.transpose(bank_t[b][:, o:o + P], s_buf[b][:, c, kc * P:(kc + 1) * P], ident[:, :])
                    else:
                        pe.transpose(bank_t[b][:, c * P:c * P + m], s_buf[b][0:m, c, 0:P], ident[0:m, 0:m])
                        mm = pe.transpose(bank_t[b][0:T_S, (2 + c) * P:(2 + c) * P + m], s_buf[b][0:m, c, P:P + T_S],
                                          ident[0:m, 0:m])
                mm.then_inc(t_done, 1)

            def out_v(U, r, b, pr, v):
                pe.wait_ge(c_done, U + 1)
                if r == 0 and not (isinstance(pr, int) and pr < 1):
                    pe.wait_ge(olo_rdy, pr)
                for c in range(2):
                    out = bank_o[c * HD:(c + 1) * HD, TOK[r]]
                    cols = slice(c * HD, (c + 1) * HD)
                    if r < 2:
                        nk = NKEY[r] // P
                        for kc in range(nk):
                            mm = pe.matmul(out, v[:, kc, cols], p_t[b][:, c * nk + kc, :], start=(kc == 0), stop=(kc == nk - 1))
                    else:
                        pe.matmul(out, v[:, 2, cols], p_t[b][:, c, 0:T_S], start=True, stop=False)
                        mm = pe.matmul(out, v[0:T_S, 3, cols], p_t[b][0:T_S, 2 + c, 0:T_S], start=False, stop=True)
                mm.then_inc(pv_done, 1)

            def attention(kind, body, turn, piece, sums):
                U, pr = body * 6, body * 2
                if kind == "cb":
                    kt, v = [kt_c, kt_b], [v_c, v_b]
                else:
                    kt, v = [kt_a[:, 0, :], kt_a[:, 1, :]], [v_a[:, :, 0:P], v_a[:, :, P:2 * P]]

                def sc(u):
                    p, r = divmod(u, 3)
                    if r == 0:
                        pe.wait_ge(qn_rdy, body * 2 + (p + 1))
                        if p == 0 and kind == "cb":
                            pe.wait_ge(qk_rdy, body + (KEY_NORMS + 1))
                    if u == 2 and kind == "cb":
                        pe.wait_ge(kc_rdy, body + 1)
                    scores(U + u, r, u % 2, q_n[p], kt[p])

                def tp(u):
                    turn_p(U + u, u % 3, u % 2)

                def pv(u):
                    p, r = divmod(u, 3)
                    if u == 0 and kind == "cb":
                        pe.wait_ge(m_free, turn + 1)
                        pe.wait_ge(vc_ld, body * 16 + 16)
                    out_v(U + u, r, u % 2, pr + p, v[p])

                for k in range(8):
                    piece(k)
                    if k == 0:
                        if kind == "cb":
                            turn_rows(turn, z_v, T_P)
                    if k < 6:
                        sc(k)
                    if 2 <= k:
                        tp(k - 2)
                    if k == 1 and kind == "cb":
                        turn_rows(turn + 1, kt_c, T_P + PAST)
                    if 3 <= k:
                        pv(k - 3)
                    if k in sums:
                        set_sums(*sums[k])
                    if k == 7:
                        pv(5)

            def prep_items(step):
                for it in PREP_ITEMS.get(step, []):
                    if it[0] == "n":
                        head_sum(misc_no[it], norm_no[it])
                    elif it[0] == "v":
                        tile, strips = {"va0": (2, 9), "va1": (3, 10), "vb": (9, 12)}[it[1]]
                        pe.wait_ge(evac, phase["prep"].n0 + strips)
                        turn_rows(misc_no[it], z_prep[:, tile, :], T_P)
                    elif it[0] == "k":
                        kt = {"ka0": kt_a[:, 0, :], "ka1": kt_a[:, 1, :], "ki": kt_i, "kb": kt_b}[it[1]]
                        if it[1] != "ki":
                            pe.wait_ge(qk_rdy, norm_no[("n", it[1])] + 1)
                        turn_rows(misc_no[it], kt, T_P + PAST)
                    elif it[0] == "s":
                        set_sums(misc_no[it], set_squares(0, 2), True, (0, 1))
                    elif it[0] == "w":
                        misc_begin(misc_no[it])
                        pe.wait_ge(evac, phase["prep"].n0 + 6)
                        for t, (a, b) in enumerate(((0, P), (P, 2 * P), (2 * P, NT))):
                            mm = pe.transpose(bank_m[0:b - a, t * H_IDX:(t + 1) * H_IDX], zw[:, a:b], ident[0:H_IDX, 0:H_IDX])
                        mm.then_inc(m_done, 1)
                    elif it[0] == "i":
                        u = it[1]
                        r, t = idx_units[u]
                        pe.wait_ge(evac, phase["prep"].n0 + 5)
                        if u >= 2:
                            pe.wait_ge(irelu, u - 1)
                        for c in range(2):
                            half = slice(c * HD, (c + 1) * HD)
                            mm = pe.matmul(psum[2 + u % 2 * 2 + c][0:ROWS[r], 0:NKEY[r]],
                                           z_prep[half, 4 + t, TOK[r]], kt_i[half, KEY0[r]:KEY0[r] + NKEY[r]],
                                           start=True, stop=True)
                        mm.then_inc(iq_done, 1)

            phase = {p.name: p for p in phases if p.name not in ("up", "down")}

            bank_start = psum[2:7]
            TURNED = 1 + DT

            def start_slot(n):
                if n >= len(bank_start):
                    pe.wait_ge(start_cp, n - len(bank_start) + 1)
                return bank_start[n % len(bank_start)]

            def turn_x(k):
                b = start_slot(1 + k)
                if k % 4 == 0:
                    pe.wait_ge(x_in[k // 4], 16)
                for t in range(2):
                    pe.transpose(b[:, t * P:(t + 1) * P], xrow[:, t, k * P:(k + 1) * P], ident[:, :])
                pe.transpose(b[:, T_P:NT], xrow[0:T_S, 2, k * P:(k + 1) * P], ident[0:T_S, 0:T_S]).then_inc(start_tr, 1)

            def turn_others():
                pe.wait_ge(small_in, 16 * 6)
                b = start_slot(TURNED)
                pe.transpose(b[:, 0:6], qk_rows[:, :], ident[0:6, 0:6]).then_inc(start_tr, 1)
                b = start_slot(TURNED + 1)
                pe.matmul(b[0:H_A + H_B, 0:VEC], t5_rows[:, :], hot[:, :], start=True, stop=True).then_inc(start_tr, 1)
                b = start_slot(TURNED + 2)
                for blk in range(3):
                    c0 = (2 - blk) * P
                    mm = pe.matmul(b[0:H_C, c0:c0 + P], c_rows[:, blk, :], flip[:, :], start=True, stop=True)
                mm.then_inc(start_tr, 1)
                pe.wait_ge(cache_in, 16 * 5)
                for i, (src, _) in enumerate(CACHE_TILES):
                    b = start_slot(TURNED + 3 + i)
                    pe.transpose(b[:, 0:P], src, ident[:, :]).then_inc(start_tr, 1)

            pe.wait_ge(consts, CONSTS)
            pe.wait_ge(gains_in, 16)
            pe.transpose(start_slot(0)[:, 0:3 * DT], gain_rows[:, :], ident[0:3 * DT, 0:3 * DT]).then_inc(start_tr, 1)
            AHEAD = 11
            pe.wait_ge(xs_in, 16)
            for k in range(AHEAD):
                turn_x(k)

            def turn_y(ph, k, s):
                pe.wait_ge(evac, k + (ph.n0 + 1))
                if not (isinstance(k, int) and k < 2):
                    pe.wait_ge(y_cp, k - 1)
                for t in range(2):
                    pe.transpose(bank_t[s][:, t * P:(t + 1) * P], y_t[s][:, t * P:(t + 1) * P], ident[:, :])
                pe.transpose(bank_t[s][0:T_S, 2 * P:3 * P], y_t[s][:, T_P:NT], ident[:, :]).then_inc(y_tr, 1)

            def h_when(index):
                def when(k):
                    pe.wait_ge(hlo_rdy, DT * index + k + 1)
                return when

            gated = 0
            for ph in phases:
                if ph.name == "up":
                    if ph.more["first"]:
                        index = 2 * ph.more["ffn"]
                        begin = ph.n0 == 0

                        def when(k, index=index, begin=begin):
                            if begin and k + AHEAD < DT:
                                turn_x(k + AHEAD)
                            h_when(index)(k)
                        strip(ph, 0, 0, h_rhs, when)
                        x_norm(index)
                        strip(ph, 0, 1, h_rhs)
                        if begin:
                            turn_others()
                    with pe.Fori(1 if ph.more["first"] else 0, ph.strips // 2) as j:
                        strip(ph, j, 0, h_rhs)
                        strip(ph, j, 1, h_rhs)
                elif ph.name == "down":
                    last = ph.tiles - 1

                    def gu_when(k, g=gated, last=last):
                        if k == 0:
                            pe.wait_ge(gul_rdy, g + last)
                        if k == last:
                            pe.wait_ge(gul_rdy, g + last + 1)
                    final = ph.next is None

                    def down_body(j, ph=ph, when=gu_when, final=final):
                        strip(ph, j, 0, gu_rhs, when)
                        if final and not (isinstance(j, int) and j == 0):
                            turn_y(ph, j * 2 - 1, 1)
                        strip(ph, j, 1, gu_rhs, when)
                        if final:
                            turn_y(ph, j * 2, 0)
                    if final:
                        down_body(0)
                    with pe.Fori(1 if final else 0, ph.strips // 2) as j:
                        down_body(j)
                    if final:
                        turn_y(ph, DT - 1, 1)
                    gated += ph.tiles
                elif ph.name == "prep":
                    strip(ph, 0, 0, h_rhs, h_when(1))
                    x_norm(1)
                    strip(ph, 0, 1, h_rhs)
                    for s in range(2, 12):
                        strip(ph, s // 2, s % 2, h_rhs)
                        prep_items(s)
                    pe.wait_ge(vcache_in, 32)
                elif ph.name == "cb":
                    for t in range(4):
                        strip(ph, t // 2, t % 2, h_rhs)
                        prep_items(12 + t)

                    def cb_body(i, ph=ph):
                        m = i * MISC_CB + (MISC_CB0 - MISC_CB)
                        pe.wait_ge(evac, i * 4 + ph.n0)
                        attention("cb", i - 1, m, lambda k: strip(ph, i * 2 + k // 4, k // 2 % 2, h_rhs, part=(k % 2 * 8, k % 2 * 8 + 8)),
                                  {6: (m + 2, set_squares(i, 2), True, (0, 1))})
                    cb_body(1)
                    with pe.Fori(2, 5) as i:
                        cb_body(i)
                elif ph.name == "a":
                    def a_body(i, ph=ph):
                        quarter = lambda k: strip(ph, i, k // 4, h_rhs, part=(k % 4 * 4, k % 4 * 4 + 4))
                        if isinstance(i, int):
                            pe.wait_ge(evac, ph.n0)
                            attention("cb", 4, MISC_A0, quarter, {6: (MISC_A0 + 2, a_squares(5, 0), False, (0,))})
                        else:
                            m = i * 2 + (MISC_A1 - 2)
                            attention("a", i + 4, None, quarter, {1: (m, a_squares(i + 4, 1), False, (1,)),
                                                                  6: (m + 1, a_squares(i + 5, 0), False, (0,))})
                    a_body(0)
                    with pe.Fori(1, 3) as i:
                        a_body(i)
                else:
                    order = [11, 12, 13, 14, 15, 8, 9, 10, 6, 7, 0, 3, 1, 4, 2, 5]

                    def wo(j, s, ks):
                        n = strip_no(ph, j, s)
                        if ks[0] == order[0]:
                            pe.wait_ge(evac, n - 1)
                            pe.wait_ge(lo_rdy, n * 2 + 1)

                        def when(k):
                            if k == order[8]:
                                pe.wait_ge(lo_rdy, n * 2 + 2)
                        mm = products(ph, j, s, o_rhs, ks, n, order[0], order[-1], when)
                        if ks[-1] == order[-1]:
                            mm.then_inc(used, 1)
                        return mm

                    def piece(k):
                        if k == 0:
                            pe.wait_ge(olo_rdy, 10)
                        if k == 2:
                            pe.wait_ge(olo_rdy, 14)
                        for s in range(2):
                            a, b = (min(max(4 * x - 14 * s, 0), 14) for x in (k, k + 1))
                            if a < b:
                                mm = wo(0, s, order[a:b])
                        if k == 1:
                            mm.then_inc(part_used, 1)
                    attention("a", 7, None, piece, {1: (MISC_END - 1, a_squares(7, 1), False, (1,))})
                    pe.wait_ge(olo_rdy, 16)
                    wo(0, 0, order[14:16])
                    wo(0, 1, order[14:16])
                    with pe.Fori(1, ph.strips // 2) as j:
                        wo(j, 0, order)
                        wo(j, 1, order)
        PAIR_TILE = {"c": 11, "b": 6}

        def v_place(name):
            if name == "vb":
                cols = slice(0, P)
                flat = lambda t: t[0, 0].rearrange("t h d -> t (h d)")
                return v_b, cols, flat(pbv), flat(sbv)[P - T_S:P], 1
            t = int(name[2])
            cols = slice(t * P, (t + 1) * P)
            flat = lambda x: x[0, 0].rearrange("t h d -> t (h d)")[:, cols]
            return v_a, cols, flat(pav), flat(sav), 0

        def k_place(name):
            flat = lambda x: x[0, 0].rearrange("t h d -> t (h d)")
            if name == "ki":
                return paki[0, 0], saki[0, 0], 0, HD
            if name == "kb":
                return flat(pbk), flat(sbk)[P - T_S:P], 1, P
            cols = slice(int(name[2]) * P, (int(name[2]) + 1) * P)
            return flat(pak)[:, cols], flat(sak)[:, cols], 0, P

        @block.scalar
        def _(act):
            act.dma_start(gain_rows[:, :], gains[0].rearrange("g (k p) -> (g k) p", p=P)).then_inc(gains_in, 16)

            def split(at, halves=(0, 1)):
                if at is None:
                    return
                ph, j, s = at
                n = strip_no(ph, j, s)
                if 0 in halves:
                    if ph.name == "wo":
                        act.wait_ge(ld_wo[s], j * (16 * WO_LOADS) + 16 * WO_LOADS)
                    else:
                        act.wait_ge(ld[s], j * 32 + (ph.ld0 * 32 + 32))
                    if halves == (0,) and ph.name == "wo" and j == 1:
                        act.wait_ge(part_used, 1)
                    elif not (isinstance(n, int) and n < 2):
                        act.wait_ge(used, n - 1)
                elif ph.name == "wo" and isinstance(j, int) and j == 1:
                    act.wait_ge(used, n - 1)
                for half in halves:
                    k = half_tiles(ph, half)
                    act.activation(w_hi[s][:, k, :], raw[s][:, k, :], ACT.Copy).then_inc(hi_rdy, 1)

            def h_tile(index, j):
                H = j + DT * index
                act.wait_ge(acc_rdy, H)
                act.activation(sqx[:, :], xT[:, j, :], ACT.Square).then_inc(sqx_rdy, 1)
                h_upper(index, j)

            def h_upper(index, j):
                act.activation(h_hi[:, j, :], xT[:, j, :], ACT.Copy, scale=g_cols[:, bass.ds(j + index * DT, 1)]).then_inc(hhi_rdy, 1)

            def x_norm(index):
                m = [0, 1, MISC_END][index]
                act.wait_ge(m_done, m + 1)
                if index:
                    act.wait_ge(rstd_rdy, index)
                act.activation(sd_x[:, :], bank_m[:, 0:NT], ACT.Sqrt, bias=eps[:, :]).then_inc(m_free, 1)

            def squares(z, n_done):
                act.wait_ge(evac, n_done)
                act.activation(sq[:, :], z, ACT.Square).then_inc(sq_rdy, 1)

            def deviation(m, q):
                act.wait_ge(m_done, m + 1)
                if not (isinstance(q, int) and q == 0):
                    act.wait_ge(rinv_rdy, q)
                act.activation(sd[:, 0:NT], bank_m[:, 0:NT], ACT.Sqrt, bias=eps[:, :]).then_inc(m_free, 1)

            def set_deviation(m, b, keys, pairs):
                act.wait_ge(m_done, m + 1)
                if keys:
                    if not (isinstance(b, int) and b == 0):
                        act.wait_ge(kinv_rdy, b)
                    else:
                        act.wait_ge(rinv_rdy, KEY_NORMS)
                else:
                    act.wait_ge(scale_rdy, scale_no("a", b, pairs[0]) - 1)
                    if isinstance(b, int):
                        act.wait_ge(kinv_rdy, 5)
                c0, c1 = NT + 4 * pairs[0], NT + 4 * pairs[-1] + 4
                act.activation(sd[:, 0 if keys else c0:c1], bank_m[:, 0 if keys else c0:c1], ACT.Sqrt, bias=eps[:, :])
                c0, c1 = NT + 8 + 2 * pairs[0], NT + 8 + 2 * pairs[-1] + 2
                act.activation(sd[0:T_S, c0:c1], bank_m[0:T_S, c0:c1], ACT.Sqrt, bias=eps[0:T_S, :]).then_inc(m_free, 1)

            def place_v(m, v, cols):
                act.wait_ge(m_done, m + 1)
                act.activation(v[:, 0:2, cols], bank_m[:, 0:2 * P].rearrange("p (t c) -> p t c", t=2), ACT.Copy)
                act.activation(v[0:T_S, 3, cols], bank_m[0:T_S, 2 * P:3 * P], ACT.Copy).then_inc(m_free, 1)

            def place_k(m, kout):
                act.wait_ge(m_done, m + 1)
                if not (isinstance(kout, int) and kout == 0):
                    act.wait_ge(k_out, kout * 32)
                act.activation(k_rows[:, 0:2, :], bank_m[:, 0:2 * P].rearrange("p (t c) -> p t c", t=2), ACT.Copy)
                act.activation(k_rows[0:T_S, 2, :], bank_m[0:T_S, 2 * P:3 * P], ACT.Copy).then_inc(m_free, 1)

            def exps(U, u, sink, sign=1.0):
                b, r = u % 2, u % 3
                m, n = ROWS[r], NKEY[r]
                act.wait_ge(mx_rdy, U + u + 1)
                for c in range(2):
                    a = act.activation(s_buf[b][0:m, c, 0:n], s_buf[b][0:m, c, 0:n], ACT.Exp, bias=nmax[b][0:m, c:c + 1], scale=sign,
                                       accum_out=esum[b][0:m, c:c + 1])
                if sink:
                    a = act.activation(esnk[b][0:m, :], snk[b][0:m, :], ACT.Exp)
                a.then_inc(e_rdy, 1)

            def copy_t(U, u):
                b, r = u % 2, u % 3
                act.wait_ge(t_done, U + u + 1)
                if not (isinstance(U, int) and U + u < 2):
                    act.wait_ge(pv_done, U + (u - 1))
                pt = bank_t[b][:, :].rearrange("p (t c) -> p t c", t=4)
                if r < 2:
                    k = 4 - 2 * r
                    a = act.activation(p_t[b][:, 0:k, :], pt[:, 0:k, :], ACT.Copy)
                else:
                    act.activation(p_t[b][:, 0:2, 0:T_S], pt[:, 0:2, 0:T_S], ACT.Copy)
                    a = act.activation(p_t[b][0:T_S, 2:4, 0:T_S], pt[0:T_S, 2:4, 0:T_S], ACT.Copy)
                a.then_inc(c_done, 1)

            def out_hi(U, p, tile):
                act.wait_ge(pv_done, U + (3 * p + 3))
                act.activation(o_hi[:, tile, :], bank_o[:, 0:NT], ACT.Copy).then_inc(ohi_rdy, 1)

            def prep_items(step):
                for it in PREP_ITEMS.get(step, []):
                    if it[0] == "n":
                        z, done = {"ka0": (0, 7), "ka1": (1, 8), "kb": (8, 11)}[it[1]]
                        squares(z_prep[:, z, :], phase["prep"].n0 + done)
                        deviation(misc_no[it], norm_no[it])
                    elif it[0] == "v":
                        v, cols, _, _, _ = v_place(it[1])
                        place_v(misc_no[it], v, cols)
                    elif it[0] == "k":
                        place_k(misc_no[it], kout_no[it])
                    elif it[0] == "s":
                        set_deviation(misc_no[it], 0, True, (0, 1))
                    elif it[0] == "w":
                        act.wait_ge(m_done, misc_no[it] + 1)
                        act.activation(w_tok[:, 0:2, :], bank_m[:, 0:2 * H_IDX].rearrange("p (t c) -> p t c", t=2), ACT.Copy)
                        act.activation(w_tok[0:T_S, 2, :], bank_m[0:T_S, 2 * H_IDX:3 * H_IDX], ACT.Copy).then_inc(m_free, 1)
                    elif it[0] == "i":
                        u = it[1]
                        r, _ = idx_units[u]
                        act.wait_ge(iq_done, u + 1)
                        if u >= 2:
                            act.wait_ge(iacc, 2 * u - 2)
                        m, n = ROWS[r], NKEY[r]
                        for c in range(2):
                            a = act.activation(s_buf[u % 2][0:m, c, 0:n], psum[2 + u % 2 * 2 + c][0:m, 0:n], ACT.Relu)
                        a.then_inc(irelu, 1)

            def attention(body, kind, turn, split_half, tiles, sums):
                U = body * 6
                for k in range(8):
                    if k == 0 and kind == "cb":
                        act.wait_ge(v_out, body * 32 + VOUT_PREP * 32)
                        if not (isinstance(body, int) and body == 0):
                            act.wait_ge(pv_done, U)
                        place_v(turn, v_c, slice(0, P))
                    if k == 1 and kind == "cb":
                        place_k(turn + 1, body + KOUT_PREP)
                    if 2 <= k:
                        copy_t(U, k - 2)
                    if k == 5:
                        out_hi(U, 0, tiles[0])
                    split_half(k + 1)
                    if k < 6:
                        exps(U, k, kind == "cb" and k >= 3, 1.0 if kind == "cb" else -1.0)
                    if k in sums:
                        set_deviation(*sums[k])
                out_hi(U, 1, tiles[1])

            phase = {p.name: p for p in phases if p.name not in ("up", "down")}

            for j in range(DT):
                act.wait_ge(start_cp, 2 + j)
                h_upper(0, j)
                if j >= 2:
                    act.wait_ge(acc_rdy, j - 1)
                act.activation((sqx, sd_x)[j % 2][:, :], xT[:, j, :], ACT.Square).then_inc(x_sq, 1)
                if j == 6:
                    split((phases[0], 0, 0))

            for ph in phases:
                if ph.name == "up":
                    F0 = sum(p.more["size"] for p in phases[:phases.index(ph)] if p.name == "up")

                    def body(j, ph=ph, F0=F0):
                        F = j + F0
                        n = strip_no(ph, j, 0)
                        split(following(ph, j, 0))
                        if ph.more["first"] and isinstance(j, int) and j == 0:
                            x_norm(2 * ph.more["ffn"])
                        act.wait_ge(evac, n + 1)
                        if not (isinstance(F, int) and F == 0):
                            act.wait_ge(gu_rdy, F)
                        act.activation(g_sig[:, :], g_act[:, :], ACT.Silu).then_inc(sig_rdy, 1)
                        split(following(ph, j, 1))
                        act.wait_ge(gu_rdy, F + 1)
                        act.activation(gu_hi[:, j, :], gu[:, :], ACT.Copy).then_inc(guh_rdy, 1)
                    bodies(act, ph, body, peel_first=ph.more["first"])
                elif ph.name == "down" or ph.name == "wo":
                    index = 1 if ph.name == "down" else 2
                    h_after = ph.name == "wo" or (ph.more["last"] and ph.more["ffn"] == 0)

                    final = ph.next is None

                    def store_y(k, s):
                        act.wait_ge(y_tr, k + 1)
                        if not (isinstance(k, int) and k < 2):
                            act.wait_ge(y_out[s], (k - s) * 16)
                        act.activation(y_rows[:, s, 0:2, :], bank_t[s][:, 0:2 * P].rearrange("p (t c) -> p t c", t=2), ACT.Copy)
                        act.activation(y_rows[0:T_S, s, 2, :], bank_t[s][0:T_S, 2 * P:3 * P], ACT.Copy).then_inc(y_cp, 1)
                        act.wait_ge(y_cp, k + 1)
                        act.dma_start(yp[0].rearrange("(t p) c -> p t c", p=P)[:, :, bass.ds(k * P, P)], y_rows[:, s, 0:2, :])\
                           .then_inc(y_out[s], 16)
                        act.dma_start(ys[0][:, bass.ds(k * P, P)], y_rows[0:T_S, s, 2, :]).then_inc(y_out[s], 16)

                    def body(j, ph=ph, index=index, h_after=h_after, final=final):
                        for s in range(2):
                            if final:
                                split(following(ph, j, s))
                                if s == 1:
                                    store_y(j * 2, 0)
                                elif not (isinstance(j, int) and j == 0):
                                    store_y(j * 2 - 1, 1)
                                continue
                            if ph.name == "wo" and isinstance(j, int) and j == 0:
                                if s == 0:
                                    attend_tail()
                                    split((ph, 1, 0), (1,))
                            else:
                                split(following(ph, j, s))
                            if h_after:
                                act.wait_ge(evac, strip_no(ph, j, s) + 1)
                                h_tile(index, j * 2 + s)

                    def attend_tail():
                        tail_split = lambda k: split((ph, 0, 1), (1,)) if k == 2 else split((ph, 1, 0), (0,)) if k == 7 else None
                        attention(7, "a", None, tail_split, (2, 5), {1: (MISC_END - 1, 7, False, (1,))})
                    bodies(act, ph, body, peel_first=ph.name == "wo" or final)
                    if final:
                        store_y(DT - 1, 1)
                elif ph.name == "prep":
                    def body(j, ph=ph):
                        split(following(ph, j, 0))
                        if isinstance(j, int) and j == 0:
                            x_norm(1)
                        split(following(ph, j, 1))
                    body(0)
                    for t in range(2, 12):
                        split(following(ph, t // 2, t % 2))
                        prep_items(t)
                elif ph.name == "cb":
                    for t in range(4):
                        split(following(ph, t // 2, t % 2))
                        prep_items(12 + t)

                    def body(i, ph=ph):
                        m = i * MISC_CB + (MISC_CB0 - MISC_CB)
                        order = [(ph, i * 2, 1), (ph, i * 2 + 1, 0), (ph, i * 2 + 1, 1)]
                        order += [(ph, i * 2 + 2, s) if not isinstance(i, int) or i < 4 else (ph.next, 0, s) for s in range(2)]
                        attention(i - 1, "cb", m, lambda k: split(order[k // 2], (k % 2,)),
                                  (i + (PAIR_TILE["c"] - 1), i + (PAIR_TILE["b"] - 1)), {6: (m + 2, i, True, (0, 1))})
                    split((ph, 2, 1), (0,))
                    body(1)
                    with act.Fori(2, 4) as i:
                        body(i)
                    body(4)
                elif ph.name == "a":
                    def body(i, ph=ph):
                        order = [(ph, i, 1), following(ph, i, 1), (ph, i + 1, 1) if i < 2 else (ph.next, 0, 1)]
                        split_half = lambda k: split(order[k // 4], (k // 2 % 2,)) if k % 2 == 0 else None
                        if i == 0:
                            attention(4, "cb", MISC_A0, split_half, (PAIR_TILE["c"] + 4, PAIR_TILE["b"] + 4),
                                      {6: (MISC_A0 + 2, 5, False, (0,))})
                        else:
                            m = i * 2 + (MISC_A1 - 2)
                            attention(i + 4, "a", None, split_half, (i - 1, i + 2),
                                      {1: (m, i + 4, False, (1,)), 6: (m + 1, i + 5, False, (0,))})
                    body(0), body(1), body(2)
            for stored in y_out:
                act.wait_ge(stored, DT // 2 * 32)

        @block.vector
        def _(dve):
            steps = [0]

            def link(ins):
                steps[0] += 1
                ins.then_inc(dve_link, 1)
                dve.wait_ge(dve_link, steps[0])

            def split(at, halves=(0, 1)):
                if at is None:
                    return
                ph, j, s = at
                n = strip_no(ph, j, s)
                for half in halves:
                    k = half_tiles(ph, half)
                    dve.wait_ge(hi_rdy, n * 2 + (half + 1))
                    dve.tensor_tensor(w_lo[s][:, k, :], raw[s][:, k, :], w_hi[s][:, k, :].bitcast(F32), ALU.subtract)\
                       .then_inc(lo_rdy, 1)

            def h_tile(index, j, own_sum=True):
                H = j + DT * index
                if own_sum:
                    dve.wait_ge(sqx_rdy, H + (1 - DT))
                    dve.wait_ge(acc_rdy, H)
                    dve.tensor_tensor(sumsq[:, :], sumsq[:, :], sqx[:, :], ALU.add).then_inc(acc_rdy, 1)
                dve.wait_ge(hhi_rdy, H + 1)
                dve.scalar_tensor_tensor(h_lo[:, j, :], xT[:, j, :], g_cols[:, bass.ds(j + index * DT, 1)],
                                         h_hi[:, j, :].bitcast(F32), ALU.mult, ALU.subtract).then_inc(hlo_rdy, 1)

            def x_norm(index, n):
                m = [0, 1, MISC_END][index]
                dve.wait_ge(m_free, m + 1)
                if n:
                    dve.wait_ge(evac, n)
                dve.reciprocal(rstd[:, :], sd_x[:, :]).then_inc(rstd_rdy, 1)
                dve.wait_ge(rstd_rdy, index + 1)

            def read(n, s, dst, rows=slice(0, P), cols=slice(0, NT)):
                dve.wait_ge(used, n + 1)
                return dve.tensor_tensor(dst, bank_w[s][rows, cols], rstd[rows, cols], ALU.mult)

            def finish(name, m, q):
                z, gain, places = norm_source(name)
                dve.wait_ge(m_free, m + 1)
                if not (isinstance(q, int) and q == 0):
                    dve.wait_ge(qk_rdy, q)
                dve.reciprocal(rinv[:, :], sd[:, 0:NT]).then_inc(rinv_rdy, 1)
                dve.wait_ge(rinv_rdy, q + 1)
                for dst, cols, rows in places:
                    ins = dve.scalar_tensor_tensor(dst, z[rows, cols], qk_cols[rows, gain:gain + 1], rinv[rows, cols], ALU.mult, ALU.mult)
                ins.then_inc(qk_rdy, 1)

            def set_inverses(m, b, keys, pairs):
                dve.wait_ge(m_free, m + 1)
                c0, c1 = 4 * pairs[0], 4 * pairs[-1] + 4
                dve.reciprocal(q_scale[:, c0:c1], sd[:, NT + c0:NT + c1])
                c0, c1 = 8 + 2 * pairs[0], 8 + 2 * pairs[-1] + 2
                dve.reciprocal(q_scale[0:T_S, c0:c1], sd[0:T_S, NT + c0:NT + c1]).then_inc(scale_rdy, 1)
                if keys:
                    dve.reciprocal(rinv[:, :], sd[:, 0:NT]).then_inc(kinv_rdy, 1)
                    dve.wait_ge(kinv_rdy, b + 1)
                    if not (isinstance(b, int) and b == 0):
                        dve.wait_ge(qk_done, b * 6 - 3)
                    z, gain, places = norm_source("kc")
                    for dst, cols, rows in places:
                        ins = dve.scalar_tensor_tensor(dst, z[rows, cols], qk_cols[rows, gain:gain + 1], rinv[rows, cols], ALU.mult, ALU.mult)
                    ins.then_inc(qk_rdy, 1)

            def smax(kind, body, u):
                U = body * 6
                b, r, p = u % 2, u % 3, u // 3
                m, n = ROWS[r], NKEY[r]
                dve.wait_ge(qk_done, U + (u + 1))
                if not (isinstance(U, int) and U + u < 2):
                    dve.wait_ge(t_done, U + (u - 1))
                if r == 0:
                    if kind == "cb":
                        dve.wait_ge(bias_rdy, body * 2 + (p + 1))
                    else:
                        dve.wait_ge(bias_ld[p], body * 16 + 16)
                rev = [slice(None, None, -1), slice(P - 1, None, -1), slice(T_P - 1, T_P - 1 - n, -1)][r]
                s = s_buf[b][0:m, :, 0:n]
                if r == 0:
                    dve.wait_ge(scale_rdy, scale_no(kind, body, p))
                for c in range(2):
                    x = scale_col(p, r) + c
                    ins = dve.scalar_tensor_tensor(s_buf[b][0:m, c, 0:n], bank_s[c][0:m, 0:n], q_scale[0:m, x:x + 1],
                                                   bias_rev[p][0:m, c, rev], ALU.mult, ALU.add)
                ins.then_inc(s_add, 1)
                dve.wait_ge(s_add, U + (u + 1))
                if kind == "a":
                    for c in range(2):
                        x = s_buf[b][0:m, c, 0:n]
                        ins = dve.tensor_tensor_reduce(x, x, a_mask[r][0:m, :], -1.0, -NEG, ALU.add, ALU.min, nmax[b][0:m, c:c + 1])
                    ins.then_inc(mx_rdy, 1)
                    return
                sink = kind == "cb" and p == 1
                red = dve.tensor_reduce(nmax[b][0:m, :], s, AX_X, ALU.max, negate=True)
                if not sink:
                    red.then_inc(mx_rdy, 1)
                else:
                    c0 = body * 6 + 2 * r
                    ns = neg_sinks[0:m, :, body]
                    red.then_inc(mx_raw, 1)
                    dve.wait_ge(mx_raw, c0 + 1)
                    dve.tensor_tensor(nmax[b][0:m, :], nmax[b][0:m, :], ns, ALU.min).then_inc(mx_raw, 1)
                    dve.wait_ge(mx_raw, c0 + 2)
                    dve.tensor_tensor(snk[b][0:m, :], nmax[b][0:m, :], ns, ALU.subtract).then_inc(mx_rdy, 1)

            def inverse(kind, body, u):
                b, r, p = u % 2, u % 3, u // 3
                m = ROWS[r]
                dve.wait_ge(e_rdy, body * 6 + (u + 1))
                if kind == "cb" and p == 1:
                    dve.tensor_tensor(esum[b][0:m, :], esum[b][0:m, :], esnk[b][0:m, :], ALU.add).then_inc(sum_sunk, 1)
                    dve.wait_ge(sum_sunk, body * 3 + (r + 1))
                dve.reciprocal(einv[b][0:m, :], esum[b][0:m, :]).then_inc(r_rdy, 1)
                dve.wait_ge(r_rdy, body * 6 + (u + 1))
                n = NKEY[r]
                for c in range(2):
                    ins = dve.tensor_scalar(s_buf[b][0:m, c, 0:n], s_buf[b][0:m, c, 0:n], einv[b][0:m, c:c + 1], None, ALU.mult)
                ins.then_inc(p_rdy, 1)

            def out_lo(body, p, tile):
                dve.wait_ge(ohi_rdy, body * 2 + (p + 1))
                dve.tensor_tensor(o_lo[:, tile, :], bank_o[:, 0:NT], o_hi[:, tile, :].bitcast(F32), ALU.subtract).then_inc(olo_rdy, 1)

            def attention(body, kind, split_half, reads, tiles, sums, late={}, late_inverse=True):
                for k in range(8):
                    if k < 6:
                        smax(kind, body, k)
                    if k == 5:
                        out_lo(body, 0, tiles[0])
                    if k in sums:
                        set_inverses(*sums[k])
                    if late_inverse and 1 <= k < 7:
                        inverse(kind, body, k - 1)
                    if k in reads:
                        reads[k]()
                    split_half(k + 1)
                    if not late_inverse and k < 6:
                        inverse(kind, body, k)
                    if k in late:
                        top_keys(*late[k])
                out_lo(body, 1, tiles[1])

            def prep_items(step):
                for it in PREP_ITEMS.get(step, []):
                    if it[0] == "n":
                        finish(it[1], misc_no[it], norm_no[it])
                    elif it[0] == "s":
                        set_inverses(misc_no[it], 0, True, (0, 1))
                    elif it[0] == "i":
                        u = it[1]
                        r, t = idx_units[u]
                        m, n = ROWS[r], NKEY[r]
                        dve.wait_ge(irelu, u + 1)
                        if u == 0:
                            dve.wait_ge(m_free, misc_no[("w",)] + 1)
                        for c in range(2):
                            w = w_tok[0:m, [1, 0, 2][r], 2 * t + c:2 * t + c + 1]
                            acc = idx_acc[r][0:m, :]
                            if t == 0 and c == 0:
                                ins = dve.tensor_scalar(acc, s_buf[u % 2][0:m, c, 0:n], w, None, ALU.mult)
                            else:
                                dve.wait_ge(iacc, 2 * u + c)
                                ins = dve.scalar_tensor_tensor(acc, s_buf[u % 2][0:m, c, 0:n], w, acc, ALU.mult, ALU.add)
                            ins.then_inc(iacc, 1)
                    elif it[0] == "t":
                        top_keys(*it[1:])

            def top_keys(r, first, last):
                m, n, rounds = ROWS[r], NKEY[r], (K_P if r < 2 else K_S) // 8
                acc = idx_acc[r][0:m, :]
                if first == 0:
                    dve.wait_ge(iacc, 8 * (r + 1))
                    link(dve.tensor_scalar(acc, acc, IDX_SCALE, None, ALU.mult))
                    if r < 2:
                        link(dve.memset(idx_acc[r][0:CHUNK, n - CHUNK:n], NEG))
                for _ in range(first, last):
                    link(dve.max(top8[0:m, :], acc))
                    link(dve.match_replace(acc, top8[0:m, :], acc, TAKEN))
                if last == rounds:
                    dve.tensor_scalar(a_mask[r][0:m, :], acc, TAKEN / 2, NEG, ALU.is_gt, ALU.mult).then_inc(mask_rdy, 1)

            for tile, value in ((sumsq[:, :], 0.0), (mean_d[:, :], 1.0 / D), (eps[:, :], EPS), (mean_hd[:, :], 0.0),
                                (mean_hd[0:HD, 0:HD], 1.0 / HD), (mean_hd2[:, :], 0.0), (mean_hd2[0:HD, 0:1], 1.0 / HD),
                                (mean_hd2[HD:P, 1:2], 1.0 / HD)):
                link(dve.memset(tile, value))
            dve.wait_ge(consts, 2)
            dve.memset(mean_hd[HD:P, HD:P], 1.0 / HD).then_inc(consts, 1)
            bank_start = psum[2:7]

            def start_copy(n, dst, src_cols, rows=slice(0, P), last=True):
                dve.wait_ge(start_tr, n + 1)
                ins = dve.tensor_copy(dst, bank_start[n % 5][rows, src_cols])
                if last:
                    ins.then_inc(start_cp, 1)
            start_copy(0, g_cols[:, :], slice(0, 3 * DT))
            start_copy(1, xT[:, 0, :], slice(0, NT))
            for j in range(DT):
                if j + 1 < DT:
                    start_copy(2 + j, xT[:, j + 1, :], slice(0, NT))
                dve.wait_ge(start_cp, 2 + j)
                h_tile(0, j, own_sum=False)
                if j == 6:
                    split((phases[0], 0, 0))

            def place_others():
                n = 1 + DT
                start_copy(n, qk_cols[:, :], slice(0, 6))
                start_copy(n + 1, vec_t5[:, :], slice(0, VEC), slice(0, H_A + H_B))
                start_copy(n + 2, vec_c[:, :], slice(0, VEC), slice(0, H_C))
                for i, (_, dst) in enumerate(CACHE_TILES):
                    start_copy(n + 3 + i, dst, slice(0, P))
                dve.wait_ge(small_in, 16 * 6)
                link(dve.tensor_scalar(neg_sinks[:, :, :].rearrange("p a b -> p (a b)"), sink_rows[:, :, :].rearrange("p a b -> p (a b)"),
                                       -1.0, None, ALU.mult))

            for ph in phases:
                if ph.name == "up":
                    F0 = sum(p.more["size"] for p in phases[:phases.index(ph)] if p.name == "up")

                    def body(j, ph=ph, F0=F0):
                        F = j + F0
                        n = strip_no(ph, j, 0)
                        later = not (isinstance(F, int) and F == 0)
                        split(following(ph, j, 0))
                        if ph.more["first"] and isinstance(j, int) and j == 0:
                            x_norm(2 * ph.more["ffn"], ph.n0)
                        if later:
                            dve.wait_ge(sig_rdy, F)
                        read(n, 0, g_act[:, :]).then_inc(evac, 1)
                        split(following(ph, j, 1))
                        if later:
                            dve.wait_ge(gu_rdy, F)
                        read(n + 1, 1, u_act[:, :]).then_inc(evac, 1)
                        dve.wait_ge(evac, n + 2)
                        dve.wait_ge(sig_rdy, F + 1)
                        if later:
                            dve.wait_ge(gul_rdy, F)
                            dve.wait_ge(guh_rdy, F)
                        dve.tensor_tensor(gu[:, :], g_sig[:, :], u_act[:, :], ALU.mult).then_inc(gu_rdy, 1)
                        dve.wait_ge(gu_rdy, F + 1)
                        dve.wait_ge(guh_rdy, F + 1)
                        dve.tensor_tensor(gu_lo[:, j, :], gu[:, :], gu_hi[:, j, :].bitcast(F32), ALU.subtract).then_inc(gul_rdy, 1)
                        if isinstance(n, int) and n == 0:
                            place_others()
                    bodies(dve, ph, body, peel_first=ph.more["first"])
                elif ph.name in ("down", "wo"):
                    index = 1 if ph.name == "down" else 2
                    factor = 0.5 if ph.name == "down" else 1.0
                    h_after = ph.name == "wo" or (ph.more["last"] and ph.more["ffn"] == 0)
                    done = 1 if ph.name == "down" and ph.more["ffn"] == 0 else 2 if ph.name == "wo" else 3
                    dve.wait_ge(hlo_rdy, DT * done)
                    if h_after:
                        dve.wait_ge(m_done, [0, 1, 2][index])
                        link(dve.memset(sumsq[:, :], 0.0))

                    final = ph.next is None

                    def body(j, ph=ph, index=index, factor=factor, h_after=h_after, final=final):
                        for s in range(2):
                            n = strip_no(ph, j, s)
                            tail = ph.name == "wo" and isinstance(j, int) and j == 0
                            if tail and s == 0:
                                attend_tail()
                            if not tail:
                                split(following(ph, j, s))
                            dve.wait_ge(used, n + 1)
                            dve.wait_ge(evac, n)
                            d = j * 2 + s
                            if final and not (isinstance(d, int) and d < 2):
                                dve.wait_ge(y_tr, d - 1)
                            dst = y_t[s][:, :] if final else xT[:, d, :]
                            dve.scalar_tensor_tensor(dst, bank_w[s][:, 0:NT], factor, xT[:, d, :], ALU.mult, ALU.add)\
                               .then_inc(evac, 1)
                            if tail and s == 0:
                                split((ph, 1, 0), (1,))
                            if h_after:
                                dve.wait_ge(evac, n + 1)
                                h_tile(index, d)

                    def attend_tail():
                        tail_split = lambda k: split((ph, 0, 1), (1,)) if k == 2 else split((ph, 1, 0), (0,)) if k == 7 else None
                        attention(7, "a", tail_split, {}, (2, 5), {2: (MISC_END - 1, 7, False, (1,))})
                    bodies(dve, ph, body, peel_first=ph.name == "wo" or final)
                elif ph.name == "prep":
                    def body(j, ph=ph):
                        n = strip_no(ph, j, 0)
                        split(following(ph, j, 0))
                        if isinstance(j, int) and j == 0:
                            x_norm(1, ph.n0)
                        read(n, 0, z_prep[:, 4 + j * 2, :]).then_inc(evac, 1)
                        split(following(ph, j, 1))
                        read(n + 1, 1, z_prep[:, 4 + j * 2 + 1, :]).then_inc(evac, 1)
                    body(0)
                    body(1)
                    n = ph.n0 + 4
                    split(following(ph, 2, 0))
                    read(n, 0, kt_i[:, 0:T_P], cols=slice(0, T_P))
                    read(n, 0, kt_i[:, T_P + PAST:KEYS], cols=slice(T_P, NT)).then_inc(evac, 1)
                    dve.wait_ge(evac, n + 1)
                    split(following(ph, 2, 1))
                    read(n + 1, 1, zw[:, :], rows=slice(0, H_IDX)).then_inc(evac, 1)
                    prep_items(5)
                    for t in range(6, 12):
                        split(following(ph, t // 2, t % 2))
                        dst = z_prep[:, t - 6 if t < 10 else t - 2, :]
                        read(ph.n0 + t, t % 2, dst).then_inc(evac, 1)
                        dve.wait_ge(evac, ph.n0 + t + 1)
                        prep_items(t)
                elif ph.name == "cb":
                    zs = [z_k, z_q[0], z_q[1], z_v]
                    for t in range(4):
                        split(following(ph, t // 2, t % 2))
                        read(ph.n0 + t, t % 2, zs[t][:, :]).then_inc(evac, 1)
                        dve.wait_ge(evac, ph.n0 + t + 1)
                        prep_items(12 + t)

                    def body(i, ph=ph):
                        n = i * 4 + ph.n0
                        m = i * MISC_CB + (MISC_CB0 - MISC_CB)
                        order = [(ph, i * 2, 1), (ph, i * 2 + 1, 0), (ph, i * 2 + 1, 1)]
                        order += [(ph, i * 2 + 2, s) if not isinstance(i, int) or i < 4 else (ph.next, 0, s) for s in range(2)]

                        def whole(t):
                            if t == 0:
                                dve.wait_ge(qk_rdy, i + KEY_NORMS)
                            elif t < 3:
                                dve.wait_ge(qn_rdy, i * 2 + (t - 2))
                            else:
                                dve.wait_ge(m_done, m + 1)
                            read(n + t, t % 2, zs[t][:, :]).then_inc(evac, 1)
                        late = {k: (2, k + 1, k + 2) for k in (1, 2, 3)} if isinstance(i, int) and i == 1 else {}
                        attention(i - 1, "cb", lambda k: split(order[k // 2], (k % 2,)),
                                  {2 * t + 1: (lambda t=t: whole(t)) for t in range(4)},
                                  (i + (PAIR_TILE["c"] - 1), i + (PAIR_TILE["b"] - 1)), {7: (m + 2, i, True, (0, 1))}, late, late_inverse=False)
                    split((ph, 2, 1), (0,))
                    body(1)
                    with dve.Fori(2, 4) as i:
                        body(i)
                    body(4)
                elif ph.name == "a":
                    dve.wait_ge(mask_rdy, 3)

                    def body(i, ph=ph):
                        n = i * 2 + ph.n0
                        order = [(ph, i, 1), following(ph, i, 1), (ph, i + 1, 1) if i < 2 else (ph.next, 0, 1)]
                        split_half = lambda k: split(order[k // 4], (k // 2 % 2,)) if k % 2 == 0 else None

                        def whole(t):
                            dve.wait_ge(qn_rdy, i * 2 + (9 + t))
                            read(n + t, t, z_q[t][:, :]).then_inc(evac, 1)
                        reads = {3: lambda: whole(0), 7: lambda: whole(1)}
                        if i == 0:
                            attention(4, "cb", split_half, reads, (PAIR_TILE["c"] + 4, PAIR_TILE["b"] + 4),
                                      {7: (MISC_A0 + 2, 5, False, (0,))})
                        else:
                            m = i * 2 + (MISC_A1 - 2)
                            attention(i + 4, "a", split_half, reads, (i - 1, i + 2),
                                      {2: (m, i + 4, False, (1,)), 7: (m + 1, i + 5, False, (0,))})
                    body(0), body(1), body(2)
        @block.gpsimd
        def _(pool):
            pool.memset(ident[:, :], 0.0).then_inc(pool_built, 1)
            pool.wait_ge(pool_built, 1)
            pool.memset(flip[:, :], 0.0).then_inc(pool_built, 1)
            pool.wait_ge(pool_built, 2)
            pool.affine_select(out=ident[:, :], in_=ident[:, :], compare_op=ALU.not_equal, fill=1.0, base=0,
                               pattern=[[-1, P]], channel_multiplier=1).then_inc(consts, 1)
            pool.wait_ge(consts, 1)
            pool.affine_select(out=flip[:, :], in_=flip[:, :], compare_op=ALU.not_equal, fill=1.0, base=1 - P,
                               pattern=[[1, P]], channel_multiplier=1).then_inc(consts, 1)
            pool.wait_ge(consts, 2)

            def settled():
                pool.sem_inc(pool_passed, 1)

            for j in range(DT):
                pool.wait_ge(x_sq, j + 1)
                if j:
                    pool.wait_ge(acc_rdy, j)
                pool.tensor_tensor(sumsq[:, :], sumsq[:, :], (sqx, sd_x)[j % 2][:, :], ALU.add).then_inc(acc_rdy, 1)
            for src, dst in ((cbk, sbk), (cbv, sbv), (cck, sck), (ccv, scv)):
                pool.dma_start(dst[0, 0, 0:P - T_S], src[0, 0, T_S:P]).then_inc(misc_out, 16)
            pool.wait_ge(start_cp, 1 + DT + 3)
            pool.dma_start(vec_dram[0:H_A + H_B, :], vec_t5[:, :]).then_inc(vec_out, 16)
            pool.dma_start(vec_dram[H_A + H_B:H_A + H_B + H_C, :], vec_c[:, :]).then_inc(vec_out, 16)
            pool.wait_ge(vec_out, 32)

            def windows(first, step, count, apart):
                return bass.AP(vec_dram.tensor, first * VEC, [[step * VEC, count], [1, P], [apart * VEC, 2], [1, T_P]])
            win = {"c": windows(H_A + H_B, 2, 5, 1), "b": windows(H_A, 1, 5, 5),
                   "a0": windows(0, 1, 3, 3), "a1": windows(6, 1, 3, 3)}

            def load_bias(kind, at, p, body):
                if not (isinstance(body, int) and body == 0):
                    pool.wait_ge(s_add, body * 6 + (3 * p - 3))
                    settled()
                pool.dma_start(bias_rev[p][:, :, :], win[kind][at]).then_inc(bias_ld[p], 16)
                if kind in "bc":
                    pool.wait_ge(bias_ld[p], body * 16 + 16)
                    settled()
                    if kind == "b":
                        pool.memset(bias_rev[p][CHUNK:P, :, T_P - CHUNK:T_P], NEG).then_inc(window_msk, 1)
                        pool.wait_ge(window_msk, body + 1)
                        settled()
                    pool.memset(bias_rev[p][0:CHUNK, :, 0:CHUNK], NEG).then_inc(bias_rdy, 1)
                    pool.wait_ge(bias_rdy, body * 2 + (p + 1))
                    settled()

            def place_c_cache(i):
                pool.tensor_copy(kt_c[:, T_P:T_P + PAST], kc_cache[:, i, :]).then_inc(kc_rdy, 1)
                pool.wait_ge(kc_rdy, i + 1)
                settled()
                pool.dma_start(v_c[:, 2, :], ccv_t[:, bass.ds(i * P, P)]).then_inc(vc_ld, 16)

            ccv_t = ccv[0, 0].rearrange("t h d -> t (h d)")

            def place_q(b, p, n_done, number, gain):
                z = z_q[p]
                square(z, 1 + p, n_done, number)
                if not (isinstance(b, int) and b == 0):
                    pool.wait_ge(qk_done, b * 6 + (3 * p - 3))
                    settled()
                pool.tensor_scalar(q_n[p][:, :], z[:, :], qk_cols[:, gain:gain + 1], ATTN_SCALE, ALU.mult, ALU.mult).then_inc(qn_rdy, 1)
                pool.wait_ge(qn_rdy, b * 2 + (p + 1))
                settled()

            def square(z, which, n_done, number):
                pool.wait_ge(evac, n_done)
                settled()
                pool.tensor_tensor(sq_set[which], z[:, :], z[:, :], ALU.mult).then_inc(set_sq, 1)
                pool.wait_ge(set_sq, number)
                settled()

            def store_v(m, v, cols, prompt, sample, first):
                pool.wait_ge(m_free, m + 1)
                settled()
                pool.dma_start(prompt.rearrange("(t p) c -> p t c", p=P), v[:, first:2, cols]).then_inc(v_out, 16)
                pool.dma_start(sample, v[0:T_S, 3, cols]).then_inc(v_out, 16)

            def store_k(m, prompt, sample, first, width):
                pool.wait_ge(m_free, m + 1)
                settled()
                pool.dma_start(prompt.rearrange("(t p) c -> p t c", p=P), k_rows[:, first:2, 0:width]).then_inc(k_out, 16)
                pool.dma_start(sample, k_rows[0:T_S, 2, 0:width]).then_inc(k_out, 16)

            flat = lambda x: x[0, 0].rearrange("t h d -> t (h d)")

            def store_c(m, i):
                cols = bass.ds(i * P, P)
                store_v(m, v_c, slice(0, P), flat(pcv)[:, cols], flat(scv)[P - T_S:P, cols], 0)
                store_k(m + 1, flat(pck)[:, cols], flat(sck)[P - T_S:P, cols], 0, P)

            prep = next(p for p in phases if p.name == "prep")
            pool.wait_ge(evac, prep.n0 + 1)
            load_bias("c", 0, 0, 0)
            load_bias("b", 0, 1, 0)
            place_c_cache(0)
            cb = next(p for p in phases if p.name == "cb")
            a_ph = next(p for p in phases if p.name == "a")
            for step in range(5, 16):
                if step == 13:
                    square(z_k, 0, cb.n0 + 1, set_squares(0, 0))
                if step == 14:
                    place_q(0, 0, cb.n0 + 2, set_squares(0, 1), 4)
                if step == 15:
                    place_q(0, 1, cb.n0 + 3, set_squares(0, 2), 2)
                for it in PREP_ITEMS[step]:
                    if it[0] == "v":
                        store_v(misc_no[it], *v_place(it[1]))
                    if it[0] == "k":
                        store_k(misc_no[it], *k_place(it[1]))

            def attend(body, nxt, at, turn, project):
                U, b = body * 6, body + 1
                if project == "cb":
                    square(z_k, 0, b * 4 + (cb.n0 + 1), set_squares(b, 0))
                if turn is not None:
                    store_c(turn, body)
                if nxt:
                    load_bias(nxt[0], at, 0, b)
                if project == "cb":
                    place_q(b, 0, b * 4 + (cb.n0 + 2), set_squares(b, 1), 4)
                    place_q(b, 1, b * 4 + (cb.n0 + 3), set_squares(b, 2), 2)
                elif project == "a":
                    place_q(b, 0, b * 2 + (a_ph.n0 - 10 + 1), a_squares(b, 0), 0)
                if nxt and nxt[0] == "c":
                    pool.wait_ge(pv_done, U + 3)
                    settled()
                    place_c_cache(at)
                if nxt:
                    load_bias(nxt[1], at, 1, b)
                if project == "a":
                    place_q(b, 1, b * 2 + (a_ph.n0 - 10 + 2), a_squares(b, 1), 0)

            attend(0, ("c", "b"), 1, MISC_CB0, "cb")
            with pool.Fori(1, 4) as i:
                attend(i, ("c", "b"), i + 1, i * MISC_CB + MISC_CB0, "cb")
            attend(4, ("a0", "a1"), 0, MISC_A0, "a")
            with pool.Fori(5, 7) as i:
                attend(i, ("a0", "a1"), i - 4, None, "a")
            pool.wait_ge(misc_out, 64)
            pool.wait_ge(v_out, 32 * (VOUT_PREP + 5))
            pool.wait_ge(k_out, 32 * (KOUT_PREP + 5))


_INS = ["x_prompt", "x_sample", "cache_a_k", "cache_a_v", "cache_a_kidx", "cache_b_k", "cache_b_v", "cache_c_k", "cache_c_v",
        "w_in", "w_out", "qk_norm", "sinks", "c_rel_bias", "t5_rel_bias", "norm_gains", "w_ffn_gate", "w_ffn_up", "w_ffn_down"]


def kernel(**inputs):
    import concourse.bacc as bacc
    from concourse.bass_utils import run_bass_kernel_spmd

    nc = bacc.Bacc("TRN2", target_bir_lowering=False, num_devices=1)
    arrays, args = {}, []

    def add_input(name, a):
        a = np.ascontiguousarray(a)
        arrays[f"in_{name}"] = a
        args.append(nc.dram_tensor(f"in_{name}", a.shape, mybir.dt.from_np(a.dtype), kind="ExternalInput").ap())

    for name in _INS:
        add_input(name, inputs[name])
    add_input("t5_onehot", t5_onehot())
    shape = {name: tuple(inputs[name].shape) for name in _INS}
    depth, batch, past = shape["cache_a_k"][:3]
    seq, dec = shape["x_prompt"][1], shape["x_sample"][1]
    window = shape["cache_b_k"][2]
    outs = [shape["x_prompt"], shape["x_sample"], (depth, batch, seq, KV_A, HD), (depth, batch, seq, KV_A, HD),
            (depth, batch, seq, HD), (depth, batch, window, KV_B, HD), (depth, batch, window, KV_B, HD),
            (depth, batch, seq, H_C, HD), (depth, batch, seq, H_C, HD),
            (depth, batch, dec, KV_A, HD), (depth, batch, dec, KV_A, HD), (depth, batch, dec, HD),
            shape["cache_b_k"], shape["cache_b_v"], shape["cache_c_k"], shape["cache_c_v"]]
    for i, s in enumerate(outs):
        args.append(nc.dram_tensor(f"out_{i}", s, F32, kind="ExternalOutput").ap())
    encoder_step(nc, *args)
    r = run_bass_kernel_spmd(nc, [arrays], core_ids=[0])
    return tuple(r.results[0][f"out_{i}"] for i in range(len(outs)))
```
